# Optimizing a Trainium2 kernel written in Bass

```python
import math
import jax
import jax.numpy as jnp
from jax import lax
import numpy as np

D_MODEL = 1024
BATCH = 1
SEQ = 256
DEPTH = 2

PLE_DIM = 256
ROPE_THETA = 10000.0
Q_BLOCK = 128
EPS = 1e-6
FOX_HEADS = 4
FOX_HD = 64
NSA_HEADS = 8
NSA_KV = 2
NSA_HD = 64
CMP_LEN = 32
CMP_STRIDE = 16
SLC_LEN = 64
SLC_TOPK = 16
WIN = 512
FORCE_BONUS = 1.0e4
DIFF_HEADS = 4
DIFF_QK = 32
DIFF_V = 64
PEER_HEADS = 8
PEER_NKEYS = 128
PEER_EXPERTS = PEER_NKEYS * PEER_NKEYS
PEER_DQ = 256
PEER_TOPK = 16
PEER_TOK_BLOCK = 128

IN_WIDTHS = (FOX_HEADS * FOX_HD, FOX_HEADS * FOX_HD, FOX_HEADS * FOX_HD, FOX_HEADS,
             NSA_HEADS * NSA_HD, NSA_KV * NSA_HD, NSA_KV * NSA_HD, NSA_KV * NSA_HD,
             NSA_KV * NSA_HD, NSA_KV * NSA_HD, NSA_KV * NSA_HD, 3 * NSA_HEADS,
             DIFF_HEADS * 2 * DIFF_QK, DIFF_HEADS * 2 * DIFF_QK, DIFF_HEADS * DIFF_V)
IN_WIDTH = sum(IN_WIDTHS)
MIX_WIDTH = FOX_HEADS * FOX_HD + NSA_HEADS * NSA_HD + DIFF_HEADS * DIFF_V

kernel_name = 'hymba_fox_nsa_diff_peer_trunk'

def rmsnorm(x, w):
    xf = x.astype(jnp.float32)
    y = xf * lax.rsqrt(jnp.mean(xf * xf, axis=-1, keepdims=True) + EPS)
    return (y * w.astype(jnp.float32)).astype(x.dtype)

def rope(x, pos):
    half = x.shape[-1] // 2
    inv_freq = ROPE_THETA ** (-jnp.arange(half, dtype=jnp.float32) / half)
    ang = pos.astype(jnp.float32)[..., None] * inv_freq
    cos = jnp.cos(ang)[:, :, None, :]
    sin = jnp.sin(ang)[:, :, None, :]
    xf = x.astype(jnp.float32)
    x1, x2 = xf[..., :half], xf[..., half:]
    return jnp.concatenate([x1 * cos - x2 * sin, x2 * cos + x1 * sin], axis=-1).astype(x.dtype)

def masked_softmax(s, mask):
    s = jnp.where(mask, s, -jnp.inf)
    m = jnp.max(s, axis=-1, keepdims=True)
    m = jnp.where(jnp.isfinite(m), m, 0.0)
    e = jnp.exp(s - m)
    den = jnp.sum(e, axis=-1, keepdims=True)
    return e / jnp.where(den > 0, den, 1.0)

def to_blocks(a, blk):
    b, s = a.shape[0], a.shape[1]
    return jnp.moveaxis(a.reshape((b, s // blk, blk) + a.shape[2:]), 1, 0)

def from_blocks(a):
    a = jnp.moveaxis(a, 0, 1)
    return a.reshape((a.shape[0], a.shape[1] * a.shape[2]) + a.shape[3:])

def split_proj(proj):
    idx = np.cumsum(np.array(IN_WIDTHS))[:-1].tolist()
    return jnp.split(proj, idx, axis=-1)

def fox_attention(q, k, v, f_logit):
    b, s, nh, hd = q.shape
    scale = hd ** -0.5
    c = jnp.cumsum(jax.nn.log_sigmoid(f_logit.astype(jnp.float32)), axis=1)
    c_keys = jnp.moveaxis(c, 1, 2)
    kpos = jnp.arange(s)

    def block(args):
        qb, cb, bi = args
        qpos = bi * Q_BLOCK + jnp.arange(Q_BLOCK)
        sc = jnp.einsum('bqhd,bkhd->bhqk', qb, k).astype(jnp.float32) * scale
        sc = sc + jnp.moveaxis(cb, 1, 2)[..., None] - c_keys[:, :, None, :]
        pr = masked_softmax(sc, kpos[None, :] <= qpos[:, None])
        return jnp.einsum('bhqk,bkhd->bqhd', pr.astype(v.dtype), v)

    out = lax.map(block, (to_blocks(q, Q_BLOCK), to_blocks(c, Q_BLOCK), jnp.arange(s // Q_BLOCK)))
    return from_blocks(out)

def nsa_compress(kv, pos_emb, w):
    b, s, g, hd = kv.shape
    n_cmp = (s - CMP_LEN) // CMP_STRIDE + 1
    idx = (jnp.arange(n_cmp) * CMP_STRIDE)[:, None] + jnp.arange(CMP_LEN)[None, :]
    blk = kv[:, idx] + pos_emb[:, None, :]
    blk = jnp.moveaxis(blk, 3, 2).reshape(b, n_cmp, g, CMP_LEN * hd)
    return blk @ w

def nsa_attention(q, kc, vc, ks, vs, kw, vw, gates, positions, q_norm_w, k_norm_w, cmp_pos, cmp_w):
    b, s, hq, hd = q.shape
    g = NSA_KV
    hpg = hq // g
    scale = hd ** -0.5
    qn = rmsnorm(q, q_norm_w)
    qr = rope(qn, positions)
    kc_c = rmsnorm(nsa_compress(kc, cmp_pos[0], cmp_w[0]), k_norm_w)
    vc_c = nsa_compress(vc, cmp_pos[1], cmp_w[1])
    ks_r = rope(rmsnorm(ks, k_norm_w), positions)
    kw_r = rope(rmsnorm(kw, k_norm_w), positions)
    n_cmp = kc_c.shape[1]
    ns = s // SLC_LEN
    n_sel = min(SLC_TOPK, ns)
    cmp_end = jnp.arange(n_cmp) * CMP_STRIDE + CMP_LEN - 1
    ci = jnp.arange(n_cmp)[:, None] * CMP_STRIDE
    sj = jnp.arange(ns)[None, :] * SLC_LEN
    overlap = ((ci < sj + SLC_LEN) & (ci + CMP_LEN > sj)).astype(jnp.float32)
    ks_g = jnp.moveaxis(ks_r.reshape(b, ns, SLC_LEN, g, hd), 3, 1)
    vs_g = jnp.moveaxis(vs.reshape(b, ns, SLC_LEN, g, hd), 3, 1)
    kw_p = jnp.pad(kw_r, ((0, 0), (WIN, 0), (0, 0), (0, 0)))
    vw_p = jnp.pad(vw, ((0, 0), (WIN, 0), (0, 0), (0, 0)))
    b_ix = jnp.arange(b)[:, None, None, None]
    g_ix = jnp.arange(g)[None, :, None, None]
    blk_ids = jnp.arange(ns)

    def block(args):
        qn_b, qr_b, g_b, bi = args
        qpos = bi * Q_BLOCK + jnp.arange(Q_BLOCK)
        qn_b = qn_b.reshape(b, Q_BLOCK, g, hpg, hd)
        qr_b = qr_b.reshape(b, Q_BLOCK, g, hpg, hd)
        s_c = jnp.einsum('bqghd,bngd->bghqn', qn_b, kc_c).astype(jnp.float32) * scale
        p_c = masked_softmax(s_c, cmp_end[None, :] <= qpos[:, None])
        o_c = jnp.einsum('bghqn,bngd->bqghd', p_c.astype(vc_c.dtype), vc_c)
        imp = jnp.einsum('bghqn,nm->bgqm', p_c, overlap)
        cur = qpos // SLC_LEN
        valid = blk_ids[None, :] * SLC_LEN <= qpos[:, None]
        forced = (blk_ids[None, :] == 0) | (blk_ids[None, :] == cur[:, None]) | (blk_ids[None, :] == cur[:, None] - 1)
        score = jnp.where(valid, imp + FORCE_BONUS * forced.astype(jnp.float32), -jnp.inf)
        _, sel = lax.top_k(score, n_sel)
        k_sel = ks_g[b_ix, g_ix, sel].reshape(b, g, Q_BLOCK, n_sel * SLC_LEN, hd)
        v_sel = vs_g[b_ix, g_ix, sel].reshape(b, g, Q_BLOCK, n_sel * SLC_LEN, hd)
        kpos_s = (sel[..., None] * SLC_LEN + jnp.arange(SLC_LEN)).reshape(b, g, Q_BLOCK, n_sel * SLC_LEN)
        mask_s = kpos_s <= qpos[None, None, :, None]
        s_s = jnp.einsum('bqghd,bgqkd->bghqk', qr_b, k_sel).astype(jnp.float32) * scale
        p_s = masked_softmax(s_s, mask_s[:, :, None])
        o_s = jnp.einsum('bghqk,bgqkd->bqghd', p_s.astype(v_sel.dtype), v_sel)
        k_w = lax.dynamic_slice_in_dim(kw_p, bi * Q_BLOCK, WIN + Q_BLOCK, axis=1)
        v_w = lax.dynamic_slice_in_dim(vw_p, bi * Q_BLOCK, WIN + Q_BLOCK, axis=1)
        kpos_w = bi * Q_BLOCK - WIN + jnp.arange(WIN + Q_BLOCK)
        dlt = qpos[:, None] - kpos_w[None, :]
        mask_w = (dlt >= 0) & (dlt < WIN) & (kpos_w[None, :] >= 0)
        s_w = jnp.einsum('bqghd,bkgd->bghqk', qr_b, k_w).astype(jnp.float32) * scale
        p_w = masked_softmax(s_w, mask_w)
        o_w = jnp.einsum('bghqk,bkgd->bqghd', p_w.astype(v_w.dtype), v_w)
        gt = jax.nn.sigmoid(g_b.astype(jnp.float32)).reshape(b, Q_BLOCK, g, hpg, 3).astype(o_c.dtype)
        out = gt[..., 0:1] * o_c + gt[..., 1:2] * o_s + gt[..., 2:3] * o_w
        return out.reshape(b, Q_BLOCK, hq, hd)

    out = lax.map(block, (to_blocks(qn, Q_BLOCK), to_blocks(qr, Q_BLOCK), to_blocks(gates, Q_BLOCK),
                          jnp.arange(s // Q_BLOCK)))
    return from_blocks(out)

def diff_lambda_init(layer):
    return 0.8 - 0.6 * math.exp(-0.3 * layer)

def diff_attention(q, k, v, positions, q_norm_w, k_norm_w, lam_vecs, subln_w, lambda_init):
    b, s = q.shape[0], q.shape[1]
    scale = DIFF_QK ** -0.5
    q = rope(rmsnorm(q.reshape(b, s, DIFF_HEADS * 2, DIFF_QK), q_norm_w), positions)
    k = rope(rmsnorm(k.reshape(b, s, DIFF_HEADS * 2, DIFF_QK), k_norm_w), positions)
    q = q.reshape(b, s, DIFF_HEADS, 2, DIFF_QK)
    k = k.reshape(b, s, DIFF_HEADS, 2, DIFF_QK)
    v = v.reshape(b, s, DIFF_HEADS, DIFF_V)
    lv = lam_vecs.astype(jnp.float32)
    lam = jnp.exp(jnp.sum(lv[0] * lv[1])) - jnp.exp(jnp.sum(lv[2] * lv[3])) + lambda_init
    kpos = jnp.arange(s)

    def block(args):
        qb, bi = args
        qpos = bi * Q_BLOCK + jnp.arange(Q_BLOCK)
        sc = jnp.einsum('bqhcd,bkhcd->bhcqk', qb, k).astype(jnp.float32) * scale
        pr = masked_softmax(sc, kpos[None, :] <= qpos[:, None])
        a = pr[:, :, 0] - lam * pr[:, :, 1]
        return jnp.einsum('bhqk,bkhd->bqhd', a.astype(v.dtype), v)

    o = from_blocks(lax.map(block, (to_blocks(q, Q_BLOCK), jnp.arange(s // Q_BLOCK))))
    return rmsnorm(o, subln_w) * (1.0 - lambda_init)

def peer_ffn(x, w_q, sub_keys, u, v):
    b, s, _ = x.shape
    q = (x @ w_q).reshape(b, s, PEER_HEADS, 2, PEER_DQ // 2)
    sc = jnp.einsum('bshcd,hcnd->bshcn', q, sub_keys).astype(jnp.float32)
    s1, i1 = lax.top_k(sc[..., 0, :], PEER_TOPK)
    s2, i2 = lax.top_k(sc[..., 1, :], PEER_TOPK)
    cand = (s1[..., :, None] + s2[..., None, :]).reshape(b, s, PEER_HEADS, PEER_TOPK * PEER_TOPK)
    cidx = (i1[..., :, None] * PEER_NKEYS + i2[..., None, :]).reshape(b, s, PEER_HEADS, PEER_TOPK * PEER_TOPK)
    top_s, pos = lax.top_k(cand, PEER_TOPK)
    eidx = jnp.take_along_axis(cidx, pos, axis=-1)
    gate = jax.nn.softmax(top_s, axis=-1)

    def block(args):
        xb, eb, gb = args
        hid = jax.nn.gelu(jnp.einsum('btd,bthkd->bthk', xb, u[eb]).astype(jnp.float32), approximate=False)
        w = (gb * hid).astype(x.dtype)
        return jnp.einsum('bthk,bthkd->btd', w, v[eb])

    out = lax.map(block, (to_blocks(x, PEER_TOK_BLOCK), to_blocks(eidx, PEER_TOK_BLOCK), to_blocks(gate, PEER_TOK_BLOCK)))
    return from_blocks(out)

def setup_inputs(seed: int = 0) -> dict:
    key = jax.random.key(seed)
    ks = iter(jax.random.split(key, 32))
    L = DEPTH
    D = D_MODEL

    def nrm(shape, scale):
        return jax.random.normal(next(ks), shape, jnp.float32) * scale

    return {
        'x': nrm((BATCH, SEQ, D), 1.0),
        'p': nrm((L, BATCH, SEQ, PLE_DIM), 1.0),
        'positions': jnp.broadcast_to(jnp.arange(SEQ, dtype=jnp.int32), (BATCH, SEQ)),
        'attn_norm_w': 1.0 + nrm((L, D), 0.02),
        'w_in': nrm((L, D, IN_WIDTH), D ** -0.5),
        'fox_f_bias': jnp.linspace(1.0, 6.0, FOX_HEADS, dtype=jnp.float32)[None, :] + nrm((L, FOX_HEADS), 0.1),
        'fox_q_norm_w': 1.0 + nrm((L, FOX_HD), 0.02),
        'fox_k_norm_w': 1.0 + nrm((L, FOX_HD), 0.02),
        'nsa_q_norm_w': 1.0 + nrm((L, NSA_HD), 0.02),
        'nsa_k_norm_w': 1.0 + nrm((L, NSA_HD), 0.02),
        'nsa_cmp_pos': nrm((L, 2, CMP_LEN, NSA_HD), 0.1),
        'nsa_cmp_w': nrm((L, 2, CMP_LEN * NSA_HD, NSA_HD), (CMP_LEN * NSA_HD) ** -0.5),
        'diff_q_norm_w': 1.0 + nrm((L, DIFF_QK), 0.02),
        'diff_k_norm_w': 1.0 + nrm((L, DIFF_QK), 0.02),
        'diff_lambda': nrm((L, 4, DIFF_QK), 0.1),
        'diff_subln_w': 1.0 + nrm((L, DIFF_V), 0.02),
        'w_out': nrm((L, MIX_WIDTH, D), MIX_WIDTH ** -0.5),
        'ffn_norm_w': 1.0 + nrm((L, D), 0.02),
        'peer_w_q': nrm((L, D, PEER_HEADS * PEER_DQ), D ** -0.5),
        'peer_sub_keys': nrm((L, PEER_HEADS, 2, PEER_NKEYS, PEER_DQ // 2), (PEER_DQ // 2) ** -0.5),
        'peer_u': nrm((L, PEER_EXPERTS, D), D ** -0.5),
        'peer_v': nrm((L, PEER_EXPERTS, D), PEER_TOPK ** -0.5),
        'ple_norm_w': 1.0 + nrm((L, D), 0.02),
        'ple_w_gate': nrm((L, D, D), D ** -0.5),
        'ple_w_proj': nrm((L, PLE_DIM, D), PLE_DIM ** -0.5),
    }

def reference(x, p, positions, attn_norm_w, w_in, fox_f_bias, fox_q_norm_w, fox_k_norm_w,
              nsa_q_norm_w, nsa_k_norm_w, nsa_cmp_pos, nsa_cmp_w, diff_q_norm_w, diff_k_norm_w,
              diff_lambda, diff_subln_w, w_out, ffn_norm_w, peer_w_q, peer_sub_keys, peer_u, peer_v,
              ple_norm_w, ple_w_gate, ple_w_proj):
    b, s, _ = x.shape
    h = x
    for i in range(DEPTH):
        a = rmsnorm(h, attn_norm_w[i])
        proj = a @ w_in[i]
        (fq, fk, fv, ff, nq, nkc, nvc, nks, nvs, nkw, nvw, ng, dq, dk, dv) = split_proj(proj)
        fq = rmsnorm(fq.reshape(b, s, FOX_HEADS, FOX_HD), fox_q_norm_w[i])
        fk = rmsnorm(fk.reshape(b, s, FOX_HEADS, FOX_HD), fox_k_norm_w[i])
        fv = fv.reshape(b, s, FOX_HEADS, FOX_HD)
        o_fox = fox_attention(fq, fk, fv, ff + fox_f_bias[i])
        kv_shape = (b, s, NSA_KV, NSA_HD)
        o_nsa = nsa_attention(nq.reshape(b, s, NSA_HEADS, NSA_HD), nkc.reshape(kv_shape), nvc.reshape(kv_shape),
                              nks.reshape(kv_shape), nvs.reshape(kv_shape), nkw.reshape(kv_shape), nvw.reshape(kv_shape),
                              ng.reshape(b, s, NSA_HEADS, 3), positions, nsa_q_norm_w[i], nsa_k_norm_w[i],
                              nsa_cmp_pos[i], nsa_cmp_w[i])
        o_diff = diff_attention(dq, dk, dv, positions, diff_q_norm_w[i], diff_k_norm_w[i], diff_lambda[i],
                                diff_subln_w[i], diff_lambda_init(i))
        mix = jnp.concatenate([o_fox.reshape(b, s, -1), o_nsa.reshape(b, s, -1), o_diff.reshape(b, s, -1)], axis=-1)
        h = h + mix @ w_out[i]
        h = h + peer_ffn(rmsnorm(h, ffn_norm_w[i]), peer_w_q[i], peer_sub_keys[i], peer_u[i], peer_v[i])
        gate = jax.nn.sigmoid((rmsnorm(h, ple_norm_w[i]) @ ple_w_gate[i]).astype(jnp.float32)).astype(h.dtype)
        h = h + gate * (p[i] @ ple_w_proj[i])
    return h


_drawn_inputs = setup_inputs


def setup_inputs(seed=0):
    import zlib

    import numpy as np

    out = dict(_drawn_inputs(seed))
    spreads = {}
    factors = {'fox_q_norm_w': 5.907,
     'fox_k_norm_w': 5.855,
     'nsa_q_norm_w': 5.749,
     'nsa_k_norm_w': 5.507,
     'diff_q_norm_w': 3.933,
     'diff_k_norm_w': 4.099,
     'diff_subln_w': 3.447,
     'ple_norm_w': 7.573}
    for name, (base, spread) in spreads.items():
        noise = np.random.default_rng([zlib.crc32(name.encode()), seed]).standard_normal(out[name].shape)
        drawn = base * np.exp(spread * noise) if base else spread * noise
        out[name] = jnp.asarray(drawn.astype(out[name].dtype))
    for name, factor in factors.items():
        out[name] = (out[name] * factor).astype(out[name].dtype)
    return out
```

```python
from contextlib import ExitStack

import numpy as np

import concourse.bass as bass
from concourse import mybir

F32 = mybir.dt.float32
F32R = mybir.dt.float32r
I32 = mybir.dt.int32
U32 = mybir.dt.uint32
ALU = mybir.AluOpType
ACT = mybir.ActivationFunctionType
AX = mybir.AxisListType.X

P = 128
D = 1024
SEQ = 256
T = SEQ // P
DC = D // P
LAYERS = 2
PLE = 256
EPS = 1e-6
THETA = 10000.0
FOX_H, NSA_H, DIFF_H = 4, 8, 4
HD, DQK = 64, 32
CMP_LEN, CMP_STRIDE = 32, 16
NCMP = (SEQ - CMP_LEN) // CMP_STRIDE + 1
NCP = 16
NKEYS, TOPK, PH = 128, 16, 8
HC = PH * 2
BIG = 1.0e30

C_FQ, C_FK, C_NQ, C_KS, C_KW, C_DQ, C_DK = 0, 256, 512, 1024, 1152, 1280, 1536
C_KC, C_VC, C_FV, C_DV, C_VS, C_VW, C_FF, C_NG = 1792, 1920, 2048, 2304, 2560, 2688, 2816, 2820
PW = 2844
G64, G32 = C_DQ // HD, (C_KC - C_DQ) // DQK
NG = G64 + G32
ROPE64 = (C_DQ - C_NQ) // HD
ROPE32 = G32
PAIRED = [0, 4, 1, 5, 2, 6, 3, 7]

SLOT = 2048
RING = 4
CHUNK = 256
N_IN = -(-PW // CHUNK)
N_CMP, N_OUT, N_Q, N_KEYS, N_EXP, N_PLEP, N_PLEG = 2, D // CHUNK, HC * P // CHUNK, 1, 128, 1, D // CHUNK
S_IN = 0
S_CMP = S_IN + N_IN
S_OUT = S_CMP + N_CMP
S_Q = S_OUT + N_OUT
S_KEYS = S_Q + N_Q
S_EXP = S_KEYS + N_KEYS
S_PLEP = S_EXP + N_EXP
S_PLEG = S_PLEP + N_PLEP
SLOTS = S_PLEG + N_PLEG
assert SLOTS % RING == 0

PAIRS = NKEYS // 2
QUARTERS = 4
QI = NKEYS // QUARTERS
QP = PAIRS // QUARTERS
TB = 16
NB = SEQ // TB
assert NB == QP

M_NORM = 0
M_FB = M_NORM + C_KC
M_KN = M_FB + FOX_H
M_SUB = M_KN + 2 * HD
M_LAM = M_SUB + DIFF_H * 2 * DQK
M_COL = M_LAM + 4 * DQK
M_POS = M_COL + 3 * DC
M_PT = M_POS + 2 * CMP_LEN
SMALL = M_PT + 2 * SEQ

K_ID = 0
K_TRI = K_ID + P
K_ONE = K_TRI + P
K_MASK = K_ONE + P
K_IOTA = K_MASK + SEQ
K_BLK = K_IOTA + P
K_REP = K_BLK + NSA_H
K_CM = K_REP + P
K_CV = K_CM + T * NCP
K_F64 = K_CV + T
K_F32 = K_F64 + HD // 2
K_LI = K_F32 + DQK // 2
CONST = K_LI + 2 * LAYERS
NANG = HD // 2 + DQK // 2

A_PROJ = 0
A_SQ = 5696
A_O = A_SQ
A_ROPE = A_SQ + T * C_KC
A_OC = A_O + 28 * T * HD
A_TMP = 11840
A_VBD, A_KCX, A_KCS = A_TMP, A_TMP + 512, A_TMP + 640
A_FA = 12608
A_FT = 13664
A_QNT, A_QRT, A_KSW, A_KCV, A_DQ, A_DK = (A_FT + x for x in (2048, 3072, 4096, 4608, 5120, 5632))
A_X = A_FT + 6144
A_P = A_X + 1024
A_PT = A_P + 4 * 384
A_MIX = 0
A_MIXT = A_FT
A_COMB = 11328
A_XN, A_XSQ = 20480, 22528
A_PQ, A_SC, A_CAND, A_EQ = 0, 4096, 8192, 12288
A_B = 16384
A_A = A_B + 2 * TB * P
A_GL = A_A + 2 * TB * QI
A_W = A_GL + 2 * 512
ARENA = A_W + 2 * 512
A_RT = A_B
assert A_PT + 3 * 384 <= ARENA and A_XSQ + 1024 <= ARENA

U_FOX, U_SLC, U_WIN, U_DIFF, UNITS = 0, 4, 12, 20, 28
TWO_PI = 2 * np.pi
PI_C = [6.28125, 0.00193500518798828125, 3.01991438e-07]
MAGIC = float(1.5 * 2 ** 23)


def u_slot(p):
    return S_EXP + (2 * p - 1 if p else 0)


def v_slot(p):
    return S_EXP + (2 * p + 2 if p < PAIRS - 1 else 2 * p + 1)


def trunk(nc, x, positions, small, consts, stream, out):
    ctx = ExitStack()
    with ctx:
        def sb(name, shape, dt=F32):
            return ctx.enter_context(nc.sbuf_tensor(name, shape, dt))

        def sem(name):
            return ctx.enter_context(nc.semaphore(name))

        h = sb("h", [P, T, D])
        xT = sb("xT", [P, DC, SEQ])
        ring = sb("ring", [P, RING, SLOT])
        arena = sb("arena", [P, ARENA])
        kst = sb("kst", [P, CONST])
        sm = sb("sm", [P, LAYERS, SMALL])
        routT = sb("routT", [P, 3, SEQ])
        posi = sb("posi", [P, T], I32)
        posf = sb("posf", [P, T])
        ang = sb("ang", [P, T, NANG])
        angk = sb("angk", [P, T, NANG])
        sin = sb("sin", [P, T, NANG])
        cos = sb("cos", [P, T, NANG])
        lamp = sb("lamp", [P, LAYERS, 2, DQK])
        lams = sb("lams", [P, LAYERS, 2])
        lame = sb("lame", [P, LAYERS, 2])
        lam = sb("lam", [P, LAYERS])
        ss = sb("ss", [P, T])
        rstd = sb("rstd", [P, 3, T])
        gss = sb("gss", [P, 3, T, NG])
        fl = sb("fl", [P, 6, T, FOX_H])
        cum = sb("cum", [P, T, FOX_H])
        kst4 = sb("kst4", [P, 4, 2])
        kcT = sb("kcT", [P, NCP])
        vcx = sb("vcx", [P, 2 * HD])
        pc = sb("pc", [P, T, NSA_H, NCP])
        pcT = sb("pcT", [P, T, P])
        cst = sb("cst", [P, 3, T, NSA_H])
        nmax = sb("nmax", [P, UNITS, T])
        den = sb("den", [P, UNITS, T])
        rden = sb("rden", [P, UNITS, T])
        gate = sb("gate", [P, T, 3, NSA_H])
        cf = sb("cf", [P, T, 3, NSA_H])
        dst = sb("dst", [P, 3, T, DIFF_H])
        zeros = sb("zeros", [P, 512], mybir.dt.bfloat16)

        psum = ctx.enter_context(nc.psum_tensor("psum", [P, 8, 512], F32))

        def ar(off, *dims, parts=P):
            n = int(np.prod(dims))
            v = arena[0:parts, off:off + n]
            if len(dims) == 1:
                return v
            names = "abcd"[:len(dims)]
            return v.rearrange(f"p ({' '.join(names)}) -> p {' '.join(names)}", **dict(zip(names[1:], dims[1:])))

        def bank(b, *dims, parts=P, at=0):
            n = int(np.prod(dims))
            v = psum[0:parts, b, at:at + n]
            if len(dims) == 1:
                return v
            names = "abcd"[:len(dims)]
            return v.rearrange(f"p ({' '.join(names)}) -> p {' '.join(names)}", **dict(zip(names[1:], dims[1:])))

        def last(v, n):
            return v.unsqueeze(len(v.shape)).to_broadcast(list(v.shape) + [n])

        def mid(v, at, n):
            s = list(v.shape)
            return v.unsqueeze(at).to_broadcast(s[:at] + [n] + s[at:])

        ident = kst[:, K_ID:K_ID + P]
        proj = ar(A_PROJ, T, PW)
        rope = ar(A_ROPE, T, C_KC - C_NQ)
        fa = ar(A_FA, T, 2, FOX_H, HD + 2)
        fT = ar(A_FT, 2, FOX_H, SEQ)
        qnT = ar(A_QNT, 4, SEQ)
        qrT = ar(A_QRT, 4, SEQ)
        kswT = ar(A_KSW, 2, SEQ)
        kcvT = ar(A_KCV, 2, SEQ)
        dqT = ar(A_DQ, 2, SEQ)
        dkT = ar(A_DK, 2, SEQ)
        X = ar(A_X, 2, CMP_LEN, NCP)
        vbd = ar(A_VBD, NSA_H, HD)
        O = ar(A_O, UNITS, T, HD)
        Oc = ar(A_OC, T, NSA_H, HD)
        mix = ar(A_MIX, T, D)
        mixT = ar(A_MIXT, DC, SEQ)
        Pb = ar(A_P, 4, 384)
        PTb = ar(A_PT, 3, 384)
        xn = ar(A_XN, T, D)
        pqT = ar(A_PQ, HC, SEQ)
        sc = ar(A_SC, T, HC, NKEYS)
        cand = ar(A_CAND, T, PH, TOPK * TOPK)
        Bh = ar(A_B, 2, TB, P)
        Ah = ar(A_A, 2, TB, QI)
        GL = ar(A_GL, 2, 512)
        W = ar(A_W, 2, 2, SEQ)
        v16 = ar(A_RT, T, HC, TOPK)
        i16 = ar(A_RT + 512, T, HC, TOPK).bitcast(U32)
        i16f = ar(A_RT + 1024, T, HC, TOPK)
        c16 = ar(A_RT + 1536, T, PH, TOPK)
        p16 = ar(A_RT + 1792, T, PH, TOPK).bitcast(U32)
        ab16 = ar(A_RT + 2048, 2, T, PH * TOPK).bitcast(U32)
        abf = ar(A_RT + 2560, 2, T, PH * TOPK)
        rout = ar(A_RT + 3072, 3, T, PH * TOPK)
        gden = ar(A_RT + 3840, 2, T, PH)

        ld_x, ld_small, ld_const, ld_pos = sem("ld_x"), sem("ld_small"), sem("ld_const"), sem("ld_pos")
        slot_ld = [sem(f"slot_ld{i}") for i in range(RING)]
        slot_used = sem("slot_used")
        zero_ok = sem("zero_ok")
        ang_ok, sin_ok, lam_in, lam_exp = sem("ang_ok"), sem("sin_ok"), sem("lam_in"), sem("lam_exp")
        h_ok = sem("h_ok")
        ss_ok, ms_ok, rt_ok, xn_ok, xt_ps, xt_ok = (sem(n) for n in ("ss_ok", "ms_ok", "rt_ok", "xn_ok", "xt_ps", "xt_ok"))
        pj_dve, pj_act = sem("pj_dve"), sem("pj_act")
        psq_ok, gms_ok, grt_ok = sem("psq_ok"), sem("gms_ok"), sem("grt_ok")
        ff_in, ff_ln, ff_ls, ff_ps = sem("ff_in"), sem("ff_ln"), sem("ff_ls"), sem("ff_ps")
        tok_ok, tb_ps, tb_dve, tb_act = sem("tok_ok"), sem("tb_ps"), sem("tb_dve"), sem("tb_act")
        x_ok, kc_ms, kc_rt, kc_tok, kc_ps, kcT_ok = (sem(n) for n in ("x_ok", "kc_ms", "kc_rt", "kc_tok", "kc_ps", "kcT_ok"))
        cs_ps, cs_ok, ce_ok, pcT_ps, pcT_ok, oc_ps, oc_ok = (sem(n) for n in ("cs_ps", "cs_ok", "ce_ok", "pcT_ps", "pcT_ok", "oc_ps", "oc_ok"))
        s_ps, neg_ok, p_ok, pt_ps, pt_ok, pv_ps, o_ok = (sem(n) for n in ("s_ps", "neg_ok", "p_ok", "pt_ps", "pt_ok", "pv_ps", "o_ok"))
        gate_ok, dms_ok, drt_ok, mix_ok, mt_ps, mt_ok = (sem(n) for n in ("gate_ok", "dms_ok", "drt_ok", "mix_ok", "mt_ps", "mt_ok"))
        q_ok, sc_ps, sc_ok = sem("q_ok"), sem("sc_ps"), sem("sc_ok")
        ge_in, ge_ok, rout_ok, rout_ps, rout_dve = (sem(n) for n in ("ge_in", "ge_ok", "rout_ok", "rout_ps", "rout_dve"))
        b_ok, a1_ok, a_ok, g_ps, g_ok = (sem(n) for n in ("b_ok", "a1_ok", "a_ok", "g_ps", "g_ok"))
        gelu_ok, w_ok, acc_ps = sem("gelu_ok"), sem("w_ok"), sem("acc_ps")
        sg_ok = sem("sg_ok")
        dve_step, act_step = sem("dve_step"), sem("act_step")
        out_st = sem("out_st")

        def used(eng, L, n):
            eng.wait_ge(slot_used, L * SLOTS + n + 1)

        block = ctx.enter_context(nc.Block())

        @block.sync
        def _(sp):
            for s in range(RING):
                sp.dma_start(ring[:, s, :], stream[s]).then_inc(slot_ld[s], 16)
            with sp.Fori(1, LAYERS * SLOTS // RING) as i:
                for s in range(RING):
                    sp.wait_ge(slot_used, RING * i + (s - RING + 1))
                    sp.dma_start(ring[:, s, :], stream[RING * i + s]).then_inc(slot_ld[s], 16)

        @block.tensor
        def _(pe):
            def slot(L, n):
                n += L * SLOTS
                pe.wait_ge(slot_ld[n % RING], 16 * (n // RING + 1))
                return ring[:, n % RING, :]

            def transposes(L, j):
                n = 3 * L + j
                pe.wait_ge(xn_ok, n + 1)
                for b in range(DC // 2):
                    for c in range(2):
                        for t in range(T):
                            k = 2 * b + c
                            ins = pe.transpose(bank(b, P, at=c * SEQ + t * P), xn[:, t, k * P:(k + 1) * P], ident)
                    ins.then_inc(xt_ps, 1)

            def token_major(b, w, src, n=CHUNK):
                wv = w[:, 0:DC * n].rearrange("p (k n) -> p k n", k=DC)
                for t in range(T):
                    for k in range(DC):
                        ins = pe.matmul(bank(b, n, at=t * CHUNK), src[:, k, t * P:(t + 1) * P], wv[:, k, :],
                                        start=(k == 0), stop=(k == DC - 1))
                return ins

            def rows_of(u):
                if u < U_SLC:
                    v = C_FV + u * HD
                    return fT[0:HD + 2, 0, u, :], fT[0:HD + 2, 1, u, :], v
                if u < U_DIFF:
                    kind, j = (u - U_SLC) // NSA_H, (u - U_SLC) % NSA_H
                    r = slice(HD * (j % 2), HD * (j % 2) + HD)
                    return qrT[r, j // 2, :], kswT[r, kind, :], (C_VS, C_VW)[kind] + (j % 2) * HD
                c = u - U_DIFF
                r = slice(DQK * (c % 4), DQK * (c % 4) + DQK)
                return dqT[r, c // 4, :], dkT[r, c // 4, :], C_DV + (c // 2) * HD

            pe.wait_ge(ld_const, 16)
            pe.wait_ge(ld_small, 16)
            pe.wait_ge(zero_ok, 1)
            for L in range(LAYERS):
                transposes(L, 0)
                pe.wait_ge(xt_ok, 4 * (3 * L) + 4)
                for i in range(N_IN):
                    w = slot(L, S_IN + i)
                    if i >= 4:
                        pe.wait_ge((pj_dve, pj_act)[i % 2], L * N_IN // 2 + (i - 4) // 2 + 1)
                    ins = token_major(4 + i % 4, w, xT, min(CHUNK, PW - i * CHUNK))
                    ins.then_inc(slot_used, 1)
                pe.wait_ge(ff_ls, L + 1)
                tri, one = kst[:, K_TRI:K_TRI + P], kst[:, K_ONE:K_ONE + P]
                pe.matmul(bank(0, FOX_H), tri, fl[:, 5, 0, :], start=True, stop=True)
                pe.matmul(bank(0, FOX_H, at=FOX_H), one, fl[:, 5, 0, :], start=True, stop=False)
                pe.matmul(bank(0, FOX_H, at=FOX_H), tri, fl[:, 5, 1, :], start=False, stop=True).then_inc(ff_ps, 1)
                pe.wait_ge(tok_ok, L + 1)
                NQ0 = [C_NQ + i * P for i in range(4)]
                batches = [[proj[:, t, c:c + P] for c in (C_KC, C_VC) for t in range(T)]]
                batches += [[proj[:, t, c:c + P] for c in NQ0] for t in range(T)]
                batches += [[rope[:, t, c - C_NQ:c - C_NQ + P] for c in (C_KS, C_KW) for t in range(T)]]
                batches += [[rope[:, t, c - C_NQ:c - C_NQ + P] for c in NQ0] for t in range(T)]
                batches += [[fa[:, t, s, i, :] for i in range(FOX_H)] for s in range(2) for t in range(T)]
                batches += [[rope[:, t, c - C_NQ + b * P:c - C_NQ + (b + 1) * P] for b in range(2) for t in range(T)]
                            for c in (C_DQ, C_DK)]
                for n, batch in enumerate(batches):
                    if n >= 4:
                        pe.wait_ge((tb_act, tb_dve)[n % 2], 6 * L + (n - 4) // 2 + 1)
                    for i, src in enumerate(batch):
                        rows = src.shape[1]
                        ins = pe.transpose(bank(n % 4, P, parts=rows, at=i * P), src, ident)
                    ins.then_inc(tb_ps, 1)
                pe.wait_ge(x_ok, L + 1)
                for kv in range(2):
                    w = slot(L, S_CMP + kv)
                    for g in range(2):
                        r = slice(HD * g, HD * g + HD)
                        for l in range(CMP_LEN):
                            ins = pe.matmul(bank(4 + g, HD, parts=NCP, at=kv * HD), X[r, kv, l, :],
                                            w[r, l * HD:(l + 1) * HD], start=(l == 0), stop=(l == CMP_LEN - 1))
                    ins.then_inc(slot_used, 1)
                pe.wait_ge(kc_tok, L + 1)
                pe.transpose(bank(4, NCP, at=256), ar(A_KCX, 2 * HD, parts=NCP), ident[0:NCP, 0:NCP])
                pe.matmul(bank(5, 2 * HD, at=256), kst[0:NCP, K_REP:K_REP + P], vcx[0:NCP, :], start=True, stop=True).then_inc(kc_ps, 1)
                pe.wait_ge(kcT_ok, L + 1)
                pe.wait_ge(tb_act, 6 * L + 6)
                pe.wait_ge(tb_dve, 6 * L + 6)
                for g in range(2):
                    r = slice(HD * g, HD * g + HD)
                    for t in range(T):
                        for j in range(4):
                            ins = pe.matmul(bank(4 + g, NCP, at=(4 * t + j) * NCP), qnT[r, j, t * P:(t + 1) * P],
                                            kcT[r, :], start=True, stop=True)
                ins.then_inc(cs_ps, 1)
                for s in range(UNITS + 3):
                    if s < UNITS:
                        q, k, _ = rows_of(s)
                        if s >= 4:
                            pe.wait_ge(neg_ok, UNITS * L + s - 3)
                        pe.matmul(bank(s % 4, P), q[:, 0:P], k[:, 0:P], start=True, stop=True)
                        pe.matmul(bank(s % 4, SEQ, at=P), q[:, P:SEQ], k, start=True, stop=True).then_inc(s_ps, 1)
                    if s == 1:
                        pe.wait_ge(ce_ok, L + 1)
                        for t in range(T):
                            ins = pe.transpose(bank(4, P, at=t * P), pc[:, t, :, :].rearrange("p j n -> p (j n)"), ident)
                        ins.then_inc(pcT_ps, 1)
                        pe.wait_ge(pcT_ok, L + 1)
                        for t in range(T):
                            ins = pe.matmul(bank(6 + t, 512), pcT[:, t, :], vbd.rearrange("p j d -> p (j d)"),
                                            start=True, stop=True)
                        ins.then_inc(oc_ps, 1)
                    u = s - 2
                    if 0 <= u < UNITS:
                        pe.wait_ge(p_ok, UNITS * L + u + 1)
                        if u >= 2:
                            pe.wait_ge(pt_ok, UNITS * L + u - 1)
                        for i in range(3):
                            ins = pe.transpose(bank(4 + u % 2, P, at=i * P), Pb[:, u % 4, i * P:(i + 1) * P], ident)
                        ins.then_inc(pt_ps, 1)
                    u = s - 3
                    if 0 <= u < UNITS:
                        _, _, v = rows_of(u)
                        if u == 0:
                            pe.wait_ge(oc_ok, L + 1)
                        if u % 4 == 0 and u >= 8:
                            pe.wait_ge(o_ok, 7 * L + u // 4 - 1)
                        pe.wait_ge(pt_ok, UNITS * L + u + 1)
                        o = [bank(6 + u // 4 % 2, HD, at=(u % 4) * P + t * HD) for t in range(T)]
                        PT = PTb[:, u % 3, :]
                        pe.matmul(o[0], PT[:, 0:P], proj[:, 0, v:v + HD], start=True, stop=True)
                        pe.matmul(o[1], PT[:, P:2 * P], proj[:, 0, v:v + HD], start=True, stop=False)
                        pe.matmul(o[1], PT[:, 2 * P:3 * P], proj[:, 1, v:v + HD], start=False, stop=True).then_inc(pv_ps, 1)
                pe.wait_ge(mix_ok, L + 1)
                for b in range(4):
                    for c in range(2):
                        for t in range(T):
                            k = 2 * b + c
                            ins = pe.transpose(bank(b, P, at=c * SEQ + t * P), mix[:, t, k * P:(k + 1) * P], ident)
                    ins.then_inc(mt_ps, 1)
                pe.wait_ge(mt_ok, 4 * L + 4)
                for i in range(N_OUT):
                    ins = token_major(4 + i, slot(L, S_OUT + i), mixT)
                    ins.then_inc(slot_used, 1)
                transposes(L, 1)
                pe.wait_ge(xt_ok, 4 * (3 * L + 1) + 4)
                for i in range(N_Q):
                    w = slot(L, S_Q + i).rearrange("p (k n) -> p k n", k=DC)
                    if i >= 4:
                        pe.wait_ge(q_ok, N_Q * L + i - 3)
                    for c in range(2):
                        for k in range(DC):
                            ins = pe.matmul(bank(i % 4, SEQ, at=c * SEQ), w[:, k, c * P:(c + 1) * P], xT[:, k, :],
                                            start=(k == 0), stop=(k == DC - 1))
                    ins.then_inc(slot_used, 1)
                keys = slot(L, S_KEYS).rearrange("p (m n) -> p m n", m=HC)
                for n in range(8):
                    g, t = n // 2, n % 2
                    pe.wait_ge(q_ok, N_Q * L + 2 * g + 2)
                    if n >= 4:
                        pe.wait_ge(sc_ok, 8 * L + n - 3)
                    for j in range(4):
                        m = 4 * g + j
                        ins = pe.matmul(bank(4 + n % 4, P, at=j * P), pqT[:, m, t * P:(t + 1) * P], keys[:, m, :],
                                        start=True, stop=True)
                    ins.then_inc(sc_ps if n < 7 else slot_used, 1)
                pe.wait_ge(rout_ok, L + 1)
                for k in range(3):
                    for t in range(T):
                        ins = pe.transpose(bank(4 + k // 2, P, at=(k % 2) * SEQ + t * P), rout[:, k, t, :], ident)
                ins.then_inc(rout_ps, 1)
                pe.wait_ge(sc_ok, 8 * L + 8)
                for b in range(4):
                    ins = pe.matmul(bank(b, 512), zeros[:, 0:P], zeros[:, :], start=True, stop=False, skip_group_check=True)

                def spread(n, par, first=False):
                    pe.wait_ge(b_ok, n + 1)
                    pe.wait_ge(a_ok, n + 1)
                    if not first:
                        pe.wait_ge(g_ok, n - 1)
                    for i in range(TB):
                        ins = pe.matmul(bank(6 + par, QI, at=i * QI), Bh[:, par, i, :], Ah[:, par, i, :],
                                        start=True, stop=True)
                    ins.then_inc(g_ps, 1)

                def hidden(i, p):
                    n = L * SLOTS + u_slot(p)
                    pe.wait_ge(slot_ld[n % RING], 16 * (i + n // RING + 1))
                    u = ring[:, n % RING, :].rearrange("p (e k n) -> p e k n", e=2, k=DC)
                    if p + L > 1 or not isinstance(i, int):
                        pe.wait_ge(gelu_ok, L * PAIRS + 2 * i + p - 1)
                    for e in range(2):
                        for k in range(DC):
                            ins = pe.matmul(bank(4 + p % 2, SEQ, at=e * SEQ), u[:, e, k, :], xT[:, k, :],
                                            start=(k == 0), stop=(k == DC - 1))
                    ins.then_inc(slot_used, 1)

                def weighted(i, p, par):
                    n = L * SLOTS + v_slot(p)
                    pe.wait_ge(slot_ld[n % RING], 16 * (i + n // RING + 1))
                    v = ring[:, n % RING, :].rearrange("p (e n) -> p e n", e=2)
                    pe.wait_ge(w_ok, L * PAIRS + 2 * i + p + 1)
                    for e in range(2):
                        for t in range(T):
                            for half in range(2):
                                ins = pe.matmul(bank(2 * t + half, 512), W[:, par, e, t * P:(t + 1) * P],
                                                v[:, e, half * 512:(half + 1) * 512], start=False, stop=False,
                                                skip_group_check=True)
                    ins.then_inc(slot_used, 1)

                pe.wait_ge(rout_dve, L + 1)
                hidden(0, 0)
                for n in range(NB):
                    spread(L * NB * QUARTERS + n, n % 2, first=(n < 2))

                def two_pairs(i, quarter):
                    for k in range(2):
                        p = quarter * QP + k
                        if quarter < QUARTERS - 1:
                            spread(L * NB * QUARTERS + (quarter + 1) * NB + 2 * i + k, k)
                        hidden(i, p + 1)
                        weighted(i, p, k)

                two_pairs(0, 0)
                for quarter in range(QUARTERS):
                    with pe.Fori(int(quarter == 0), QP // 2 - (quarter == QUARTERS - 1)) as i:
                        two_pairs(i, quarter)
                p = PAIRS - 2
                hidden(0, p + 1)
                weighted(0, p, 0)
                weighted(0, p + 1, 1)
                for b in range(4):
                    ins = pe.matmul(bank(b, 512), zeros[:, 0:P], zeros[:, :], start=False, stop=True, skip_group_check=True)
                ins.then_inc(acc_ps, 1)
                transposes(L, 2)
                pe.wait_ge(xt_ok, 4 * (3 * L + 2) + 4)
                wp = slot(L, S_PLEP).rearrange("p (c n) -> p c n", c=2)
                pT = sm[:, L, M_PT:M_PT + 2 * SEQ].rearrange("p (c n) -> p c n", c=2)
                for i in range(N_PLEG):
                    for t in range(T):
                        for c in range(2):
                            ins = pe.matmul(bank(i, CHUNK, at=t * CHUNK), pT[:, c, t * P:(t + 1) * P],
                                            wp[:, c, i * CHUNK:(i + 1) * CHUNK], start=(c == 0), stop=(c == 1))
                ins.then_inc(slot_used, 1)
                for i in range(N_PLEG):
                    ins = token_major(4 + i, slot(L, S_PLEG + i), xT)
                    ins.then_inc(slot_used, 1)

        @block.scalar
        def _(act):
            act.dma_start(kst[:, :], consts).then_inc(ld_const, 16)
            act.dma_start(h[:, :, :], x.rearrange("o (t p) d -> p (o t) d", p=P)).then_inc(ld_x, 16)
            act.dma_start(posi[:, :], positions.rearrange("o (t p) -> p (o t)", p=P),
                          allow_slow_non_contiguous=True).then_inc(ld_pos, 16)
            act.dma_start(sm[:, :, :], small.rearrange("l p n -> p l n")).then_inc(ld_small, 16)

            def square_rows(L, j):
                n = 3 * L + j
                if n:
                    act.wait_ge(h_ok, n)
                else:
                    act.wait_ge(ld_x, 16)
                for t in range(T):
                    if n or t:
                        act.wait_ge(ss_ok, 2 * n + t)
                    act.activation(ar(A_XSQ, D), h[:, t, :], ACT.Square, accum_out=ss[:, t:t + 1]).then_inc(ss_ok, 1)
                act.wait_ge(ms_ok, n + 1)
                act.activation(rstd[:, 1, :], rstd[:, 0, :], ACT.Sqrt).then_inc(rt_ok, 1)

            act.wait_ge(ang_ok, 1)
            act.activation(sin[:, :, :], ang[:, :, :], ACT.Sin)
            act.activation(cos[:, :, :], ang[:, :, :], ACT.Sin, scale=0.5).then_inc(sin_ok, 1)
            act.wait_ge(lam_in, 1)
            act.activation(lame[:, :, :], lams[:, :, :], ACT.Exp).then_inc(lam_exp, 1)

            for L in range(LAYERS):
                square_rows(L, 0)
                for i in range(1, N_IN, 2):
                    used(act, L, S_IN + i)
                    n = min(CHUNK, PW - i * CHUNK)
                    act.activation(proj[:, :, i * CHUNK:i * CHUNK + n], bank(4 + i % 4, T, CHUNK)[:, :, 0:n],
                                   ACT.Copy).then_inc(pj_act, 1)
                    if i == 7:
                        act.wait_ge(pj_dve, N_IN // 2 * L + 4)
                        act.wait_ge(pj_act, N_IN // 2 * L + 3)
                        for t in range(T):
                            act.activation(ar(A_SQ, T, C_KC)[:, t, :], proj[:, t, 0:C_KC], ACT.Square).then_inc(psq_ok, 1)
                act.wait_ge(gms_ok, L + 1)
                act.activation(gss[:, 1, :, :], gss[:, 0, :, :], ACT.Sqrt).then_inc(grt_ok, 1)
                act.wait_ge(ff_in, L + 1)
                act.activation(fl[:, 3, :, :], fl[:, 2, :, :], ACT.Exp).then_inc(act_step, 1)
                act.wait_ge(act_step, L + 1)
                act.activation(fl[:, 4, :, :], fl[:, 3, :, :], ACT.Ln, bias=1.0).then_inc(ff_ln, 1)
                act.wait_ge(pj_dve, N_IN // 2 * (L + 1))
                act.wait_ge(pj_act, N_IN // 2 * (L + 1))
                act.activation(gate[:, :, :, :].rearrange("p t k j -> p t (k j)"), proj[:, :, C_NG:PW],
                               ACT.Sigmoid).then_inc(gate_ok, 1)
                for n in range(0, 12, 2):
                    act.wait_ge(tb_ps, 12 * L + n + 1)
                    if n == 0:
                        dst_ = kcvT.rearrange("p k t -> p (k t)")
                    elif n in (2, 4):
                        dst_ = (qnT, qrT)[n // 4][:, :, (1 if n == 2 else 0) * P:][:, :, 0:P]
                    elif n in (6, 8):
                        dst_ = fT[0:HD + 2, n // 2 - 3, :, 0:P]
                    else:
                        dst_ = dqT.rearrange("p k t -> p (k t)")
                    rows = HD + 2 if n in (6, 8) else P
                    src = bank(n % 4, 4, P, parts=rows) if n in (2, 4, 6, 8) else bank(n % 4, 512)
                    act.activation(dst_, src, ACT.Copy).then_inc(tb_act, 1)
                act.wait_ge(kc_ms, L + 1)
                act.activation(kst4[0:NCP, 2, :], kst4[0:NCP, 1, :], ACT.Sqrt).then_inc(kc_rt, 1)
                act.wait_ge(cs_ok, L + 1)
                act.activation(pc[:, :, :, :], pc[:, :, :, :], ACT.Exp, scale=HD ** -0.5).then_inc(ce_ok, 1)
                act.wait_ge(pcT_ps, L + 1)
                act.activation(pcT[:, :, :], bank(4, T, P), ACT.Copy).then_inc(pcT_ok, 1)
                act.wait_ge(oc_ps, L + 1)
                act.activation(Oc.rearrange("p t j d -> p t (j d)"), psum[:, 6:8, :], ACT.Copy).then_inc(oc_ok, 1)
                for u in range(UNITS + 4):
                    if u < UNITS:
                        act.wait_ge(neg_ok, UNITS * L + u + 1)
                        Pu = Pb[:, u % 4, :]
                        act.activation(Pu[:, 0:P], Pu[:, 0:P], ACT.Exp, bias=nmax[:, u, 0:1], scale=-1.0,
                                       accum_out=den[:, u, 0:1])
                        act.activation(Pu[:, P:384], Pu[:, P:384], ACT.Exp, bias=nmax[:, u, 1:2], scale=-1.0,
                                       accum_out=den[:, u, 1:2]).then_inc(p_ok, 1)
                    if u >= 7 and u % 4 == 3:
                        g = (u - 7) // 4
                        act.wait_ge(pv_ps, UNITS * L + 4 * g + 4)
                        act.activation(O[:, 4 * g:4 * g + 4, :, :].rearrange("p u t d -> p (u t d)"),
                                       bank(6 + g % 2, 512), ACT.Copy).then_inc(o_ok, 1)
                act.wait_ge(dms_ok, L + 1)
                act.activation(dst[:, 1, :, :], dst[:, 0, :, :], ACT.Sqrt).then_inc(drt_ok, 1)
                for b in range(4):
                    act.wait_ge(mt_ps, 4 * L + b + 1)
                    act.activation(mixT[:, 2 * b:2 * b + 2, :], bank(b, 2, SEQ), ACT.Copy).then_inc(mt_ok, 1)
                square_rows(L, 1)
                for i in range(N_Q):
                    used(act, L, S_Q + i)
                    act.activation(pqT[:, 2 * i:2 * i + 2, :], bank(i % 4, 2, SEQ), ACT.Copy).then_inc(q_ok, 1)
                for n in range(8):
                    g, t = n // 2, n % 2
                    act.wait_ge(sc_ps, 7 * L + n + 1) if n < 7 else used(act, L, S_KEYS)
                    act.activation(sc[:, t, 4 * g:4 * g + 4, :], bank(4 + n % 4, 4, P), ACT.Copy).then_inc(sc_ok, 1)
                act.wait_ge(ge_in, L + 1)
                act.activation(c16, c16, ACT.Exp).then_inc(ge_ok, 1)

                def gelu(i, p, par):
                    used(act, L, u_slot(p) + 4 * i)
                    if p + L > 1 or not isinstance(i, int):
                        act.wait_ge(w_ok, L * PAIRS + 2 * i + p - 1)
                    act.activation(GL[:, par, :], bank(4 + par, 512), ACT.Gelu).then_inc(gelu_ok, 1)

                def gates_out(n, i, par, quarter):
                    act.wait_ge(g_ps, (L * QUARTERS + quarter) * NB + 2 * i + n + 1)
                    buf = ar((quarter % 2) * SEQ * QI, SEQ * QI)
                    act.activation(buf[:, bass.ds((2 * i + n) * TB * QI, TB * QI)], bank(6 + par, 512),
                                   ACT.Copy).then_inc(g_ok, 1)

                act.wait_ge(rout_dve, L + 1)
                for n in range(NB):
                    gates_out(n, 0, n % 2, 0)
                gelu(0, 0, 0)

                def two_pairs(i, quarter):
                    for k in range(2):
                        if quarter < QUARTERS - 1:
                            gates_out(k, i, k, quarter + 1)
                        gelu(i, quarter * QP + k + 1, (k + 1) % 2)

                two_pairs(0, 0)
                for quarter in range(QUARTERS):
                    if quarter:
                        act.wait_ge(w_ok, L * PAIRS + quarter * QP)
                    with act.Fori(int(quarter == 0), QP // 2 - (quarter == QUARTERS - 1)) as i:
                        two_pairs(i, quarter)
                gelu(0, PAIRS - 1, 1)
                square_rows(L, 2)
                for i in range(N_PLEG):
                    used(act, L, S_PLEG + i)
                    act.activation(ar(i * 512, 512), bank(4 + i, 512), ACT.Sigmoid).then_inc(sg_ok, 1)
            act.wait_ge(h_ok, 3 * LAYERS)
            act.dma_start(out.rearrange("o (t p) d -> p (o t) d", p=P), h[:, :, :]).then_inc(out_st, 16)
            act.wait_ge(out_st, 16)

        @block.gpsimd
        def _(pool):
            def gated(L, quarter, i, n, par):
                pool.wait_ge(a1_ok, (L * QUARTERS + quarter) * NB + 2 * i + n + 1)
                at = bass.ds((2 * i + n) * TB, TB)
                A = Ah[:, par, :, :]
                pool.tensor_tensor(A, A, last(routT[:, 2, at], QI), ALU.mult).then_inc(a_ok, 1)

            pool.memset(zeros[:, :], 0.0).then_inc(zero_ok, 1)
            for L in range(LAYERS):
                pool.wait_ge(rout_dve, L + 1)
                for n in range(NB):
                    gated(L, 0, 0, n, n % 2)
                for quarter in range(1, QUARTERS):
                    with pool.Fori(0, NB // 2) as i:
                        for k in range(2):
                            gated(L, quarter, i, k, k)

        @block.vector
        def _(dve):
            steps = [0]

            def step(ins):
                steps[0] += 1
                ins.then_inc(dve_step, 1)

            def settle():
                dve.wait_ge(dve_step, steps[0])

            def mean_rstd(L, j):
                n = 3 * L + j
                dve.wait_ge(ss_ok, 2 * n + 2)
                dve.tensor_scalar(rstd[:, 0, :], ss[:, :], 1.0 / D, EPS, ALU.mult, ALU.add).then_inc(ms_ok, 1)
                dve.wait_ge(rt_ok, n + 1)
                step(dve.reciprocal(rstd[:, 2, :], rstd[:, 1, :]))
                settle()
                for t in range(T):
                    ins = dve.tensor_scalar(xn[:, t, :], h[:, t, :], rstd[:, 2, t:t + 1], None, ALU.mult)
                ins.then_inc(xn_ok, 1)
                for b in range(4):
                    dve.wait_ge(xt_ps, 4 * n + b + 1)
                    w = sm[:, L, M_COL + j * DC + 2 * b:M_COL + j * DC + 2 * b + 2]
                    dve.tensor_tensor(xT[:, 2 * b:2 * b + 2, :], bank(b, 2, SEQ), last(w, SEQ), ALU.mult).then_inc(xt_ok, 1)

            dve.wait_ge(ld_pos, 16)
            dve.wait_ge(ld_const, 16)
            step(dve.tensor_copy(posf[:, :], posi[:, :]))
            settle()
            for t in range(T):
                step(dve.tensor_scalar(ang[:, t, :], kst[:, K_F64:K_F64 + NANG], posf[:, t:t + 1], None, ALU.mult))
            settle()
            step(dve.tensor_scalar(angk[:, :, :], ang[:, :, :], float(1 / TWO_PI), MAGIC, ALU.mult, ALU.add))
            settle()
            step(dve.tensor_scalar(angk[:, :, :], angk[:, :, :], -MAGIC, None, ALU.add))
            for c in PI_C:
                settle()
                step(dve.scalar_tensor_tensor(out=ang[:, :, :], in0=angk[:, :, :], scalar=-c, in1=ang[:, :, :],
                                              op0=ALU.mult, op1=ALU.add))
            settle()
            dve.tensor_scalar(ang[:, :, :], ang[:, :, :], 3.1415925, -3.1415925, ALU.min, ALU.max).then_inc(ang_ok, 1)
            dve.wait_ge(sin_ok, 1)
            step(dve.tensor_tensor(cos[:, :, :], cos[:, :, :], cos[:, :, :], ALU.mult))
            settle()
            step(dve.tensor_scalar(cos[:, :, :], cos[:, :, :], -2.0, 1.0, ALU.mult, ALU.add))
            dve.wait_ge(ld_small, 16)
            lv = sm[:, :, M_LAM:M_LAM + 4 * DQK].rearrange("p l (a b c) -> p l a b c", a=2, b=2)
            for L in range(LAYERS):
                step(dve.tensor_tensor(lamp[:, L, :, :], lv[:, L, :, 0, :], lv[:, L, :, 1, :], ALU.mult))
            settle()
            dve.tensor_reduce(lams[:, :, :], lamp[:, :, :, :], AX, ALU.add).then_inc(lam_in, 1)
            dve.wait_ge(lam_exp, 1)
            step(dve.tensor_tensor(lam[:, :], lame[:, :, 1], lame[:, :, 0], ALU.subtract))
            settle()
            step(dve.tensor_tensor(lam[:, :], lam[:, :], kst[:, K_LI:K_LI + LAYERS], ALU.subtract))

            for L in range(LAYERS):
                mean_rstd(L, 0)
                for i in range(0, N_IN, 2):
                    used(dve, L, S_IN + i)
                    n = min(CHUNK, PW - i * CHUNK)
                    dve.tensor_copy(proj[:, :, i * CHUNK:i * CHUNK + n], bank(4 + i % 4, T, CHUNK)[:, :, 0:n]).then_inc(pj_dve, 1)
                dve.wait_ge(pj_act, N_IN // 2 * (L + 1))
                dve.wait_ge(pj_dve, N_IN // 2 * (L + 1))
                step(dve.tensor_tensor(fl[:, 0, :, :], proj[:, :, C_FF:C_FF + FOX_H], mid(sm[:, L, M_FB:M_FB + FOX_H], 1, T), ALU.add))
                settle()
                step(dve.tensor_scalar(fl[:, 1, :, :], fl[:, 0, :, :], 0.0, None, ALU.min))
                step(dve.tensor_scalar(fl[:, 2, :, :], fl[:, 0, :, :], -1.0, None, ALU.mult))
                settle()
                dve.tensor_tensor(fl[:, 2, :, :], fl[:, 2, :, :], fl[:, 0, :, :], ALU.min).then_inc(ff_in, 1)
                dve.wait_ge(psq_ok, T * (L + 1))
                sq = ar(A_SQ, T, C_KC)
                for t in range(T):
                    step(dve.tensor_reduce(gss[:, 0, t, 0:G64], sq[:, t, 0:C_DQ].rearrange("p (g d) -> p g d", d=HD), AX, ALU.add))
                    step(dve.tensor_reduce(gss[:, 0, t, G64:NG], sq[:, t, C_DQ:C_KC].rearrange("p (g d) -> p g d", d=DQK), AX, ALU.add))
                settle()
                dve.tensor_scalar(gss[:, 0, :, 0:G64], gss[:, 0, :, 0:G64], 1.0 / HD, EPS, ALU.mult, ALU.add)
                dve.tensor_scalar(gss[:, 0, :, G64:NG], gss[:, 0, :, G64:NG], 1.0 / DQK, EPS, ALU.mult, ALU.add).then_inc(gms_ok, 1)
                dve.wait_ge(ff_ln, L + 1)
                dve.tensor_tensor(fl[:, 5, :, :], fl[:, 1, :, :], fl[:, 4, :, :], ALU.subtract).then_inc(ff_ls, 1)
                dve.wait_ge(grt_ok, L + 1)
                step(dve.reciprocal(gss[:, 2, :, :], gss[:, 1, :, :]))
                for t in range(T):
                    a = proj[:, t, 0:C_DQ].rearrange("p (g d) -> p g d", d=HD)
                    b = proj[:, t, C_DQ:C_KC].rearrange("p (g d) -> p g d", d=DQK)
                    settle()
                    step(dve.tensor_tensor(a, a, last(gss[:, 2, t, 0:G64], HD), ALU.mult))
                    step(dve.tensor_tensor(b, b, last(gss[:, 2, t, G64:NG], DQK), ALU.mult))
                settle()
                for t in range(T):
                    step(dve.tensor_tensor(proj[:, t, 0:C_KC], proj[:, t, 0:C_KC], sm[:, L, 0:C_KC], ALU.mult))
                settle()
                for t in range(T):
                    for c0, n, d, f in ((C_NQ, ROPE64, HD, 0), (C_DQ, ROPE32, DQK, HD // 2)):
                        hf = d // 2
                        src = proj[:, t, c0:c0 + n * d].rearrange("p (g s d) -> p g s d", s=2, d=hf)
                        dst_ = rope[:, t, c0 - C_NQ:c0 - C_NQ + n * d].rearrange("p (g s d) -> p g s d", s=2, d=hf)
                        cs, sn = cos[:, t, f:f + hf], sin[:, t, f:f + hf]
                        t1 = ar(A_TMP, n, hf)
                        t2 = ar(A_TMP + n * hf, n, hf)
                        settle()
                        step(dve.tensor_tensor(dst_, src, mid(mid(cs, 1, 2), 1, n), ALU.mult))
                        step(dve.tensor_tensor(t1, src[:, :, 1, :], mid(sn, 1, n), ALU.mult))
                        step(dve.tensor_tensor(t2, src[:, :, 0, :], mid(sn, 1, n), ALU.mult))
                        settle()
                        step(dve.tensor_tensor(dst_[:, :, 0, :], dst_[:, :, 0, :], t1, ALU.subtract))
                        step(dve.tensor_tensor(dst_[:, :, 1, :], dst_[:, :, 1, :], t2, ALU.add))
                for t in range(T):
                    for s in range(2):
                        dve.tensor_copy(fa[:, t, s, :, 0:HD], proj[:, t, s * 256:(s + 1) * 256].rearrange("p (g d) -> p g d", d=HD))
                        dve.memset(fa[:, t, s, :, HD + 1 - s:HD + 2 - s], 1.0)
                dve.wait_ge(ff_ps, L + 1)
                cps = bank(0, T, FOX_H)
                root = float(HD ** 0.5)
                for t in range(T):
                    dve.tensor_scalar(fa[:, t, 0, :, HD], cps[:, t, :], root, None, ALU.mult)
                    ins = dve.tensor_scalar(fa[:, t, 1, :, HD + 1], cps[:, t, :], -root, None, ALU.mult)
                step(ins)
                settle()
                dve.memset(X[:, :, :, NCMP:NCP], 0.0).then_inc(tok_ok, 1)
                for n in range(1, 12, 2):
                    dve.wait_ge(tb_ps, 12 * L + n + 1)
                    if n == 1:
                        dve.wait_ge(tb_act, 6 * L + 1)
                        pos = sm[:, L, M_POS:M_POS + 2 * CMP_LEN].rearrange("p (k l) -> p k l", k=2)
                        for kv in range(2):
                            for s in range(2):
                                win = kcvT[:, kv, s * 16:s * 16 + NCMP * 16].rearrange("p (n l) -> p l n", l=16)
                                ins = dve.tensor_tensor(X[:, kv, s * 16:s * 16 + 16, 0:NCMP], win,
                                                        last(pos[:, kv, s * 16:s * 16 + 16], NCMP), ALU.add)
                        ins.then_inc(x_ok, 1)
                    if n in (1, 5):
                        dst_ = (qnT, qrT)[n // 4][:, :, (0 if n == 1 else 1) * P:][:, :, 0:P]
                    elif n in (7, 9):
                        dst_ = fT[0:HD + 2, n // 2 - 3, :, P:SEQ]
                    elif n == 3:
                        dst_ = kswT.rearrange("p k t -> p (k t)")
                    else:
                        dst_ = dkT.rearrange("p k t -> p (k t)")
                    rows = HD + 2 if n in (7, 9) else P
                    src = bank(n % 4, 4, P, parts=rows) if n in (1, 5, 7, 9) else bank(n % 4, 512)
                    dve.tensor_copy(dst_, src).then_inc(tb_dve, 1)
                used(dve, L, S_CMP + 1)
                kcx = ar(A_KCX, 2, HD, parts=NCP)
                kcs = ar(A_KCS, 2, HD, parts=NCP)
                for g in range(2):
                    step(dve.tensor_copy(kcx[:, g, :], bank(4 + g, HD, parts=NCP)))
                    dve.tensor_copy(vcx[0:NCP, g * HD:(g + 1) * HD], bank(4 + g, HD, parts=NCP, at=HD))
                settle()
                step(dve.tensor_tensor(kcs, kcx, kcx, ALU.mult))
                settle()
                step(dve.tensor_reduce(kst4[0:NCP, 0, :], kcs, AX, ALU.add))
                settle()
                dve.tensor_scalar(kst4[0:NCP, 1, :], kst4[0:NCP, 0, :], 1.0 / HD, EPS, ALU.mult, ALU.add).then_inc(kc_ms, 1)
                dve.wait_ge(kc_rt, L + 1)
                step(dve.reciprocal(kst4[0:NCP, 3, :], kst4[0:NCP, 2, :]))
                settle()
                step(dve.tensor_tensor(kcx, kcx, last(kst4[0:NCP, 3, :], HD), ALU.mult))
                settle()
                dve.tensor_tensor(kcx, kcx, sm[0:NCP, L, M_KN:M_KN + 2 * HD].rearrange("p (g d) -> p g d", g=2), ALU.mult).then_inc(kc_tok, 1)
                dve.wait_ge(kc_ps, L + 1)
                vb = vbd.rearrange("p (j g) d -> p j g d", g=2)
                blk = kst[:, K_BLK:K_BLK + NSA_H].rearrange("p (j g) -> p j g", g=2)
                for g in range(2):
                    dve.tensor_tensor(vb[:, :, g, :], mid(bank(5, HD, at=256 + g * HD), 1, 4), last(blk[:, :, g], HD), ALU.mult)
                dve.tensor_copy(kcT[:, :], bank(4, NCP, at=256)).then_inc(kcT_ok, 1)
                dve.wait_ge(cs_ps, L + 1)
                pv = pc[:, :, :, :].rearrange("p t (j g) n -> p t j g n", g=2)
                for g in range(2):
                    for t in range(T):
                        step(dve.tensor_tensor(pv[:, t, :, g, :], bank(4 + g, 4, NCP, at=t * 4 * NCP),
                                               mid(kst[:, K_CM + t * NCP:K_CM + (t + 1) * NCP], 1, 4), ALU.add))
                settle()
                step(dve.tensor_reduce(cst[:, 0, :, :], pc[:, :, :, :], AX, ALU.max))
                settle()
                dve.tensor_tensor(pc[:, :, :, :], pc[:, :, :, :], last(cst[:, 0, :, :], NCP), ALU.subtract).then_inc(cs_ok, 1)
                for s in range(UNITS + 3):
                    u = s
                    if u < UNITS:
                        dve.wait_ge(s_ps, UNITS * L + u + 1)
                        if u >= 4:
                            dve.wait_ge(pt_ps, UNITS * L + u - 3)
                        scale = (DQK if u >= U_DIFF else HD) ** -0.5
                        mask = kst[:, K_MASK:K_MASK + SEQ]
                        Pu = Pb[:, u % 4, :]
                        dve.tensor_tensor_reduce(Pu[:, 0:P], bank(u % 4, P), mask[:, P:SEQ], -scale, 3e38, ALU.add, ALU.min,
                                                 nmax[:, u, 0:1])
                        dve.tensor_tensor_reduce(Pu[:, P:384], bank(u % 4, SEQ, at=P), mask, -scale, 3e38, ALU.add, ALU.min,
                                                 nmax[:, u, 1:2]).then_inc(neg_ok, 1)
                    if u == 1:
                        dve.wait_ge(ce_ok, L + 1)
                        step(dve.tensor_reduce(cst[:, 1, :, :], pc[:, :, :, :], AX, ALU.add))
                    u = s - 2
                    if 0 <= u < UNITS:
                        dve.wait_ge(pt_ps, UNITS * L + u + 1)
                        if u >= 3:
                            dve.wait_ge(pv_ps, UNITS * L + u - 2)
                        dve.tensor_copy(PTb[:, u % 3, :], bank(4 + u % 2, 384)).then_inc(pt_ok, 1)
                settle()
                dve.wait_ge(p_ok, UNITS * (L + 1))
                step(dve.reciprocal(rden[:, :, :], den[:, :, :]))
                step(dve.reciprocal(cst[:, 2, :, :], cst[:, 1, :, :]))
                settle()
                step(dve.tensor_tensor(cst[:, 2, :, :], cst[:, 2, :, :], last(kst[:, K_CV:K_CV + T], NSA_H), ALU.mult))
                dve.wait_ge(gate_ok, L + 1)
                rd = rden[:, :, :].rearrange("p u t -> p t u")
                step(dve.tensor_tensor(cf[:, :, 1, :], gate[:, :, 1, :], rd[:, :, U_SLC:U_WIN], ALU.mult))
                step(dve.tensor_tensor(cf[:, :, 2, :], gate[:, :, 2, :], rd[:, :, U_WIN:U_DIFF], ALU.mult))
                settle()
                step(dve.tensor_tensor(cf[:, :, 0, :], gate[:, :, 0, :], cst[:, 2, :, :], ALU.mult))
                rdo = rden[:, U_DIFF:UNITS, :].rearrange("p (h c) t -> p h c t", c=2)[:, :, 1, :]
                step(dve.tensor_scalar(rdo, rdo, lam[:, L:L + 1], None, ALU.mult))
                dve.wait_ge(o_ok, 7 * (L + 1))
                dve.wait_ge(oc_ok, L + 1)
                settle()
                for t in range(T):
                    settle()
                    fx = mix[:, t, 0:256].rearrange("p (g d) -> p g d", d=HD)
                    step(dve.tensor_tensor(fx, O[:, 0:4, t, :], last(rden[:, 0:4, t], HD), ALU.mult))
                    nm = mix[:, t, 256:768].rearrange("p (g d) -> p g d", d=HD)
                    step(dve.tensor_tensor(nm, Oc[:, t, :, :], last(cf[:, t, 0, :], HD), ALU.mult))
                    tmps = [ar(A_COMB + k * 512, NSA_H, HD) for k in range(2)]
                    for k, u0, tmp in ((1, U_SLC, tmps[0]), (2, U_WIN, tmps[1])):
                        step(dve.tensor_tensor(tmp, O[:, u0:u0 + NSA_H, t, :], last(cf[:, t, k, :], HD), ALU.mult))
                    for tmp in tmps:
                        settle()
                        step(dve.tensor_tensor(nm, nm, tmp, ALU.add))
                    dm = mix[:, t, 768:D].rearrange("p (g d) -> p g d", d=HD)
                    od = O[:, U_DIFF:UNITS, t, :].rearrange("p (h c) d -> p h c d", c=2)
                    rr = rden[:, U_DIFF:UNITS, t].rearrange("p (h c) -> p h c", c=2)
                    tm = ar(A_COMB + 1024, DIFF_H, HD)
                    step(dve.tensor_tensor(dm, od[:, :, 0, :], last(rr[:, :, 0], HD), ALU.mult))
                    step(dve.tensor_tensor(tm, od[:, :, 1, :], last(rr[:, :, 1], HD), ALU.mult))
                    settle()
                    step(dve.tensor_tensor(dm, dm, tm, ALU.add))
                    settle()
                    step(dve.tensor_tensor(tm, dm, dm, ALU.mult))
                    settle()
                    step(dve.tensor_reduce(dst[:, 0, t, :], tm, AX, ALU.add))
                settle()
                dve.tensor_scalar(dst[:, 0, :, :], dst[:, 0, :, :], 1.0 / HD, EPS, ALU.mult, ALU.add).then_inc(dms_ok, 1)
                dve.wait_ge(drt_ok, L + 1)
                step(dve.reciprocal(dst[:, 2, :, :], dst[:, 1, :, :]))
                settle()
                step(dve.tensor_scalar(dst[:, 2, :, :], dst[:, 2, :, :], kst[:, K_LI + LAYERS + L:K_LI + LAYERS + L + 1], None, ALU.mult))
                settle()
                for t in range(T):
                    dm = mix[:, t, 768:D].rearrange("p (g d) -> p g d", d=HD)
                    step(dve.tensor_tensor(dm, dm, last(dst[:, 2, t, :], HD), ALU.mult))
                settle()
                for t in range(T):
                    ins = dve.tensor_tensor(mix[:, t, 768:D], mix[:, t, 768:D], sm[:, L, M_SUB:M_SUB + 256], ALU.mult)
                ins.then_inc(mix_ok, 1)
                for i in range(N_OUT):
                    used(dve, L, S_OUT + i)
                    hc_ = h[:, :, i * CHUNK:(i + 1) * CHUNK]
                    ins = dve.tensor_tensor(hc_, bank(4 + i, T, CHUNK), hc_, ALU.add)
                ins.then_inc(h_ok, 1)

                mean_rstd(L, 1)

                def best16(values, indices, scores):
                    for o in (0, 8):
                        for v, _, s in zip(values, indices, scores):
                            step(dve.max(v[:, o:o + 8], s))
                        settle()
                        for v, i, s in zip(values, indices, scores):
                            step(dve.max_index(i[:, o:o + 8], v[:, o:o + 8], s))
                        settle()
                        if o == 0:
                            for v, s in zip(values, scores):
                                step(dve.match_replace(s, v[:, 0:8], s, -3.0e38))
                            settle()

                for n in range(8):
                    g, t = n // 2, n % 2
                    dve.wait_ge(sc_ok, 8 * L + n + 1)
                    m = range(4 * g, 4 * g + 4)
                    best16([v16[:, t, j, :] for j in m], [i16[:, t, j, :] for j in m], [sc[:, t, j, :] for j in m])
                for t in range(T):
                    c4 = cand[:, t, :, :].rearrange("p h (a b) -> p h a b", a=TOPK)
                    vv = v16[:, t, :, :].rearrange("p (h c) k -> p h c k", c=2)
                    step(dve.tensor_tensor(c4, last(vv[:, :, 0, :], TOPK), mid(vv[:, :, 1, :], 2, TOPK), ALU.add))
                settle()
                for t in range(T):
                    m = range(PH)
                    best16([c16[:, t, j, :] for j in m], [p16[:, t, j, :] for j in m], [cand[:, t, j, :] for j in m])
                step(dve.tensor_copy(gden[:, 0, :, :], c16[:, :, :, 0]))
                step(dve.tensor_scalar(ab16[:, 0, :, :], p16.rearrange("p t h k -> p t (h k)"), 4, None, ALU.logical_shift_right))
                step(dve.tensor_scalar(ab16[:, 1, :, :], p16.rearrange("p t h k -> p t (h k)"), 15, None, ALU.bitwise_and))
                step(dve.tensor_copy(i16f, i16))
                settle()
                dve.tensor_tensor(c16, c16, last(gden[:, 0, :, :], TOPK), ALU.subtract).then_inc(ge_in, 1)
                step(dve.tensor_copy(abf, ab16))
                settle()
                iota = kst[:, K_IOTA:K_IOTA + TOPK]
                for s in range(2):
                    for t in range(T):
                        eq = ar(A_EQ + (t % 2) * 2048, PH * TOPK, TOPK)
                        eqh = ar(A_EQ + (t % 2) * 2048, PH, TOPK, TOPK)
                        ii = i16f[:, t, :, :].rearrange("p (h c) k -> p h c k", c=2)[:, :, s, :]
                        step(dve.tensor_tensor(eq, last(abf[:, s, t, :], TOPK), mid(iota, 1, PH * TOPK), ALU.is_equal))
                        settle()
                        step(dve.tensor_tensor(eqh, eqh, mid(ii, 2, TOPK), ALU.mult))
                        settle()
                        step(dve.tensor_reduce(rout[:, s, t, :], eq, AX, ALU.add))
                dve.wait_ge(ge_ok, L + 1)
                step(dve.tensor_reduce(gden[:, 0, :, :], c16, AX, ALU.add))
                settle()
                step(dve.reciprocal(gden[:, 1, :, :], gden[:, 0, :, :]))
                settle()
                dve.tensor_tensor(rout[:, 2, :, :].rearrange("p t (h k) -> p t h k", k=TOPK), c16,
                                  last(gden[:, 1, :, :], TOPK), ALU.mult).then_inc(rout_ok, 1)
                dve.wait_ge(rout_ps, L + 1)
                step(dve.tensor_copy(routT[:, 0:2, :], bank(4, 2, SEQ)))
                dve.tensor_copy(routT[:, 2, :], bank(5, SEQ)).then_inc(rout_dve, 1)
                settle()

                def onehots(quarter, i, n, par, first=False):
                    m = (L * QUARTERS + quarter) * NB
                    if not first:
                        dve.wait_ge(g_ps, m + 2 * i + n - 1)
                    dve.tensor_tensor(Ah[:, par, :, :], last(routT[:, 0, bass.ds((2 * i + n) * TB, TB)], QI),
                                      mid(kst[:, K_IOTA + quarter * QI:K_IOTA + (quarter + 1) * QI], 1, TB),
                                      ALU.is_equal).then_inc(a1_ok, 1)
                    dve.tensor_tensor(Bh[:, par, :, :], last(routT[:, 1, bass.ds((2 * i + n) * TB, TB)], P),
                                      mid(kst[:, K_IOTA:K_IOTA + P], 1, TB), ALU.is_equal).then_inc(b_ok, 1)

                def weigh(i, p, par, quarter):
                    dve.wait_ge(gelu_ok, L * PAIRS + 2 * i + p + 1)
                    used(dve, L, v_slot(p) - 4 + 4 * i)
                    g = ar((quarter % 2) * SEQ * QI, SEQ, QI)
                    q = p - quarter * QP
                    gv = g[:, :, bass.ds(4 * i + 2 * q, 2)].rearrange("p t e -> p e t")
                    dve.tensor_tensor(W[:, par, :, :], GL[:, par, :].rearrange("p (e t) -> p e t", e=2), gv, ALU.mult).then_inc(w_ok, 1)

                for n in range(NB):
                    onehots(0, 0, n, n % 2, first=(L == 0 and n < 2))
                for quarter in range(QUARTERS):
                    dve.wait_ge(g_ok, (L * QUARTERS + quarter + 1) * NB)
                    with dve.Fori(0, QP // 2) as i:
                        for k in range(2):
                            weigh(i, quarter * QP + k, k, quarter)
                            if quarter < QUARTERS - 1:
                                onehots(quarter + 1, i, k, k)
                dve.wait_ge(acc_ps, L + 1)
                for t in range(T):
                    for half in range(2):
                        hh = h[:, t, half * 512:(half + 1) * 512]
                        ins = dve.tensor_tensor(hh, bank(2 * t + half, 512), hh, ALU.add)
                ins.then_inc(h_ok, 1)
                mean_rstd(L, 2)
                used(dve, L, S_PLEP)
                for i in range(N_PLEG):
                    dve.wait_ge(sg_ok, N_PLEG * L + i + 1)
                    g2 = ar(i * 512, 512)
                    step(dve.tensor_tensor(g2, bank(i, 512), g2, ALU.mult))
                settle()
                for i in range(N_PLEG):
                    hc_ = h[:, :, i * CHUNK:(i + 1) * CHUNK]
                    ins = dve.tensor_tensor(hc_, ar(i * 512, T, CHUNK), hc_, ALU.add)
                ins.then_inc(h_ok, 1)


def _columns():
    widths = (256, 256, 256, 4, 512, 128, 128, 128, 128, 128, 128, 24, 256, 256, 256)
    at = np.concatenate([[0], np.cumsum(widths)])
    fq, fk, fv, ff, nq, kc, vc, ks, vs, kw, vw, ng, dq, dk, dv = (np.arange(at[i], at[i + 1]) for i in range(15))
    nq = nq.reshape(NSA_H, HD)[PAIRED].reshape(-1)
    ng = ng.reshape(NSA_H, 3)[PAIRED].T.reshape(-1)
    return np.concatenate([fq, fk, nq, ks, kw, dq, dk, kc, vc, fv, dv, vs, vw, ff, ng])


def _consts():
    c = np.zeros((P, CONST), np.float32)
    r = np.arange(P)
    c[:, K_ID:K_ID + P] = np.eye(P)
    c[:, K_TRI:K_TRI + P] = r[:, None] <= r[None, :]
    c[:, K_ONE:K_ONE + P] = 1.0
    c[:, K_MASK + P:K_MASK + SEQ] = np.where(r[None, :] <= r[:, None], 0.0, -BIG)
    c[:, K_IOTA:K_IOTA + P] = r[None, :]
    c[:, K_BLK:K_BLK + NSA_H] = (r[:, None] // NCP) == np.arange(NSA_H)[None, :]
    c[0:NCP, K_REP:K_REP + P] = np.arange(NCP)[:, None] == (r[None, :] % NCP)
    for t in range(T):
        end = np.arange(NCP) * CMP_STRIDE + CMP_LEN - 1
        ok = (end[None, :] <= (t * P + r)[:, None]) & (np.arange(NCP) < NCMP)[None, :]
        c[:, K_CM + t * NCP:K_CM + (t + 1) * NCP] = np.where(ok, 0.0, -BIG)
        c[:, K_CV + t] = ok.any(1)
    for at, d in ((K_F64, HD), (K_F32, DQK)):
        half = d // 2
        f = np.float32(THETA) ** (-np.arange(half, dtype=np.float32) / np.float32(half))
        c[:, at:at + half] = f.astype(np.float32)
    for i in range(LAYERS):
        init = 0.8 - 0.6 * np.exp(-0.3 * i)
        c[:, K_LI + i] = init
        c[:, K_LI + LAYERS + i] = 1.0 - init
    return c


def _stream(a):
    s = np.zeros((LAYERS, SLOTS, P, SLOT), np.float32)
    cols = _columns()

    def wide(dst, w):
        for i in range(-(-w.shape[1] // CHUNK)):
            part = w[:, i * CHUNK:(i + 1) * CHUNK]
            n = part.shape[1]
            dst[i, :, 0:DC * n] = part.reshape(DC, P, n).transpose(1, 0, 2).reshape(P, DC * n)

    for L in range(LAYERS):
        wide(s[L, S_IN:S_CMP], a["w_in"][L][:, cols])
        for kv in range(2):
            w = a["nsa_cmp_w"][L, kv].reshape(CMP_LEN, HD, HD).transpose(1, 0, 2).reshape(HD, SLOT)
            s[L, S_CMP + kv, 0:HD] = w
            s[L, S_CMP + kv, HD:P] = w
        wo = a["w_out"][L]
        nsa = wo[256:768].reshape(NSA_H, HD, D)[PAIRED].reshape(512, D)
        wide(s[L, S_OUT:S_Q], np.concatenate([wo[0:256], nsa, wo[768:]]))
        wide(s[L, S_Q:S_KEYS], a["peer_w_q"][L])
        s[L, S_KEYS] = a["peer_sub_keys"][L].reshape(HC, NKEYS, P).transpose(2, 0, 1).reshape(P, SLOT)
        u = a["peer_u"][L].reshape(PAIRS, 2, P, DC, P).transpose(0, 4, 1, 3, 2).reshape(PAIRS, P, SLOT)
        v = a["peer_v"][L].reshape(PAIRS, 2, P, D).transpose(0, 2, 1, 3).reshape(PAIRS, P, SLOT)
        e = s[L, S_EXP:S_PLEP]
        e[0] = u[0]
        e[1:N_EXP - 1:2] = u[1:]
        e[2:N_EXP - 1:2] = v[:-1]
        e[N_EXP - 1] = v[-1]
        s[L, S_PLEP] = a["ple_w_proj"][L].reshape(2, P, D).transpose(1, 0, 2).reshape(P, SLOT)
        wide(s[L, S_PLEG:SLOTS], a["ple_w_gate"][L])
    return s.reshape(LAYERS * SLOTS, P, SLOT)


def _small(a):
    s = np.zeros((LAYERS, P, SMALL), np.float32)
    for L in range(LAYERS):
        rows = [np.tile(a["fox_q_norm_w"][L], FOX_H), np.tile(a["fox_k_norm_w"][L], FOX_H),
                np.tile(a["nsa_q_norm_w"][L], NSA_H), np.tile(a["nsa_k_norm_w"][L], 4),
                np.tile(a["diff_q_norm_w"][L], 2 * DIFF_H), np.tile(a["diff_k_norm_w"][L], 2 * DIFF_H),
                a["fox_f_bias"][L], np.tile(a["nsa_k_norm_w"][L], 2), np.tile(a["diff_subln_w"][L], DIFF_H),
                a["diff_lambda"][L].reshape(-1)]
        s[L, :, 0:M_COL] = np.concatenate(rows)[None, :]
        for j, name in enumerate(("attn_norm_w", "ffn_norm_w", "ple_norm_w")):
            s[L, :, M_COL + j * DC:M_COL + (j + 1) * DC] = a[name][L].reshape(DC, P).T
        pos = a["nsa_cmp_pos"][L].transpose(2, 0, 1).reshape(HD, 2 * CMP_LEN)
        s[L, 0:HD, M_POS:M_PT] = pos
        s[L, HD:P, M_POS:M_PT] = pos
        s[L, :, M_PT:SMALL] = a["p"][L, 0].T.reshape(2, P, SEQ).transpose(1, 0, 2).reshape(P, 2 * SEQ)
    return s


def kernel(**inputs):
    import numpy as _np
    import concourse.bacc as _bacc
    from concourse import mybir as _mybir
    from concourse.bass_utils import run_bass_kernel_spmd as _run

    a = {k: _np.asarray(v) for k, v in inputs.items()}
    arrays = {
        "x": _np.ascontiguousarray(a["x"]),
        "positions": _np.ascontiguousarray(a["positions"]),
        "small": _small(a),
        "consts": _consts(),
        "stream": _stream(a),
    }
    nc = _bacc.Bacc("TRN2", target_bir_lowering=False, num_devices=1)
    args = [nc.dram_tensor(k, v.shape, _mybir.dt.from_np(v.dtype), kind="ExternalInput").ap() for k, v in arrays.items()]
    out = nc.dram_tensor("out", (1, SEQ, D), _mybir.dt.float32, kind="ExternalOutput").ap()
    trunk(nc, *args, out)
    r = _run(nc, [arrays], core_ids=[0])
    return r.results[0]["out"]
```

```python
from contextlib import ExitStack

import numpy as np

import concourse.bass as bass
from concourse import mybir

F32 = mybir.dt.float32
F32R = mybir.dt.float32r
BF16 = mybir.dt.bfloat16
I32 = mybir.dt.int32
U32 = mybir.dt.uint32
ALU = mybir.AluOpType
ACT = mybir.ActivationFunctionType
AX = mybir.AxisListType.X

P = 128
D = 1024
SEQ = 256
T = SEQ // P
DC = D // P
LAYERS = 2
PLE = 256
EPS = 1e-6
THETA = 10000.0
FOX_H, NSA_H, DIFF_H = 4, 8, 4
HD, DQK = 64, 32
CMP_LEN, CMP_STRIDE = 32, 16
NCMP = (SEQ - CMP_LEN) // CMP_STRIDE + 1
NCP = 16
NKEYS, TOPK, PH = 128, 16, 8
HC = PH * 2
BIG = 1.0e30

C_FQ, C_FK, C_NQ, C_KS, C_KW, C_DQ, C_DK = 0, 256, 512, 1024, 1152, 1280, 1536
C_KC, C_VC, C_FV, C_DV, C_VS, C_VW, C_FF, C_NG = 1792, 1920, 2048, 2304, 2560, 2688, 2816, 2820
PW = 2844
G64, G32 = C_DQ // HD, (C_KC - C_DQ) // DQK
NG = G64 + G32
ROPE64 = (C_DQ - C_NQ) // HD
ROPE32 = G32
PAIRED = [0, 4, 1, 5, 2, 6, 3, 7]

SLOT = 2048
RING = 4
CHUNK = 256
N_IN = -(-PW // CHUNK)
N_CMP, N_OUT, N_Q, N_EXP, N_PLEP, N_PLEG = 2, D // CHUNK, HC * P // CHUNK, 128, 1, D // CHUNK
S_IN = 0
S_CMP = S_IN + N_IN
S_OUT = S_CMP + N_CMP
S_Q = S_OUT + N_OUT
S_EXP = S_Q + N_Q
S_PLEP = S_EXP + N_EXP
S_PLEG = S_PLEP + N_PLEP
SLOTS = S_PLEG + N_PLEG

PAIRS = NKEYS // 2
QUARTERS = 4
QI = NKEYS // QUARTERS
QP = PAIRS // QUARTERS
TB = 16
NB = SEQ // TB
LEAD = QP + 1
assert NB == QP

M_NORM = 0
M_FB = M_NORM + C_KC
M_KN = M_FB + FOX_H
M_SUB = M_KN + 2 * HD
ROWS = M_SUB + DIFF_H * 2 * DQK
M_COL = 0
M_POS = M_COL + 3 * DC
M_PT = M_POS + 2 * CMP_LEN
M_LAM = M_PT + 2 * SEQ
COLS = M_LAM + 4 * DQK

K_ID = 0
K_TRI = K_ID + P
K_ONE = K_TRI + P
K_MASK = K_ONE + P
K_IOTA = K_MASK + SEQ
K_BLK = K_IOTA + P
K_REP = K_BLK + NSA_H
K_CM = K_REP + P
K_CV = K_CM + T * NCP
K_F64 = K_CV + T
K_F32 = K_F64 + HD // 2
K_LI = K_F32 + DQK // 2
CONST = K_LI + 2 * LAYERS
NANG = HD // 2 + DQK // 2

A_PROJ = 0
A_SQ = 5696
A_O = A_SQ
A_ROPE = A_SQ + T * C_KC
A_OC = A_O + 28 * T * HD
A_TMP = 11840
A_VBD, A_KCX, A_KCS = A_TMP, A_TMP + 512, A_TMP + 640
A_FA = 12608
A_FT = 13664
A_PC, A_PCT, A_VCX, A_KCT = (A_FA + x for x in (0, T * P, 2 * T * P, 2 * T * P + 2 * HD))
A_SM = A_KCT + NCP
A_ANG = A_FT
A_QNT, A_QRT, A_KSW, A_KCV, A_DQ, A_DK = (A_FT + x for x in (2048, 3072, 4096, 4608, 5120, 5632))
A_X = A_FT + 6144
A_P = A_X + 1024
A_PT = A_P + 4 * 384
A_MIX = 0
A_MIXT = 2048
A_COMB = 11328
A_XN, A_XSQ = 20480, 22528
A_XF = 0
A_PQ, A_SC, A_CAND, A_EQ = 0, 4096, 0, 4096
A_LEAD = SEQ * QI
A_KEYS = A_LEAD + (QP - 4) * 512
A_B = 2 * SEQ * QI
A_E = A_B + TB * P
A_A = A_E + TB * QI
A_GL = A_A + 3 * TB * QI
A_W = A_GL + 2 * 512
ARENA = 23552
A_RT = A_B
assert A_W + 512 <= ARENA
assert A_PT + 3 * 384 <= ARENA and A_XSQ + 1024 <= ARENA

U_FOX, U_SLC, U_WIN, U_DIFF, UNITS = 0, 4, 12, 20, 28
TWO_PI = 2 * np.pi
PI_C = [6.28125, 0.00193500518798828125, 3.01991438e-07]
MAGIC = float(1.5 * 2 ** 23)


def u_slot(p):
    return S_EXP + (p if p < LEAD else 2 * p - 1)


def v_slot(p):
    return S_EXP + (LEAD + p if p < QP else 2 * p + 2 if p < PAIRS - 1 else 2 * p + 1)


WHOLE = (S_CMP, S_CMP + 1, S_PLEP)
SPLIT = [n for n in range(SLOTS) if n not in WHOLE]
ORDER = {n: m for m, n in enumerate(SPLIT)}
assert len(SPLIT) % 2 == 0
V_ALL = [v_slot(p) for p in range(PAIRS)]
REST = [n for n in SPLIT if n not in V_ALL]
WIDTH = {n: DC * min(CHUNK, PW - (n - S_IN) * CHUNK) if n < S_CMP else SLOT for n in SPLIT}
V_STEP = {v_slot(p): 4 if p < QP else 2 for p in range(PAIRS)}
U_STEP = {n: 2 if n > u_slot(LEAD - 1) else 4 for n in REST}


def trunk(nc, x, positions, rows, cols, consts, keys, stream, out):
    ctx = ExitStack()
    with ctx:
        def sb(name, shape, dt=F32):
            return ctx.enter_context(nc.sbuf_tensor(name, shape, dt))

        def sem(name):
            return ctx.enter_context(nc.semaphore(name))

        h = sb("h", [P, T, D])
        xh = sb("xh", [P, DC, SEQ], F32R)
        xl = sb("xl", [P, DC, SEQ], F32R)
        wh = sb("wh", [P, 2, SLOT], F32R)
        wl = sb("wl", [P, 2, SLOT], F32R)
        Wh = sb("Wh", [P, 2, SEQ], F32R)
        Wl = sb("Wl", [P, 2, SEQ], F32R)
        ring = sb("ring", [P, RING, SLOT])
        arena = sb("arena", [P, ARENA])
        kst = sb("kst", [P, CONST])
        smr = sb("smr", [P, ROWS])
        sm = sb("sm", [P, LAYERS, COLS])
        routT = sb("routT", [P, 3, SEQ])
        g3 = sb("g3", [P, 3, SEQ], BF16)
        posi = sb("posi", [P, T], I32)
        posf = sb("posf", [P, T])
        sin = sb("sin", [P, T, NANG])
        cos = sb("cos", [P, T, NANG])
        lams = sb("lams", [P, LAYERS, 2])
        lame = sb("lame", [P, LAYERS, 2])
        lam = sb("lam", [P, LAYERS])
        ss = sb("ss", [P, T])
        rstd = sb("rstd", [P, 3, T])
        gate = sb("gate", [P, T, 3, NSA_H])

        psum = ctx.enter_context(nc.psum_tensor("psum", [P, 8, 512], F32))

        def ar(off, *dims, parts=P):
            n = int(np.prod(dims))
            v = arena[0:parts, off:off + n]
            if len(dims) == 1:
                return v
            names = "abcd"[:len(dims)]
            return v.rearrange(f"p ({' '.join(names)}) -> p {' '.join(names)}", **dict(zip(names[1:], dims[1:])))

        def bank(b, *dims, parts=P, at=0):
            n = int(np.prod(dims))
            v = psum[0:parts, b, at:at + n]
            if len(dims) == 1:
                return v
            names = "abcd"[:len(dims)]
            return v.rearrange(f"p ({' '.join(names)}) -> p {' '.join(names)}", **dict(zip(names[1:], dims[1:])))

        def last(v, n):
            return v.unsqueeze(len(v.shape)).to_broadcast(list(v.shape) + [n])

        def mid(v, at, n):
            s = list(v.shape)
            return v.unsqueeze(at).to_broadcast(s[:at] + [n] + s[at:])

        ident = kst[:, K_ID:K_ID + P]
        zeros = kst[:, K_MASK:K_MASK + P // 2].bitcast(BF16)
        finite = kst[:, K_ID:K_ID + SEQ].bitcast(BF16)
        ang, angk = ar(A_ANG, T, NANG), ar(A_ANG + T * NANG, T, NANG)
        lamp = ar(A_ANG + 2 * T * NANG, LAYERS, 2, DQK)
        pc, pcT, vcx, kcT = ar(A_PC, T, NSA_H, NCP), ar(A_PCT, T, P), ar(A_VCX, 2 * HD), ar(A_KCT, NCP)
        gss, fl = ar(A_PT, 3, T, NG), ar(A_PT + 3 * T * NG, 6, T, FOX_H)
        nmax, den, rden = (ar(A_SM + k * T * UNITS, UNITS, T) for k in range(3))
        cst, cf = (ar(A_SM + 3 * T * UNITS + k * 3 * T * NSA_H, *d) for k, d in enumerate(((3, T, NSA_H), (T, 3, NSA_H))))
        dst, kst4 = ar(A_SM + 3 * T * (UNITS + 2 * NSA_H), 3, T, DIFF_H), ar(A_SM + 3 * T * (UNITS + 2 * NSA_H + DIFF_H), 4, 2)
        proj = ar(A_PROJ, T, PW)
        rope = ar(A_ROPE, T, C_KC - C_NQ)
        fa = ar(A_FA, T, 2, FOX_H, HD + 2)
        fT = ar(A_FT, 2, FOX_H, SEQ)
        qnT = ar(A_QNT, 4, SEQ)
        qrT = ar(A_QRT, 4, SEQ)
        kswT = ar(A_KSW, 2, SEQ)
        kcvT = ar(A_KCV, 2, SEQ)
        dqT = ar(A_DQ, 2, SEQ)
        dkT = ar(A_DK, 2, SEQ)
        X = ar(A_X, 2, CMP_LEN, NCP)
        vbd = ar(A_VBD, NSA_H, HD)
        O = ar(A_O, UNITS, T, HD)
        Oc = ar(A_OC, T, NSA_H, HD)
        mix = ar(A_MIX, T, D)
        Pb = ar(A_P, 4, 384)
        PTb = ar(A_PT, 3, 384)
        xn = ar(A_XN, T, D)
        pqT = ar(A_PQ, HC, SEQ)
        sc = ar(A_SC, T, HC, NKEYS)
        cand = ar(A_CAND, T, PH, TOPK * TOPK)
        Bh = ar(A_B, TB * P).bitcast(BF16).rearrange("p (a b c) -> p a b c", a=2, b=TB)
        Eh = ar(A_E, TB * QI).bitcast(BF16).rearrange("p (a b c) -> p a b c", a=2, b=TB)
        Ah = ar(A_A, 3 * TB * QI).bitcast(BF16).rearrange("p (a k b c) -> p a k b c", a=2, k=3, b=TB)
        GL = ar(A_GL, 2, 512)
        W = ar(A_W, 2, SEQ)
        xf = ar(A_XF, DC, SEQ)
        v16 = ar(A_RT, T, HC, TOPK)
        i16 = ar(A_RT + 512, T, HC, TOPK).bitcast(U32)
        i16f = ar(A_RT + 1024, T, HC, TOPK)
        c16 = ar(A_RT + 1536, T, PH, TOPK)
        p16 = ar(A_RT + 1792, T, PH, TOPK).bitcast(U32)
        ab16 = ar(A_RT + 2048, 2, T, PH * TOPK).bitcast(U32)
        abf = ar(A_RT + 2560, 2, T, PH * TOPK)
        rout = ar(A_RT + 3072, 3, T, PH * TOPK)
        gden = ar(A_RT + 3840, 2, T, PH)

        ld_x, ld_rows, ld_cols, ld_const, ld_pos = (sem(n) for n in ("ld_x", "ld_rows", "ld_cols", "ld_const", "ld_pos"))
        hi_ok, lo_ok, vlo_ok, vlo2_ok, xf_ok, xh_ok, rows_free = (sem(n) for n in ("hi_ok", "lo_ok", "vlo_ok", "vlo2_ok", "xf_ok", "xh_ok", "rows_free"))
        w1_ok, w2_ok = sem("w1_ok"), sem("w2_ok")
        slot_ld = [sem(f"slot_ld{i}") for i in range(RING)]
        slot_used = sem("slot_used")
        ang_ok, sin_ok, lam_in, lam_exp = sem("ang_ok"), sem("sin_ok"), sem("lam_in"), sem("lam_exp")
        h_ok = sem("h_ok")
        ss_ok, ms_ok, rt_ok, xn_ok, xt_ps, xt_ok = (sem(n) for n in ("ss_ok", "ms_ok", "rt_ok", "xn_ok", "xt_ps", "xt_ok"))
        pj_dve, pj_act = sem("pj_dve"), sem("pj_act")
        psq_ok, gms_ok, grt_ok = sem("psq_ok"), sem("gms_ok"), sem("grt_ok")
        ff_in, ff_ln, ff_ls, ff_ps = sem("ff_in"), sem("ff_ln"), sem("ff_ls"), sem("ff_ps")
        tok_ok, tb_ps, tb_dve, tb_act = sem("tok_ok"), sem("tb_ps"), sem("tb_dve"), sem("tb_act")
        x_ok, kc_ms, kc_rt, kc_tok, kc_ps, kcT_ok = (sem(n) for n in ("x_ok", "kc_ms", "kc_rt", "kc_tok", "kc_ps", "kcT_ok"))
        cs_ps, cs_ok, ce_ok, pcT_ps, pcT_ok, oc_ps, oc_ok = (sem(n) for n in ("cs_ps", "cs_ok", "ce_ok", "pcT_ps", "pcT_ok", "oc_ps", "oc_ok"))
        s_ps, neg_ok, p_ok, pt_ps, pt_ok, pv_ps, o_ok = (sem(n) for n in ("s_ps", "neg_ok", "p_ok", "pt_ps", "pt_ok", "pv_ps", "o_ok"))
        gate_ok, dms_ok, drt_ok, mix_ok = (sem(n) for n in ("gate_ok", "dms_ok", "drt_ok", "mix_ok"))
        ld_keys = sem("ld_keys")
        q_ok, sc_ps, sc_ok = sem("q_ok"), sem("sc_ps"), sem("sc_ok")
        ge_in, ge_ok, rout_ok, rout_ps, rout_dve = (sem(n) for n in ("ge_in", "ge_ok", "rout_ok", "rout_ps", "rout_dve"))
        b_ok, a1_ok, a_ok, g_ps, g_ok = (sem(n) for n in ("b_ok", "a1_ok", "a_ok", "g_ps", "g_ok"))
        gelu_ok, w_ok, acc_ps = sem("gelu_ok"), sem("w_ok"), sem("acc_ps")
        sg_ok = sem("sg_ok")
        dve_step, act_step = sem("dve_step"), sem("act_step")
        out_st = sem("out_st")

        def split_ready(eng, L, n, i=0):
            m = ORDER[n]
            k = L * SLOTS + n
            eng.wait_ge(slot_ld[k % RING], 16 * (i + k // RING + 1))
            if m >= 2 or L:
                eng.wait_ge(slot_used, (L * SLOTS + SPLIT[m - 2] if m >= 2 else (L - 1) * SLOTS + SPLIT[m - 2]) + 4 * i + 1)

        def half_of(n, j):
            return slice(j * WIDTH[n] // 2, (j + 1) * WIDTH[n] // 2)

        def high(L, n, i=0):
            split_ready(nc.scalar, L, n, i)
            for j in range(2):
                c = half_of(n, j)
                nc.scalar.activation(wh[:, ORDER[n] % 2, c], ring[:, (L * SLOTS + n) % RING, c], ACT.Copy).then_inc(hi_ok, 1)

        def low_half(eng, L, n, i, j, done):
            m, c = ORDER[n], half_of(n, j)
            split_ready(eng, L, n, i)
            eng.wait_ge(hi_ok, 2 * (L * len(SPLIT) + m + 4 * i) + j + 1)
            eng.tensor_tensor(wl[:, m % 2, c], ring[:, (L * SLOTS + n) % RING, c], wh[:, m % 2, c].bitcast(F32),
                              ALU.subtract).then_inc(done, 1)

        def used(eng, L, n):
            eng.wait_ge(slot_used, L * SLOTS + n + 1)

        block = ctx.enter_context(nc.Block())

        @block.sync
        def _(sp):
            sp.dma_start(h[:, :, :], x.rearrange("o (t p) d -> p (o t) d", p=P)).then_inc(ld_x, 16)
            for s in range(RING):
                sp.dma_start(ring[:, s, :], stream[s]).then_inc(slot_ld[s], 16)
                if s == 0:
                    sp.dma_start(kst[:, :], consts).then_inc(ld_const, 16)
                    sp.dma_start(sm[:, :, :], cols.rearrange("l p n -> p l n")).then_inc(ld_cols, 16)
                    sp.dma_start(smr[:, :], rows[0]).then_inc(ld_rows, 16)
                    sp.dma_start(posi[:, :], positions.rearrange("o (t p) -> p (o t)", p=P),
                                 allow_slow_non_contiguous=True).then_inc(ld_pos, 16)
            with sp.Fori(1, LAYERS * SLOTS // RING) as i:
                for s in range(RING):
                    sp.wait_ge(slot_used, RING * i + (s - RING + 1))
                    sp.dma_start(ring[:, s, :], stream[RING * i + s]).then_inc(slot_ld[s], 16)
            for k in range(LAYERS * SLOTS // RING * RING, LAYERS * SLOTS):
                sp.wait_ge(slot_used, k - RING + 1)
                sp.dma_start(ring[:, k % RING, :], stream[k]).then_inc(slot_ld[k % RING], 16)

        @block.tensor
        def _(pe):
            def parts(L, n):
                return wh[:, ORDER[n] % 2, :], wl[:, ORDER[n] % 2, :]

            def half(L, n, j, i=0):
                if n in V_ALL[0:QP]:
                    pe.wait_ge((vlo_ok, vlo2_ok)[j], L * (2 * PAIRS - QP, QP)[j] + V_ALL.index(n) + 4 * i + 1)
                elif n in V_ALL:
                    pe.wait_ge(vlo_ok, L * (2 * PAIRS - QP) + 2 * (V_ALL.index(n) + V_STEP[n] * i) - QP + j + 1)
                else:
                    pe.wait_ge(lo_ok, 2 * (L * len(REST) + REST.index(n) + U_STEP[n] * i) + j + 1)

            def product(o, a, b, start, stop, **kw):
                pe.matmul(o, a[0], b[0], start=start, stop=False, **kw)
                pe.matmul(o, a[0], b[1], start=False, stop=False, **kw)
                return pe.matmul(o, a[1], b[0], start=False, stop=stop, **kw)

            def slot(L, n):
                n += L * SLOTS
                pe.wait_ge(slot_ld[n % RING], 16 * (n // RING + 1))
                return ring[:, n % RING, :]

            def transposes(L, j):
                n = 3 * L + j
                pe.wait_ge(xn_ok, n + 1)
                for b in range(DC // 2):
                    for c in range(2):
                        for t in range(T):
                            k = 2 * b + c
                            ins = pe.transpose(bank(b, P, at=c * SEQ + t * P), xn[:, t, k * P:(k + 1) * P], ident)
                    ins.then_inc(xt_ps, 1)

            def token_major(b, L, s, n=CHUNK):
                w = parts(L, s)
                wv = [a[:, 0:DC * n].rearrange("p (k n) -> p k n", k=DC) for a in w]
                for t in range(T):
                    for k in range(DC):
                        if t == 0 and k % (DC // 2) == 0:
                            half(L, s, 2 * k // DC)
                        ins = product(bank(b, n, at=t * CHUNK), [a[:, k, t * P:(t + 1) * P] for a in (xh, xl)],
                                      [a[:, k, :] for a in wv], k == 0, k == DC - 1)
                return ins

            def rows_of(u):
                if u < U_SLC:
                    v = C_FV + u * HD
                    return fT[0:HD + 2, 0, u, :], fT[0:HD + 2, 1, u, :], v
                if u < U_DIFF:
                    kind, j = (u - U_SLC) // NSA_H, (u - U_SLC) % NSA_H
                    r = slice(HD * (j % 2), HD * (j % 2) + HD)
                    return qrT[r, j // 2, :], kswT[r, kind, :], (C_VS, C_VW)[kind] + (j % 2) * HD
                c = u - U_DIFF
                r = slice(DQK * (c % 4), DQK * (c % 4) + DQK)
                return dqT[r, c // 4, :], dkT[r, c // 4, :], C_DV + (c // 2) * HD

            pe.wait_ge(ld_const, 16)
            pe.wait_ge(ld_cols, 16)
            for L in range(LAYERS):
                transposes(L, 0)
                pe.wait_ge(xt_ok, 4 * (4 * L) + 4)
                for i in range(N_IN):
                    if i >= 4:
                        pe.wait_ge((pj_dve, pj_act)[i % 2], L * N_IN // 2 + (i - 4) // 2 + 1)
                    ins = token_major(4 + i % 4, L, S_IN + i, min(CHUNK, PW - i * CHUNK))
                    ins.then_inc(slot_used, 1)
                pe.wait_ge(ff_ls, L + 1)
                tri, one = kst[:, K_TRI:K_TRI + P], kst[:, K_ONE:K_ONE + P]
                pe.matmul(bank(0, FOX_H), tri, fl[:, 5, 0, :], start=True, stop=True)
                pe.matmul(bank(0, FOX_H, at=FOX_H), one, fl[:, 5, 0, :], start=True, stop=False)
                pe.matmul(bank(0, FOX_H, at=FOX_H), tri, fl[:, 5, 1, :], start=False, stop=True).then_inc(ff_ps, 1)
                pe.wait_ge(tok_ok, L + 1)
                NQ0 = [C_NQ + i * P for i in range(4)]
                batches = [[proj[:, t, c:c + P] for c in (C_KC, C_VC) for t in range(T)]]
                batches += [[proj[:, t, c:c + P] for c in NQ0] for t in range(T)]
                batches += [[rope[:, t, c - C_NQ:c - C_NQ + P] for c in (C_KS, C_KW) for t in range(T)]]
                batches += [[rope[:, t, c - C_NQ:c - C_NQ + P] for c in NQ0] for t in range(T)]
                batches += [[fa[:, t, s, i, :] for i in range(FOX_H)] for s in range(2) for t in range(T)]
                batches += [[rope[:, t, c - C_NQ + b * P:c - C_NQ + (b + 1) * P] for b in range(2) for t in range(T)]
                            for c in (C_DQ, C_DK)]
                for n, batch in enumerate(batches):
                    if n >= 4:
                        pe.wait_ge((tb_act, tb_dve)[n % 2], 6 * L + (n - 4) // 2 + 1)
                    for i, src in enumerate(batch):
                        rows = src.shape[1]
                        ins = pe.transpose(bank(n % 4, P, parts=rows, at=i * P), src, ident)
                    ins.then_inc(tb_ps, 1)
                pe.wait_ge(x_ok, L + 1)
                for kv in range(2):
                    w = slot(L, S_CMP + kv)
                    for g in range(2):
                        r = slice(HD * g, HD * g + HD)
                        for l in range(CMP_LEN):
                            ins = pe.matmul(bank(4 + g, HD, parts=NCP, at=kv * HD), X[r, kv, l, :],
                                            w[r, l * HD:(l + 1) * HD], start=(l == 0), stop=(l == CMP_LEN - 1))
                    ins.then_inc(slot_used, 1)
                pe.wait_ge(kc_tok, L + 1)
                pe.transpose(bank(4, NCP, at=256), ar(A_KCX, 2 * HD, parts=NCP), ident[0:NCP, 0:NCP])
                pe.matmul(bank(5, 2 * HD, at=256), kst[0:NCP, K_REP:K_REP + P], vcx[0:NCP, :], start=True, stop=True).then_inc(kc_ps, 1)
                pe.wait_ge(kcT_ok, L + 1)
                pe.wait_ge(tb_act, 6 * L + 6)
                pe.wait_ge(tb_dve, 6 * L + 6)
                for g in range(2):
                    r = slice(HD * g, HD * g + HD)
                    for t in range(T):
                        for j in range(4):
                            ins = pe.matmul(bank(4 + g, NCP, at=(4 * t + j) * NCP), qnT[r, j, t * P:(t + 1) * P],
                                            kcT[r, :], start=True, stop=True)
                ins.then_inc(cs_ps, 1)
                for s in range(UNITS + 3):
                    if s < UNITS:
                        q, k, _ = rows_of(s)
                        if s >= 4:
                            pe.wait_ge(neg_ok, UNITS * L + s - 3)
                        pe.matmul(bank(s % 4, P), q[:, 0:P], k[:, 0:P], start=True, stop=True)
                        pe.matmul(bank(s % 4, SEQ, at=P), q[:, P:SEQ], k, start=True, stop=True).then_inc(s_ps, 1)
                    if s == 1:
                        pe.wait_ge(ce_ok, L + 1)
                        for t in range(T):
                            ins = pe.transpose(bank(4, P, at=t * P), pc[:, t, :, :].rearrange("p j n -> p (j n)"), ident)
                        ins.then_inc(pcT_ps, 1)
                        pe.wait_ge(pcT_ok, L + 1)
                        for t in range(T):
                            ins = pe.matmul(bank(6 + t, 512), pcT[:, t, :], vbd.rearrange("p j d -> p (j d)"),
                                            start=True, stop=True)
                        ins.then_inc(oc_ps, 1)
                    u = s - 2
                    if 0 <= u < UNITS:
                        pe.wait_ge(p_ok, UNITS * L + u + 1)
                        if u >= 2:
                            pe.wait_ge(pt_ok, UNITS * L + u - 1)
                        for i in range(3):
                            ins = pe.transpose(bank(4 + u % 2, P, at=i * P), Pb[:, u % 4, i * P:(i + 1) * P], ident)
                        ins.then_inc(pt_ps, 1)
                    u = s - 3
                    if 0 <= u < UNITS:
                        _, _, v = rows_of(u)
                        if u == 0:
                            pe.wait_ge(oc_ok, L + 1)
                        if u % 4 == 0 and u >= 8:
                            pe.wait_ge(o_ok, 7 * L + u // 4 - 1)
                        pe.wait_ge(pt_ok, UNITS * L + u + 1)
                        o = [bank(6 + u // 4 % 2, HD, at=(u % 4) * P + t * HD) for t in range(T)]
                        PT = PTb[:, u % 3, :]
                        pe.matmul(o[0], PT[:, 0:P], proj[:, 0, v:v + HD], start=True, stop=True)
                        pe.matmul(o[1], PT[:, P:2 * P], proj[:, 0, v:v + HD], start=True, stop=False)
                        pe.matmul(o[1], PT[:, 2 * P:3 * P], proj[:, 1, v:v + HD], start=False, stop=True).then_inc(pv_ps, 1)
                pe.wait_ge(mix_ok, L + 1)
                for b in range(4):
                    for c in range(2):
                        for t in range(T):
                            k = 2 * b + c
                            ins = pe.transpose(bank(b, P, at=c * SEQ + t * P), mix[:, t, k * P:(k + 1) * P], ident)
                    ins.then_inc(xt_ps, 1)
                pe.wait_ge(xt_ok, 4 * (4 * L + 1) + 4)
                for i in range(N_OUT):
                    ins = token_major(4 + i, L, S_OUT + i)
                    ins.then_inc(slot_used, 1)
                transposes(L, 1)
                pe.wait_ge(xt_ok, 4 * (4 * L + 2) + 4)
                def scores(g):
                    pe.wait_ge(q_ok, N_Q * L + 2 * g + 2)
                    for t in range(T):
                        n = 2 * g + t
                        if n >= 4:
                            pe.wait_ge(sc_ok, 8 * L + n - 3)
                        for j in range(4):
                            m = 4 * g + j
                            ins = pe.matmul(bank(4 + n % 4, P, at=j * P), pqT[:, m, t * P:(t + 1) * P], subkeys[:, m, :],
                                            start=True, stop=True)
                        ins.then_inc(sc_ps, 1)

                subkeys = ar(A_KEYS, HC, NKEYS)
                pe.wait_ge(ld_keys, 16 * (L + 1))
                for i in range(N_Q):
                    w = [a.rearrange("p (k n) -> p k n", k=DC) for a in parts(L, S_Q + i)]
                    if i >= 4:
                        pe.wait_ge(q_ok, N_Q * L + i - 3)
                    for c in range(2):
                        for k in range(DC):
                            if c == 0 and k % (DC // 2) == 0:
                                half(L, S_Q + i, 2 * k // DC)
                            ins = product(bank(i % 4, SEQ, at=c * SEQ), [a[:, k, c * P:(c + 1) * P] for a in w],
                                          [xh[:, k, :], xl[:, k, :]], k == 0, k == DC - 1)
                    ins.then_inc(slot_used, 1)
                    if i >= 2 and i % 2 == 0:
                        scores(i // 2 - 1)
                def spread(n, par, first=False):
                    pe.wait_ge(b_ok, n + 1)
                    pe.wait_ge(a_ok, n + 1)
                    if not first:
                        pe.wait_ge(g_ok, n - 1)
                    for i in range(TB):
                        for k in range(3):
                            ins = pe.matmul(bank(6 + par, QI, at=i * QI), Bh[:, par, i, :], Ah[:, par, k, i, :],
                                            start=(k == 0), stop=(k == 2))
                    ins.then_inc(g_ps, 1)

                def hidden(i, p, step=2):
                    w = [a.rearrange("p (e k n) -> p e k n", e=2, k=DC) for a in parts(L, u_slot(p))]
                    if p + L > 1 or not isinstance(i, int):
                        pe.wait_ge(gelu_ok, L * PAIRS + step * i + p - 1)
                    for e in range(2):
                        half(L, u_slot(p), e, i)
                        for k in range(DC):
                            ins = product(bank(4 + p % 2, SEQ, at=e * SEQ), [a[:, e, k, :] for a in w],
                                          [xh[:, k, :], xl[:, k, :]], k == 0, k == DC - 1)
                    ins.then_inc(slot_used, 1)

                def weighted(i, p, step=2):
                    w = [a.rearrange("p (e n) -> p e n", e=2) for a in parts(L, v_slot(p))]
                    pe.wait_ge(w_ok, L * PAIRS + step * i + p + 1)
                    for e in range(2):
                        half(L, v_slot(p), e, i)
                        for t in range(T):
                            for c in range(2):
                                ins = product(bank(2 * t + c, 512), [a[:, e, t * P:(t + 1) * P] for a in (Wh, Wl)],
                                              [a[:, e, c * 512:(c + 1) * 512] for a in w], False, False,
                                              skip_group_check=True)
                    ins.then_inc(slot_used, 1)

                q0 = L * NB * QUARTERS
                pe.wait_ge(sc_ok, 8 * L + 6)
                hidden(0, 0, 4)
                scores(3)
                for k in range(1, 4):
                    hidden(0, k, 4)
                with pe.Fori(1, QP // 4 - 1) as i:
                    for k in range(4):
                        hidden(i, k, 4)
                for p in range(QP - 4, QP - 1):
                    hidden(0, p)
                for b in range(4):
                    pe.matmul(bank(b, 512), zeros, finite, start=True, stop=False, skip_group_check=True)
                pe.wait_ge(rout_ok, L + 1)
                pe.wait_ge(sc_ok, 8 * L + 8)
                for k in range(3):
                    for t in range(T):
                        ins = pe.transpose(bank(6 + k // 2, P, at=(k % 2) * SEQ + t * P), rout[:, k, t, :], ident)
                ins.then_inc(rout_ps, 1)
                hidden(0, QP - 1)
                pe.wait_ge(rout_dve, L + 1)
                for n in range(NB):
                    spread(q0 + n, n % 2, first=(n < 2))
                    if n == 1:
                        hidden(0, QP)
                with pe.Fori(0, QP // 4) as i:
                    for k in range(4):
                        weighted(i, k, 4)
                        spread(q0 + NB + 4 * i + k, k % 2)
                for quarter in range(1, QUARTERS):
                    with pe.Fori(0, QP // 2 - (quarter == QUARTERS - 1)) as i:
                        for k in range(2):
                            p = quarter * QP + k
                            hidden(i, p + 1)
                            weighted(i, p)
                            if quarter < QUARTERS - 1:
                                spread(q0 + (quarter + 1) * NB + 2 * i + k, k)
                hidden(0, PAIRS - 1)
                weighted(0, PAIRS - 2)
                weighted(0, PAIRS - 1)
                for b in range(4):
                    ins = pe.matmul(bank(b, 512), zeros, finite, start=False, stop=True, skip_group_check=True)
                ins.then_inc(acc_ps, 1)
                transposes(L, 2)
                pe.wait_ge(xt_ok, 4 * (4 * L + 3) + 4)
                wp = slot(L, S_PLEP).rearrange("p (c n) -> p c n", c=2)
                pT = sm[:, L, M_PT:M_PT + 2 * SEQ].rearrange("p (c n) -> p c n", c=2)
                for i in range(N_PLEG):
                    for t in range(T):
                        for c in range(2):
                            ins = pe.matmul(bank(i, CHUNK, at=t * CHUNK), pT[:, c, t * P:(t + 1) * P],
                                            wp[:, c, i * CHUNK:(i + 1) * CHUNK], start=(c == 0), stop=(c == 1))
                ins.then_inc(slot_used, 1)
                for i in range(N_PLEG):
                    ins = token_major(4 + i, L, S_PLEG + i)
                    ins.then_inc(slot_used, 1)

        @block.scalar
        def _(act):
            def square_rows(L, j):
                n = 3 * L + j
                if n:
                    act.wait_ge(h_ok, n)
                else:
                    act.wait_ge(ld_x, 16)
                for t in range(T):
                    if n or t:
                        act.wait_ge(ss_ok, 2 * n + t)
                    act.activation(ar(A_XSQ, D), h[:, t, :], ACT.Square, accum_out=ss[:, t:t + 1]).then_inc(ss_ok, 1)
                act.wait_ge(ms_ok, n + 1)
                act.activation(rstd[:, 1, :], rstd[:, 0, :], ACT.Sqrt).then_inc(rt_ok, 1)

            act.wait_ge(ang_ok, 1)
            act.activation(sin[:, :, :], ang[:, :, :], ACT.Sin)
            act.activation(cos[:, :, :], ang[:, :, :], ACT.Sin, scale=0.5).then_inc(sin_ok, 1)
            act.wait_ge(lam_in, 1)
            act.activation(lame[:, :, :], lams[:, :, :], ACT.Exp).then_inc(lam_exp, 1)

            def first_parts(n):
                for b in range(4):
                    act.wait_ge(xf_ok, 4 * n + b + 1)
                    src = ar(A_MIXT, DC, SEQ) if n % 4 == 1 else xf
                    act.activation(xh[:, 2 * b:2 * b + 2, :], src[:, 2 * b:2 * b + 2, :], ACT.Copy).then_inc(xh_ok, 1)

            for L in range(LAYERS):
                high(L, S_IN)
                high(L, S_IN + 1)
                square_rows(L, 0)
                first_parts(4 * L)
                high(L, S_IN + 2)
                for i in range(1, N_IN, 2):
                    for n in (i + 2, i + 3):
                        if n < N_IN:
                            high(L, S_IN + n)
                        elif n < N_IN + 2:
                            high(L, S_OUT + n - N_IN)
                    used(act, L, S_IN + i)
                    n = min(CHUNK, PW - i * CHUNK)
                    act.activation(proj[:, :, i * CHUNK:i * CHUNK + n], bank(4 + i % 4, T, CHUNK)[:, :, 0:n],
                                   ACT.Copy).then_inc(pj_act, 1)
                    if i == 7:
                        act.wait_ge(pj_dve, N_IN // 2 * L + 4)
                        act.wait_ge(pj_act, N_IN // 2 * L + 3)
                        for t in range(T):
                            act.activation(ar(A_SQ, T, C_KC)[:, t, :], proj[:, t, 0:C_KC], ACT.Square).then_inc(psq_ok, 1)
                act.wait_ge(gms_ok, L + 1)
                act.activation(gss[:, 1, :, :], gss[:, 0, :, :], ACT.Sqrt).then_inc(grt_ok, 1)
                act.wait_ge(ff_in, L + 1)
                act.activation(fl[:, 3, :, :], fl[:, 2, :, :], ACT.Exp).then_inc(act_step, 1)
                act.wait_ge(act_step, L + 1)
                act.activation(fl[:, 4, :, :], fl[:, 3, :, :], ACT.Ln, bias=1.0).then_inc(ff_ln, 1)
                act.wait_ge(pj_dve, N_IN // 2 * (L + 1))
                act.wait_ge(pj_act, N_IN // 2 * (L + 1))
                act.activation(gate[:, :, :, :].rearrange("p t k j -> p t (k j)"), proj[:, :, C_NG:PW],
                               ACT.Sigmoid).then_inc(gate_ok, 1)
                for n in range(0, 12, 2):
                    act.wait_ge(tb_ps, 12 * L + n + 1)
                    if n == 0:
                        dst_ = kcvT.rearrange("p k t -> p (k t)")
                    elif n in (2, 4):
                        dst_ = (qnT, qrT)[n // 4][:, :, (1 if n == 2 else 0) * P:][:, :, 0:P]
                    elif n in (6, 8):
                        dst_ = fT[0:HD + 2, n // 2 - 3, :, 0:P]
                    else:
                        dst_ = dqT.rearrange("p k t -> p (k t)")
                    height = HD + 2 if n in (6, 8) else P
                    src = bank(n % 4, 4, P, parts=height) if n in (2, 4, 6, 8) else bank(n % 4, 512)
                    act.activation(dst_, src, ACT.Copy).then_inc(tb_act, 1)
                act.wait_ge(kc_ms, L + 1)
                act.activation(kst4[0:NCP, 2, :], kst4[0:NCP, 1, :], ACT.Sqrt).then_inc(kc_rt, 1)
                act.wait_ge(cs_ok, L + 1)
                act.activation(pc[:, :, :, :], pc[:, :, :, :], ACT.Exp, scale=HD ** -0.5).then_inc(ce_ok, 1)
                act.wait_ge(pcT_ps, L + 1)
                act.activation(pcT[:, :, :], bank(4, T, P), ACT.Copy).then_inc(pcT_ok, 1)
                act.wait_ge(oc_ps, L + 1)
                act.activation(Oc.rearrange("p t j d -> p t (j d)"), psum[:, 6:8, :], ACT.Copy).then_inc(oc_ok, 1)
                for u in range(UNITS + 4):
                    if u < UNITS:
                        act.wait_ge(neg_ok, UNITS * L + u + 1)
                        Pu = Pb[:, u % 4, :]
                        act.activation(Pu[:, 0:P], Pu[:, 0:P], ACT.Exp, bias=nmax[:, u, 0:1], scale=-1.0,
                                       accum_out=den[:, u, 0:1])
                        act.activation(Pu[:, P:384], Pu[:, P:384], ACT.Exp, bias=nmax[:, u, 1:2], scale=-1.0,
                                       accum_out=den[:, u, 1:2]).then_inc(p_ok, 1)
                    if u >= 7 and u % 4 == 3:
                        g = (u - 7) // 4
                        act.wait_ge(pv_ps, UNITS * L + 4 * g + 4)
                        act.activation(O[:, 4 * g:4 * g + 4, :, :].rearrange("p u t d -> p (u t d)"),
                                       bank(6 + g % 2, 512), ACT.Copy).then_inc(o_ok, 1)
                act.wait_ge(dms_ok, L + 1)
                act.activation(dst[:, 1, :, :], dst[:, 0, :, :], ACT.Sqrt).then_inc(drt_ok, 1)
                act.wait_ge(mix_ok, L + 1)
                if L < LAYERS - 1:
                    act.dma_start(smr[:, :], rows[L + 1]).then_inc(ld_rows, 16)
                act.dma_start(ar(A_KEYS, SLOT), keys[L]).then_inc(ld_keys, 16)
                first_parts(4 * L + 1)
                high(L, S_OUT + 2)
                high(L, S_OUT + 3)
                high(L, S_Q)
                high(L, S_Q + 1)
                square_rows(L, 1)
                first_parts(4 * L + 2)
                def scores_out(g):
                    for t in range(T):
                        n = 2 * g + t
                        act.wait_ge(sc_ps, 8 * L + n + 1)
                        act.activation(sc[:, t, 4 * g:4 * g + 4, :], bank(4 + n % 4, 4, P), ACT.Copy).then_inc(sc_ok, 1)

                for i in range(N_Q):
                    high(L, S_Q + i + 2 if i + 2 < N_Q else u_slot(i + 2 - N_Q))
                    used(act, L, S_Q + i)
                    act.activation(pqT[:, 2 * i:2 * i + 2, :], bank(i % 4, 2, SEQ), ACT.Copy).then_inc(q_ok, 1)
                    if i >= 2 and i % 2 == 0:
                        scores_out(i // 2 - 1)

                def gelu(i, p, step=2):
                    used(act, L, u_slot(p) + 4 * i)
                    if p < QP:
                        out_ = ar(A_LEAD, QP * 512)[:, bass.ds((step * i + p) * 512, 512)]
                    else:
                        if p > QP:
                            act.wait_ge(w_ok, L * PAIRS + step * i + p - 1)
                        out_ = GL[:, p % 2, :]
                    act.activation(out_, bank(4 + p % 2, 512), ACT.Gelu).then_inc(gelu_ok, 1)

                def gates_out(quarter, i, n, step=2):
                    act.wait_ge(g_ps, (L * QUARTERS + quarter) * NB + step * i + n + 1)
                    buf = ar((quarter % 2) * SEQ * QI, SEQ * QI)
                    act.activation(buf[:, bass.ds((step * i + n) * TB * QI, TB * QI)], bank(6 + n % 2, 512),
                                   ACT.Copy).then_inc(g_ok, 1)

                def lead(i, ks):
                    for k in ks:
                        gelu(i, k, 4)
                        high(L, u_slot(0) + k + 2, i)

                gelu(0, 0)
                high(L, u_slot(2))
                scores_out(3)
                lead(0, range(1, 4))
                with act.Fori(1, QP // 4 - 1) as i:
                    lead(i, range(4))
                lead(QP // 4 - 1, range(2))
                act.wait_ge(ge_in, L + 1)
                act.activation(c16, c16, ACT.Exp).then_inc(ge_ok, 1)
                lead(QP // 4 - 1, range(2, 4))
                act.wait_ge(rout_dve, L + 1)
                for n in range(NB):
                    gates_out(0, 0, n)
                    if n == 1:
                        gelu(0, QP)

                def first_quarter(i, ks):
                    for k in ks:
                        high(L, v_slot(k + 1), i)
                        gates_out(1, i, k, 4)

                with act.Fori(0, QP // 4 - 1) as i:
                    first_quarter(i, range(4))
                first_quarter(QP // 4 - 1, range(3))
                high(L, u_slot(QP + 1))
                high(L, v_slot(QP))
                gates_out(1, 0, QP - 1)
                for quarter in range(1, QUARTERS):
                    act.wait_ge(w_ok, L * PAIRS + quarter * QP)
                    with act.Fori(0, QP // 2 - (quarter == QUARTERS - 1)) as i:
                        for k in range(2):
                            p = quarter * QP + k
                            gelu(i, p + 1)
                            high(L, u_slot(p + 2), i)
                            high(L, v_slot(p + 1), i)
                            if quarter < QUARTERS - 1:
                                gates_out(quarter + 1, i, k)
                gelu(0, PAIRS - 1)
                high(L, v_slot(PAIRS - 1))
                high(L, S_PLEG)
                high(L, S_PLEG + 1)
                square_rows(L, 2)
                first_parts(4 * L + 3)
                for i in range(N_PLEG):
                    if i + 2 < N_PLEG:
                        high(L, S_PLEG + i + 2)
                    used(act, L, S_PLEG + i)
                    act.activation(ar(i * 512, 512), bank(4 + i, 512), ACT.Sigmoid).then_inc(sg_ok, 1)
            act.wait_ge(h_ok, 3 * LAYERS)
            act.dma_start(out.rearrange("o (t p) d -> p (o t) d", p=P), h[:, :, :]).then_inc(out_st, 16)
            act.wait_ge(out_st, 16)

        @block.gpsimd
        def _(pool):
            def low(L, n, i=0):
                for j in range(2):
                    low_half(pool, L, n, i, j, lo_ok)

            def gated(L, quarter, i, n, step=2):
                pool.wait_ge(a1_ok, (L * QUARTERS + quarter) * NB + step * i + n + 1)
                pool.tensor_tensor(Ah[:, n % 2, :, :, :], mid(Eh[:, n % 2, :, :], 1, 3),
                                   last(g3[:, :, bass.ds((step * i + n) * TB, TB)], QI), ALU.mult).then_inc(a_ok, 1)

            for L in range(LAYERS):
                for n in REST:
                    if n < S_EXP:
                        low(L, n)
                with pool.Fori(0, QP // 4) as i:
                    for k in range(4):
                        low(L, u_slot(k), i)
                low(L, u_slot(QP))
                for n in range(NB):
                    gated(L, 0, 0, n)
                gated(L, 1, 0, 0)

                def ahead(quarter, i, k, step):
                    if not isinstance(i, int) or step * i + k < NB - 1:
                        gated(L, quarter + 1, i, k + 1, step)
                    elif quarter < QUARTERS - 2:
                        gated(L, quarter + 2, 0, 0)

                def first_quarter(i):
                    for k in range(4):
                        low_half(pool, L, v_slot(k), i, 1, vlo2_ok)
                        ahead(0, i, k, 4)

                with pool.Fori(0, QP // 4 - 1) as i:
                    first_quarter(i)
                first_quarter(QP // 4 - 1)
                low(L, u_slot(QP + 1))
                for quarter in range(1, QUARTERS - 1):
                    def body(i):
                        for k in range(2):
                            low(L, u_slot(quarter * QP + k + 2), i)
                            ahead(quarter, i, k, 2)

                    with pool.Fori(0, QP // 2 - 1) as i:
                        body(i)
                    body(QP // 2 - 1)
                with pool.Fori(0, QP // 2 - 1) as i:
                    for k in range(2):
                        low(L, u_slot(PAIRS - QP + k + 2), i)
                for i in range(N_PLEG):
                    low(L, S_PLEG + i)

        @block.vector
        def _(dve):
            steps = [0]

            def step(ins):
                steps[0] += 1
                ins.then_inc(dve_step, 1)

            def settle():
                dve.wait_ge(dve_step, steps[0])

            def feature_major(n, weight=None):
                dst_ = xf if weight is not None else ar(A_MIXT, DC, SEQ)
                for b in range(5):
                    r = slice(2 * b, 2 * b + 2)
                    if b < 4:
                        dve.wait_ge(xt_ps, 4 * n + b + 1)
                        if weight is not None:
                            dve.tensor_tensor(dst_[:, r, :], bank(b, 2, SEQ), last(weight[:, r], SEQ), ALU.mult).then_inc(xf_ok, 1)
                        else:
                            dve.tensor_copy(dst_[:, r, :], bank(b, 2, SEQ)).then_inc(xf_ok, 1)
                    if b:
                        r = slice(2 * b - 2, 2 * b)
                        dve.wait_ge(xf_ok, 4 * n + b)
                        dve.wait_ge(xh_ok, 4 * n + b)
                        dve.tensor_tensor(xl[:, r, :], dst_[:, r, :], xh[:, r, :].bitcast(F32), ALU.subtract).then_inc(xt_ok, 1)

            def mean_rstd(L, j):
                n = 3 * L + j
                dve.wait_ge(ss_ok, 2 * n + 2)
                dve.tensor_scalar(rstd[:, 0, :], ss[:, :], 1.0 / D, EPS, ALU.mult, ALU.add).then_inc(ms_ok, 1)
                dve.wait_ge(rt_ok, n + 1)
                step(dve.reciprocal(rstd[:, 2, :], rstd[:, 1, :]))
                settle()
                for t in range(T):
                    ins = dve.tensor_scalar(xn[:, t, :], h[:, t, :], rstd[:, 2, t:t + 1], None, ALU.mult)
                ins.then_inc(xn_ok, 1)
                feature_major(4 * L + (0, 2, 3)[j], sm[:, L, M_COL + j * DC:M_COL + (j + 1) * DC])

            dve.wait_ge(ld_pos, 16)
            dve.wait_ge(ld_const, 16)
            step(dve.tensor_copy(posf[:, :], posi[:, :]))
            settle()
            for t in range(T):
                step(dve.tensor_scalar(ang[:, t, :], kst[:, K_F64:K_F64 + NANG], posf[:, t:t + 1], None, ALU.mult))
            settle()
            step(dve.tensor_scalar(angk[:, :, :], ang[:, :, :], float(1 / TWO_PI), MAGIC, ALU.mult, ALU.add))
            settle()
            step(dve.tensor_scalar(angk[:, :, :], angk[:, :, :], -MAGIC, None, ALU.add))
            for c in PI_C:
                settle()
                step(dve.scalar_tensor_tensor(out=ang[:, :, :], in0=angk[:, :, :], scalar=-c, in1=ang[:, :, :],
                                              op0=ALU.mult, op1=ALU.add))
            settle()
            dve.tensor_scalar(ang[:, :, :], ang[:, :, :], 3.1415925, -3.1415925, ALU.min, ALU.max).then_inc(ang_ok, 1)
            dve.wait_ge(sin_ok, 1)
            step(dve.tensor_tensor(cos[:, :, :], cos[:, :, :], cos[:, :, :], ALU.mult))
            settle()
            step(dve.tensor_scalar(cos[:, :, :], cos[:, :, :], -2.0, 1.0, ALU.mult, ALU.add))
            dve.wait_ge(ld_cols, 16)
            lv = sm[:, :, M_LAM:M_LAM + 4 * DQK].rearrange("p l (a b c) -> p l a b c", a=2, b=2)
            for L in range(LAYERS):
                step(dve.tensor_tensor(lamp[:, L, :, :], lv[:, L, :, 0, :], lv[:, L, :, 1, :], ALU.mult))
            settle()
            dve.tensor_reduce(lams[:, :, :], lamp[:, :, :, :], AX, ALU.add).then_inc(lam_in, 1)
            dve.wait_ge(lam_exp, 1)
            step(dve.tensor_tensor(lam[:, :], lame[:, :, 1], lame[:, :, 0], ALU.subtract))
            settle()
            step(dve.tensor_tensor(lam[:, :], lam[:, :], kst[:, K_LI:K_LI + LAYERS], ALU.subtract))

            for L in range(LAYERS):
                mean_rstd(L, 0)
                for i in range(0, N_IN, 2):
                    used(dve, L, S_IN + i)
                    n = min(CHUNK, PW - i * CHUNK)
                    dve.tensor_copy(proj[:, :, i * CHUNK:i * CHUNK + n], bank(4 + i % 4, T, CHUNK)[:, :, 0:n]).then_inc(pj_dve, 1)
                dve.wait_ge(pj_act, N_IN // 2 * (L + 1))
                dve.wait_ge(pj_dve, N_IN // 2 * (L + 1))
                dve.wait_ge(ld_rows, 16 * (L + 1))
                step(dve.tensor_tensor(fl[:, 0, :, :], proj[:, :, C_FF:C_FF + FOX_H], mid(smr[:, M_FB:M_FB + FOX_H], 1, T), ALU.add))
                settle()
                step(dve.tensor_scalar(fl[:, 1, :, :], fl[:, 0, :, :], 0.0, None, ALU.min))
                step(dve.tensor_scalar(fl[:, 2, :, :], fl[:, 0, :, :], -1.0, None, ALU.mult))
                settle()
                dve.tensor_tensor(fl[:, 2, :, :], fl[:, 2, :, :], fl[:, 0, :, :], ALU.min).then_inc(ff_in, 1)
                dve.wait_ge(psq_ok, T * (L + 1))
                sq = ar(A_SQ, T, C_KC)
                for t in range(T):
                    step(dve.tensor_reduce(gss[:, 0, t, 0:G64], sq[:, t, 0:C_DQ].rearrange("p (g d) -> p g d", d=HD), AX, ALU.add))
                    step(dve.tensor_reduce(gss[:, 0, t, G64:NG], sq[:, t, C_DQ:C_KC].rearrange("p (g d) -> p g d", d=DQK), AX, ALU.add))
                settle()
                dve.tensor_scalar(gss[:, 0, :, 0:G64], gss[:, 0, :, 0:G64], 1.0 / HD, EPS, ALU.mult, ALU.add)
                dve.tensor_scalar(gss[:, 0, :, G64:NG], gss[:, 0, :, G64:NG], 1.0 / DQK, EPS, ALU.mult, ALU.add).then_inc(gms_ok, 1)
                dve.wait_ge(ff_ln, L + 1)
                dve.tensor_tensor(fl[:, 5, :, :], fl[:, 1, :, :], fl[:, 4, :, :], ALU.subtract).then_inc(ff_ls, 1)
                dve.wait_ge(grt_ok, L + 1)
                step(dve.reciprocal(gss[:, 2, :, :], gss[:, 1, :, :]))
                for t in range(T):
                    a = proj[:, t, 0:C_DQ].rearrange("p (g d) -> p g d", d=HD)
                    b = proj[:, t, C_DQ:C_KC].rearrange("p (g d) -> p g d", d=DQK)
                    settle()
                    step(dve.tensor_tensor(a, a, last(gss[:, 2, t, 0:G64], HD), ALU.mult))
                    step(dve.tensor_tensor(b, b, last(gss[:, 2, t, G64:NG], DQK), ALU.mult))
                settle()
                for t in range(T):
                    step(dve.tensor_tensor(proj[:, t, 0:C_KC], proj[:, t, 0:C_KC], smr[:, 0:C_KC], ALU.mult))
                settle()
                for t in range(T):
                    for c0, n, d, f in ((C_NQ, ROPE64, HD, 0), (C_DQ, ROPE32, DQK, HD // 2)):
                        hf = d // 2
                        src = proj[:, t, c0:c0 + n * d].rearrange("p (g s d) -> p g s d", s=2, d=hf)
                        dst_ = rope[:, t, c0 - C_NQ:c0 - C_NQ + n * d].rearrange("p (g s d) -> p g s d", s=2, d=hf)
                        cs, sn = cos[:, t, f:f + hf], sin[:, t, f:f + hf]
                        t1 = ar(A_TMP, n, hf)
                        t2 = ar(A_TMP + n * hf, n, hf)
                        settle()
                        step(dve.tensor_tensor(dst_, src, mid(mid(cs, 1, 2), 1, n), ALU.mult))
                        step(dve.tensor_tensor(t1, src[:, :, 1, :], mid(sn, 1, n), ALU.mult))
                        step(dve.tensor_tensor(t2, src[:, :, 0, :], mid(sn, 1, n), ALU.mult))
                        settle()
                        step(dve.tensor_tensor(dst_[:, :, 0, :], dst_[:, :, 0, :], t1, ALU.subtract))
                        step(dve.tensor_tensor(dst_[:, :, 1, :], dst_[:, :, 1, :], t2, ALU.add))
                for t in range(T):
                    for s in range(2):
                        dve.tensor_copy(fa[:, t, s, :, 0:HD], proj[:, t, s * 256:(s + 1) * 256].rearrange("p (g d) -> p g d", d=HD))
                        dve.memset(fa[:, t, s, :, HD + 1 - s:HD + 2 - s], 1.0)
                dve.wait_ge(ff_ps, L + 1)
                cps = bank(0, T, FOX_H)
                root = float(HD ** 0.5)
                for t in range(T):
                    dve.tensor_scalar(fa[:, t, 0, :, HD], cps[:, t, :], root, None, ALU.mult)
                    ins = dve.tensor_scalar(fa[:, t, 1, :, HD + 1], cps[:, t, :], -root, None, ALU.mult)
                step(ins)
                settle()
                dve.memset(X[:, :, :, NCMP:NCP], 0.0).then_inc(tok_ok, 1)
                for n in range(1, 12, 2):
                    dve.wait_ge(tb_ps, 12 * L + n + 1)
                    if n == 1:
                        dve.wait_ge(tb_act, 6 * L + 1)
                        pos = sm[:, L, M_POS:M_POS + 2 * CMP_LEN].rearrange("p (k l) -> p k l", k=2)
                        for kv in range(2):
                            for s in range(2):
                                win = kcvT[:, kv, s * 16:s * 16 + NCMP * 16].rearrange("p (n l) -> p l n", l=16)
                                ins = dve.tensor_tensor(X[:, kv, s * 16:s * 16 + 16, 0:NCMP], win,
                                                        last(pos[:, kv, s * 16:s * 16 + 16], NCMP), ALU.add)
                        ins.then_inc(x_ok, 1)
                    if n in (1, 5):
                        dst_ = (qnT, qrT)[n // 4][:, :, (0 if n == 1 else 1) * P:][:, :, 0:P]
                    elif n in (7, 9):
                        dst_ = fT[0:HD + 2, n // 2 - 3, :, P:SEQ]
                    elif n == 3:
                        dst_ = kswT.rearrange("p k t -> p (k t)")
                    else:
                        dst_ = dkT.rearrange("p k t -> p (k t)")
                    height = HD + 2 if n in (7, 9) else P
                    src = bank(n % 4, 4, P, parts=height) if n in (1, 5, 7, 9) else bank(n % 4, 512)
                    dve.tensor_copy(dst_, src).then_inc(tb_dve, 1)
                used(dve, L, S_CMP + 1)
                kcx = ar(A_KCX, 2, HD, parts=NCP)
                kcs = ar(A_KCS, 2, HD, parts=NCP)
                for g in range(2):
                    step(dve.tensor_copy(kcx[:, g, :], bank(4 + g, HD, parts=NCP)))
                    dve.tensor_copy(vcx[0:NCP, g * HD:(g + 1) * HD], bank(4 + g, HD, parts=NCP, at=HD))
                settle()
                step(dve.tensor_tensor(kcs, kcx, kcx, ALU.mult))
                settle()
                step(dve.tensor_reduce(kst4[0:NCP, 0, :], kcs, AX, ALU.add))
                settle()
                dve.tensor_scalar(kst4[0:NCP, 1, :], kst4[0:NCP, 0, :], 1.0 / HD, EPS, ALU.mult, ALU.add).then_inc(kc_ms, 1)
                dve.wait_ge(kc_rt, L + 1)
                step(dve.reciprocal(kst4[0:NCP, 3, :], kst4[0:NCP, 2, :]))
                settle()
                step(dve.tensor_tensor(kcx, kcx, last(kst4[0:NCP, 3, :], HD), ALU.mult))
                settle()
                dve.tensor_tensor(kcx, kcx, smr[0:NCP, M_KN:M_KN + 2 * HD].rearrange("p (g d) -> p g d", g=2), ALU.mult).then_inc(kc_tok, 1)
                dve.wait_ge(kc_ps, L + 1)
                vb = vbd.rearrange("p (j g) d -> p j g d", g=2)
                blk = kst[:, K_BLK:K_BLK + NSA_H].rearrange("p (j g) -> p j g", g=2)
                for g in range(2):
                    dve.tensor_tensor(vb[:, :, g, :], mid(bank(5, HD, at=256 + g * HD), 1, 4), last(blk[:, :, g], HD), ALU.mult)
                dve.tensor_copy(kcT[:, :], bank(4, NCP, at=256)).then_inc(kcT_ok, 1)
                dve.wait_ge(cs_ps, L + 1)
                pv = pc[:, :, :, :].rearrange("p t (j g) n -> p t j g n", g=2)
                for g in range(2):
                    for t in range(T):
                        step(dve.tensor_tensor(pv[:, t, :, g, :], bank(4 + g, 4, NCP, at=t * 4 * NCP),
                                               mid(kst[:, K_CM + t * NCP:K_CM + (t + 1) * NCP], 1, 4), ALU.add))
                settle()
                step(dve.tensor_reduce(cst[:, 0, :, :], pc[:, :, :, :], AX, ALU.max))
                settle()
                dve.tensor_tensor(pc[:, :, :, :], pc[:, :, :, :], last(cst[:, 0, :, :], NCP), ALU.subtract).then_inc(cs_ok, 1)
                for s in range(UNITS + 3):
                    u = s
                    if u < UNITS:
                        dve.wait_ge(s_ps, UNITS * L + u + 1)
                        if u >= 4:
                            dve.wait_ge(pt_ps, UNITS * L + u - 3)
                        scale = (DQK if u >= U_DIFF else HD) ** -0.5
                        mask = kst[:, K_MASK:K_MASK + SEQ]
                        Pu = Pb[:, u % 4, :]
                        dve.tensor_tensor_reduce(Pu[:, 0:P], bank(u % 4, P), mask[:, P:SEQ], -scale, 3e38, ALU.add, ALU.min,
                                                 nmax[:, u, 0:1])
                        dve.tensor_tensor_reduce(Pu[:, P:384], bank(u % 4, SEQ, at=P), mask, -scale, 3e38, ALU.add, ALU.min,
                                                 nmax[:, u, 1:2]).then_inc(neg_ok, 1)
                    if u == 1:
                        dve.wait_ge(ce_ok, L + 1)
                        step(dve.tensor_reduce(cst[:, 1, :, :], pc[:, :, :, :], AX, ALU.add))
                    u = s - 2
                    if 0 <= u < UNITS:
                        dve.wait_ge(pt_ps, UNITS * L + u + 1)
                        if u >= 3:
                            dve.wait_ge(pv_ps, UNITS * L + u - 2)
                        dve.tensor_copy(PTb[:, u % 3, :], bank(4 + u % 2, 384)).then_inc(pt_ok, 1)
                settle()
                dve.wait_ge(p_ok, UNITS * (L + 1))
                step(dve.reciprocal(rden[:, :, :], den[:, :, :]))
                step(dve.reciprocal(cst[:, 2, :, :], cst[:, 1, :, :]))
                settle()
                step(dve.tensor_tensor(cst[:, 2, :, :], cst[:, 2, :, :], last(kst[:, K_CV:K_CV + T], NSA_H), ALU.mult))
                dve.wait_ge(gate_ok, L + 1)
                rd = rden[:, :, :].rearrange("p u t -> p t u")
                step(dve.tensor_tensor(cf[:, :, 1, :], gate[:, :, 1, :], rd[:, :, U_SLC:U_WIN], ALU.mult))
                step(dve.tensor_tensor(cf[:, :, 2, :], gate[:, :, 2, :], rd[:, :, U_WIN:U_DIFF], ALU.mult))
                settle()
                step(dve.tensor_tensor(cf[:, :, 0, :], gate[:, :, 0, :], cst[:, 2, :, :], ALU.mult))
                rdo = rden[:, U_DIFF:UNITS, :].rearrange("p (h c) t -> p h c t", c=2)[:, :, 1, :]
                step(dve.tensor_scalar(rdo, rdo, lam[:, L:L + 1], None, ALU.mult))
                dve.wait_ge(o_ok, 7 * (L + 1))
                dve.wait_ge(oc_ok, L + 1)
                settle()
                for t in range(T):
                    settle()
                    fx = mix[:, t, 0:256].rearrange("p (g d) -> p g d", d=HD)
                    step(dve.tensor_tensor(fx, O[:, 0:4, t, :], last(rden[:, 0:4, t], HD), ALU.mult))
                    nm = mix[:, t, 256:768].rearrange("p (g d) -> p g d", d=HD)
                    step(dve.tensor_tensor(nm, Oc[:, t, :, :], last(cf[:, t, 0, :], HD), ALU.mult))
                    tmps = [ar(A_COMB + k * 512, NSA_H, HD) for k in range(2)]
                    for k, u0, tmp in ((1, U_SLC, tmps[0]), (2, U_WIN, tmps[1])):
                        step(dve.tensor_tensor(tmp, O[:, u0:u0 + NSA_H, t, :], last(cf[:, t, k, :], HD), ALU.mult))
                    for tmp in tmps:
                        settle()
                        step(dve.tensor_tensor(nm, nm, tmp, ALU.add))
                    dm = mix[:, t, 768:D].rearrange("p (g d) -> p g d", d=HD)
                    od = O[:, U_DIFF:UNITS, t, :].rearrange("p (h c) d -> p h c d", c=2)
                    rr = rden[:, U_DIFF:UNITS, t].rearrange("p (h c) -> p h c", c=2)
                    tm = ar(A_COMB + 1024, DIFF_H, HD)
                    step(dve.tensor_tensor(dm, od[:, :, 0, :], last(rr[:, :, 0], HD), ALU.mult))
                    step(dve.tensor_tensor(tm, od[:, :, 1, :], last(rr[:, :, 1], HD), ALU.mult))
                    settle()
                    step(dve.tensor_tensor(dm, dm, tm, ALU.add))
                    settle()
                    step(dve.tensor_tensor(tm, dm, dm, ALU.mult))
                    settle()
                    step(dve.tensor_reduce(dst[:, 0, t, :], tm, AX, ALU.add))
                settle()
                dve.tensor_scalar(dst[:, 0, :, :], dst[:, 0, :, :], 1.0 / HD, EPS, ALU.mult, ALU.add).then_inc(dms_ok, 1)
                dve.wait_ge(drt_ok, L + 1)
                step(dve.reciprocal(dst[:, 2, :, :], dst[:, 1, :, :]))
                settle()
                step(dve.tensor_scalar(dst[:, 2, :, :], dst[:, 2, :, :], kst[:, K_LI + LAYERS + L:K_LI + LAYERS + L + 1], None, ALU.mult))
                settle()
                for t in range(T):
                    dm = mix[:, t, 768:D].rearrange("p (g d) -> p g d", d=HD)
                    step(dve.tensor_tensor(dm, dm, last(dst[:, 2, t, :], HD), ALU.mult))
                settle()
                for t in range(T):
                    ins = dve.tensor_tensor(mix[:, t, 768:D], mix[:, t, 768:D], smr[:, M_SUB:M_SUB + 256], ALU.mult)
                ins.then_inc(mix_ok, 1)
                feature_major(4 * L + 1)
                for i in range(N_OUT):
                    used(dve, L, S_OUT + i)
                    hc_ = h[:, :, i * CHUNK:(i + 1) * CHUNK]
                    ins = dve.tensor_tensor(hc_, bank(4 + i, T, CHUNK), hc_, ALU.add)
                ins.then_inc(h_ok, 1)

                mean_rstd(L, 1)

                def best16(values, indices, scores):
                    for o in (0, 8):
                        for v, _, s in zip(values, indices, scores):
                            step(dve.max(v[:, o:o + 8], s))
                        settle()
                        for v, i, s in zip(values, indices, scores):
                            step(dve.max_index(i[:, o:o + 8], v[:, o:o + 8], s))
                        settle()
                        if o == 0:
                            for v, s in zip(values, scores):
                                step(dve.match_replace(s, v[:, 0:8], s, -3.0e38))
                            settle()

                for n in range(8):
                    g, t = n // 2, n % 2
                    dve.wait_ge(sc_ok, 8 * L + n + 1)
                    m = range(4 * g, 4 * g + 4)
                    best16([v16[:, t, j, :] for j in m], [i16[:, t, j, :] for j in m], [sc[:, t, j, :] for j in m])
                for t in range(T):
                    c4 = cand[:, t, :, :].rearrange("p h (a b) -> p h a b", a=TOPK)
                    vv = v16[:, t, :, :].rearrange("p (h c) k -> p h c k", c=2)
                    step(dve.tensor_tensor(c4, last(vv[:, :, 0, :], TOPK), mid(vv[:, :, 1, :], 2, TOPK), ALU.add))
                settle()
                for t in range(T):
                    m = range(PH)
                    best16([c16[:, t, j, :] for j in m], [p16[:, t, j, :] for j in m], [cand[:, t, j, :] for j in m])
                step(dve.tensor_copy(gden[:, 0, :, :], c16[:, :, :, 0]))
                step(dve.tensor_scalar(ab16[:, 0, :, :], p16.rearrange("p t h k -> p t (h k)"), 4, None, ALU.logical_shift_right))
                step(dve.tensor_scalar(ab16[:, 1, :, :], p16.rearrange("p t h k -> p t (h k)"), 15, None, ALU.bitwise_and))
                step(dve.tensor_copy(i16f, i16))
                settle()
                dve.tensor_tensor(c16, c16, last(gden[:, 0, :, :], TOPK), ALU.subtract).then_inc(ge_in, 1)
                step(dve.tensor_copy(abf, ab16))
                settle()
                iota = kst[:, K_IOTA:K_IOTA + TOPK]
                for s in range(2):
                    for t in range(T):
                        eq = ar(A_EQ + (t % 2) * 2048, PH * TOPK, TOPK)
                        eqh = ar(A_EQ + (t % 2) * 2048, PH, TOPK, TOPK)
                        ii = i16f[:, t, :, :].rearrange("p (h c) k -> p h c k", c=2)[:, :, s, :]
                        step(dve.tensor_tensor(eq, last(abf[:, s, t, :], TOPK), mid(iota, 1, PH * TOPK), ALU.is_equal))
                        settle()
                        step(dve.tensor_tensor(eqh, eqh, mid(ii, 2, TOPK), ALU.mult))
                        settle()
                        step(dve.tensor_reduce(rout[:, s, t, :], eq, AX, ALU.add))
                dve.wait_ge(ge_ok, L + 1)
                step(dve.tensor_reduce(gden[:, 0, :, :], c16, AX, ALU.add))
                settle()
                step(dve.reciprocal(gden[:, 1, :, :], gden[:, 0, :, :]))
                settle()
                dve.tensor_tensor(rout[:, 2, :, :].rearrange("p t (h k) -> p t h k", k=TOPK), c16,
                                  last(gden[:, 1, :, :], TOPK), ALU.mult).then_inc(rout_ok, 1)
                dve.wait_ge(rout_ps, L + 1)
                step(dve.tensor_copy(routT[:, 0:2, :], bank(6, 2, SEQ)))
                step(dve.tensor_copy(routT[:, 2, :], bank(7, SEQ)))
                for k in range(3):
                    settle()
                    ins = dve.tensor_copy(g3[:, k, :], routT[:, 2, :])
                    if k < 2:
                        step(ins)
                        settle()
                        step(dve.tensor_tensor(routT[:, 2, :], routT[:, 2, :], g3[:, k, :], ALU.subtract))
                ins.then_inc(rout_dve, 1)

                def onehots(quarter, i, n, step_=2, first=False):
                    m = (L * QUARTERS + quarter) * NB
                    if not first:
                        dve.wait_ge(g_ps, m + step_ * i + n - 1)
                    at = bass.ds((step_ * i + n) * TB, TB)
                    dve.tensor_tensor(Eh[:, n % 2, :, :], last(routT[:, 0, at], QI),
                                      mid(kst[:, K_IOTA + quarter * QI:K_IOTA + (quarter + 1) * QI], 1, TB),
                                      ALU.is_equal).then_inc(a1_ok, 1)
                    dve.tensor_tensor(Bh[:, n % 2, :, :], last(routT[:, 1, at], P),
                                      mid(kst[:, K_IOTA:K_IOTA + P], 1, TB), ALU.is_equal).then_inc(b_ok, 1)

                def weigh(i, p, step_=2):
                    n = L * PAIRS + step_ * i + p
                    dve.wait_ge(gelu_ok, n + 1)
                    src = ar(A_LEAD, QP * 512)[:, bass.ds((step_ * i + p) * 512, 512)] if p < QP else GL[:, p % 2, :]
                    if L or not isinstance(i, int) or step_ * i + p:
                        dve.wait_ge(w_ok, n)
                        if not isinstance(i, int):
                            used(dve, L, v_slot(p) - (1 if p < QP else 2) + 4 * i)
                        elif step_ * i + p:
                            used(dve, L, v_slot(step_ * i + p - 1))
                        else:
                            used(dve, L - 1, v_slot(PAIRS - 1))
                    g = ar(p // QP % 2 * SEQ * QI, SEQ, QI)
                    gv = g[:, :, bass.ds(2 * step_ * i + 2 * (p % QP), 2)].rearrange("p t e -> p e t")
                    dve.tensor_tensor(W, src.rearrange("p (e t) -> p e t", e=2), gv, ALU.mult).then_inc(w1_ok, 1)
                    dve.wait_ge(w1_ok, n + 1)
                    dve.tensor_copy(Wh[:, :, :], W).then_inc(w2_ok, 1)
                    dve.wait_ge(w2_ok, n + 1)
                    dve.tensor_tensor(Wl[:, :, :], W, Wh[:, :, :].bitcast(F32), ALU.subtract).then_inc(w_ok, 1)

                def low(i, p):
                    for j in range(1 if p < QP else 2):
                        low_half(dve, L, v_slot(p), i, j, vlo_ok)

                def ahead(quarter, i, k, step_=2):
                    if not isinstance(i, int) or step_ * i + k < NB - 1:
                        onehots(quarter + 1, i, k + 1, step_)
                    elif quarter < QUARTERS - 2:
                        onehots(quarter + 2, 0, 0)

                for n in range(NB):
                    onehots(0, 0, n, first=(L == 0 and n < 2))
                onehots(1, 0, 0)
                dve.wait_ge(g_ok, (L * QUARTERS + 1) * NB)

                def first_quarter(i):
                    for k in range(4):
                        low(i, k)
                        weigh(i, k, 4)
                        ahead(0, i, k, 4)

                first_quarter(0)
                with dve.Fori(1, QP // 4 - 1) as i:
                    first_quarter(i)
                first_quarter(QP // 4 - 1)
                for quarter in range(1, QUARTERS):
                    dve.wait_ge(g_ok, (L * QUARTERS + quarter + 1) * NB)

                    def body(i):
                        for k in range(2):
                            weigh(i, quarter * QP + k)
                            low(i, quarter * QP + k)
                            if quarter < QUARTERS - 1:
                                ahead(quarter, i, k)

                    with dve.Fori(0, QP // 2 - 1) as i:
                        body(i)
                    if quarter < QUARTERS - 1:
                        body(QP // 2 - 1)
                for p in (PAIRS - 2, PAIRS - 1):
                    weigh(0, p)
                    low(0, p)
                dve.wait_ge(acc_ps, L + 1)
                for t in range(T):
                    for half in range(2):
                        hh = h[:, t, half * 512:(half + 1) * 512]
                        ins = dve.tensor_tensor(hh, bank(2 * t + half, 512), hh, ALU.add)
                ins.then_inc(h_ok, 1)
                mean_rstd(L, 2)
                used(dve, L, S_PLEP)
                for i in range(N_PLEG):
                    dve.wait_ge(sg_ok, N_PLEG * L + i + 1)
                    g2 = ar(i * 512, 512)
                    step(dve.tensor_tensor(g2, bank(i, 512), g2, ALU.mult))
                settle()
                for i in range(N_PLEG):
                    hc_ = h[:, :, i * CHUNK:(i + 1) * CHUNK]
                    ins = dve.tensor_tensor(hc_, ar(i * 512, T, CHUNK), hc_, ALU.add)
                ins.then_inc(h_ok, 1)


def _columns():
    widths = (256, 256, 256, 4, 512, 128, 128, 128, 128, 128, 128, 24, 256, 256, 256)
    at = np.concatenate([[0], np.cumsum(widths)])
    fq, fk, fv, ff, nq, kc, vc, ks, vs, kw, vw, ng, dq, dk, dv = (np.arange(at[i], at[i + 1]) for i in range(15))
    nq = nq.reshape(NSA_H, HD)[PAIRED].reshape(-1)
    ng = ng.reshape(NSA_H, 3)[PAIRED].T.reshape(-1)
    return np.concatenate([fq, fk, nq, ks, kw, dq, dk, kc, vc, fv, dv, vs, vw, ff, ng])


def _consts():
    c = np.zeros((P, CONST), np.float32)
    r = np.arange(P)
    c[:, K_ID:K_ID + P] = np.eye(P)
    c[:, K_TRI:K_TRI + P] = r[:, None] <= r[None, :]
    c[:, K_ONE:K_ONE + P] = 1.0
    c[:, K_MASK + P:K_MASK + SEQ] = np.where(r[None, :] <= r[:, None], 0.0, -BIG)
    c[:, K_IOTA:K_IOTA + P] = r[None, :]
    c[:, K_BLK:K_BLK + NSA_H] = (r[:, None] // NCP) == np.arange(NSA_H)[None, :]
    c[0:NCP, K_REP:K_REP + P] = np.arange(NCP)[:, None] == (r[None, :] % NCP)
    for t in range(T):
        end = np.arange(NCP) * CMP_STRIDE + CMP_LEN - 1
        ok = (end[None, :] <= (t * P + r)[:, None]) & (np.arange(NCP) < NCMP)[None, :]
        c[:, K_CM + t * NCP:K_CM + (t + 1) * NCP] = np.where(ok, 0.0, -BIG)
        c[:, K_CV + t] = ok.any(1)
    for at, d in ((K_F64, HD), (K_F32, DQK)):
        half = d // 2
        f = np.float32(THETA) ** (-np.arange(half, dtype=np.float32) / np.float32(half))
        c[:, at:at + half] = f.astype(np.float32)
    for i in range(LAYERS):
        init = 0.8 - 0.6 * np.exp(-0.3 * i)
        c[:, K_LI + i] = init
        c[:, K_LI + LAYERS + i] = 1.0 - init
    return c


def _stream(a):
    s = np.zeros((LAYERS, SLOTS, P, SLOT), np.float32)
    cols = _columns()

    def wide(dst, w):
        for i in range(-(-w.shape[1] // CHUNK)):
            part = w[:, i * CHUNK:(i + 1) * CHUNK]
            n = part.shape[1]
            dst[i, :, 0:DC * n] = part.reshape(DC, P, n).transpose(1, 0, 2).reshape(P, DC * n)

    for L in range(LAYERS):
        wide(s[L, S_IN:S_CMP], a["w_in"][L][:, cols])
        for kv in range(2):
            w = a["nsa_cmp_w"][L, kv].reshape(CMP_LEN, HD, HD).transpose(1, 0, 2).reshape(HD, SLOT)
            s[L, S_CMP + kv, 0:HD] = w
            s[L, S_CMP + kv, HD:P] = w
        wo = a["w_out"][L]
        nsa = wo[256:768].reshape(NSA_H, HD, D)[PAIRED].reshape(512, D)
        wide(s[L, S_OUT:S_Q], np.concatenate([wo[0:256], nsa, wo[768:]]))
        wide(s[L, S_Q:S_EXP], a["peer_w_q"][L])
        u = a["peer_u"][L].reshape(PAIRS, 2, P, DC, P).transpose(0, 4, 1, 3, 2).reshape(PAIRS, P, SLOT)
        v = a["peer_v"][L].reshape(PAIRS, 2, P, D).transpose(0, 2, 1, 3).reshape(PAIRS, P, SLOT)
        for i in range(PAIRS):
            s[L, u_slot(i)] = u[i]
            s[L, v_slot(i)] = v[i]
        s[L, S_PLEP] = a["ple_w_proj"][L].reshape(2, P, D).transpose(1, 0, 2).reshape(P, SLOT)
        wide(s[L, S_PLEG:SLOTS], a["ple_w_gate"][L])
    return s.reshape(LAYERS * SLOTS, P, SLOT)


def _keys(a):
    return np.ascontiguousarray(a["peer_sub_keys"].reshape(LAYERS, HC, NKEYS, P).transpose(0, 3, 1, 2).reshape(LAYERS, P, SLOT))


def _rows(a):
    s = np.zeros((LAYERS, P, ROWS), np.float32)
    for L in range(LAYERS):
        rows = [np.tile(a["fox_q_norm_w"][L], FOX_H), np.tile(a["fox_k_norm_w"][L], FOX_H),
                np.tile(a["nsa_q_norm_w"][L], NSA_H), np.tile(a["nsa_k_norm_w"][L], 4),
                np.tile(a["diff_q_norm_w"][L], 2 * DIFF_H), np.tile(a["diff_k_norm_w"][L], 2 * DIFF_H),
                a["fox_f_bias"][L], np.tile(a["nsa_k_norm_w"][L], 2), np.tile(a["diff_subln_w"][L], DIFF_H)]
        s[L] = np.concatenate(rows)[None, :]
    return s


def _cols(a):
    s = np.zeros((LAYERS, P, COLS), np.float32)
    for L in range(LAYERS):
        for j, name in enumerate(("attn_norm_w", "ffn_norm_w", "ple_norm_w")):
            s[L, :, M_COL + j * DC:M_COL + (j + 1) * DC] = a[name][L].reshape(DC, P).T
        pos = a["nsa_cmp_pos"][L].transpose(2, 0, 1).reshape(HD, 2 * CMP_LEN)
        s[L, 0:HD, M_POS:M_PT] = pos
        s[L, HD:P, M_POS:M_PT] = pos
        s[L, :, M_PT:M_LAM] = a["p"][L, 0].T.reshape(2, P, SEQ).transpose(1, 0, 2).reshape(P, 2 * SEQ)
        s[L, :, M_LAM:COLS] = a["diff_lambda"][L].reshape(1, -1)
    return s


def kernel(**inputs):
    import numpy as _np
    import concourse.bacc as _bacc
    from concourse import mybir as _mybir
    from concourse.bass_utils import run_bass_kernel_spmd as _run

    a = {k: _np.asarray(v) for k, v in inputs.items()}
    arrays = {
        "x": _np.ascontiguousarray(a["x"]),
        "positions": _np.ascontiguousarray(a["positions"]),
        "rows": _rows(a),
        "cols": _cols(a),
        "consts": _consts(),
        "keys": _keys(a),
        "stream": _stream(a),
    }
    nc = _bacc.Bacc("TRN2", target_bir_lowering=False, num_devices=1)
    args = [nc.dram_tensor(k, v.shape, _mybir.dt.from_np(v.dtype), kind="ExternalInput").ap() for k, v in arrays.items()]
    out = nc.dram_tensor("out", (1, SEQ, D), _mybir.dt.float32, kind="ExternalOutput").ap()
    trunk(nc, *args, out)
    r = _run(nc, [arrays], core_ids=[0])
    return r.results[0]["out"]
```

```python
from contextlib import ExitStack

import numpy as np

import concourse.bass as bass
from concourse import mybir

F32 = mybir.dt.float32
F32R = mybir.dt.float32r
BF16 = mybir.dt.bfloat16
I32 = mybir.dt.int32
U32 = mybir.dt.uint32
ALU = mybir.AluOpType
ACT = mybir.ActivationFunctionType
AX = mybir.AxisListType.X

P = 128
D = 1024
SEQ = 256
T = SEQ // P
DC = D // P
LAYERS = 2
PLE = 256
EPS = 1e-6
THETA = 10000.0
FOX_H, NSA_H, DIFF_H = 4, 8, 4
HD, DQK = 64, 32
CMP_LEN, CMP_STRIDE = 32, 16
NCMP = (SEQ - CMP_LEN) // CMP_STRIDE + 1
NCP = 16
NKEYS, TOPK, PH = 128, 16, 8
HC = PH * 2
BIG = 1.0e30

C_FQ, C_FK, C_NQ, C_KS, C_KW, C_DQ, C_DK = 0, 256, 512, 1024, 1152, 1280, 1536
C_KC, C_VC, C_FV, C_DV, C_VS, C_VW, C_FF, C_NG = 1792, 1920, 2048, 2304, 2560, 2688, 2816, 2820
PW = 2844
REM = PW - C_FF
G64, G32 = C_DQ // HD, (C_KC - C_DQ) // DQK
NG = G64 + G32
ROPE64 = (C_DQ - C_NQ) // HD
ROPE32 = G32
PAIRED = [0, 4, 1, 5, 2, 6, 3, 7]

SLOT = 2048
RING = 4
CHUNK = 256
N_IN = -(-PW // CHUNK)
N_CMP, N_OUT, N_Q, N_EXP, N_PLEP, N_PLEG = 2, D // CHUNK, HC * P // CHUNK, 128, 1, D // CHUNK
S_IN = 0
S_CMP = S_IN + N_IN
S_OUT = S_CMP + N_CMP
S_Q = S_OUT + N_OUT
S_EXP = S_Q + N_Q
S_PLEP = S_EXP + N_EXP
S_PLEG = S_PLEP + N_PLEP
SLOTS = S_PLEG + N_PLEG

PAIRS = NKEYS // 2
QUARTERS = 4
QI = NKEYS // QUARTERS
QP = PAIRS // QUARTERS
TB = 16
NB = SEQ // TB
LEAD = QP + 1
assert NB == QP

M_NORM = 0
M_FB = M_NORM + C_KC
M_KN = M_FB + FOX_H
M_SUB = M_KN + 2 * HD
ROWS = M_SUB + DIFF_H * 2 * DQK
M_COL = 0
M_POS = M_COL + 3 * DC
M_PT = M_POS + 2 * CMP_LEN
M_LAM = M_PT + 2 * SEQ
COLS = M_LAM + 4 * DQK

K_ID = 0
K_TRI = K_ID + P
K_ONE = K_TRI + P
K_MASK = K_ONE + P
K_IOTA = K_MASK + SEQ
K_BLK = K_IOTA + P
K_REP = K_BLK + NSA_H
K_CM = K_REP + P
K_CV = K_CM + T * NCP
K_F64 = K_CV + T
K_F32 = K_F64 + HD // 2
K_LI = K_F32 + DQK // 2
CONST = K_LI + 2 * LAYERS
NANG = HD // 2 + DQK // 2

A_PROJ = 0
A_SQ = 5696
A_O = A_SQ
A_ROPE = A_SQ + T * C_KC
A_OC = A_O + 28 * T * HD
A_TMP = 11840
A_VBD, A_KCX, A_KCS = A_TMP, A_TMP + 512, A_TMP + 640
A_FA = 12608
A_FT = 13664
A_PC, A_PCT, A_VCX, A_KCT = (A_FA + x for x in (0, T * P, 2 * T * P, 2 * T * P + 2 * HD))
A_SM = A_KCT + NCP
A_ANG = A_FT
A_QNT, A_QRT, A_KSW, A_KCV, A_DQ, A_DK = (A_FT + x for x in (2048, 3072, 4096, 4608, 5120, 5632))
A_X = A_FT + 6144
A_P = A_OC + T * NSA_H * HD
A_PT = A_X
A_ROT = A_COMB = A_PT + 3 * 384
A_MIX = 0
A_MIXT = 2048
A_XN, A_XSQ = 6144, 4608
A_XF = 0
A_PQ, A_SC, A_CAND, A_EQ = 0, 4096, 0, 4096
A_LEAD = SEQ * QI
A_KEYS = A_LEAD + (QP - 4) * 512
A_B = 2 * SEQ * QI
A_E = A_B + TB * P
A_A = A_E + TB * QI
A_GL = A_A + 3 * TB * QI
A_W = A_GL + 2 * 512
ARENA = A_W + 512
A_RT = A_B
assert A_PT + 3 * 384 <= ARENA and A_P + 4 * 384 <= A_TMP

U_FOX, U_SLC, U_WIN, U_DIFF, UNITS = 0, 4, 12, 20, 28
NSA_STEPS = 10
TWO_PI = 2 * np.pi
PI_C = [6.28125, 0.00193500518798828125, 3.01991438e-07]
MAGIC = float(1.5 * 2 ** 23)


def u_slot(p):
    return S_EXP + (p if p < LEAD else 2 * p - 1)


def v_slot(p):
    return S_EXP + (LEAD + p if p < QP else 2 * p + 2 if p < PAIRS - 1 else 2 * p + 1)


WHOLE = (S_CMP, S_CMP + 1)
SPLIT = [n for n in range(SLOTS) if n not in WHOLE]
ORDER = {n: m for m, n in enumerate(SPLIT)}
V_ALL = [v_slot(p) for p in range(PAIRS)]
REST = [n for n in SPLIT if n not in V_ALL]
WIDTH = {n: DC * min(CHUNK, PW - (n - S_IN) * CHUNK) if n < S_CMP else SLOT for n in SPLIT}
V_STEP = {v_slot(p): 4 if p < QP else 2 for p in range(PAIRS)}
U_STEP = {n: 2 if n > u_slot(LEAD - 1) else 4 for n in REST}


def trunk(nc, x, positions, rows, cols, consts, keys, stream, out):
    ctx = ExitStack()
    with ctx:
        def sb(name, shape, dt=F32):
            return ctx.enter_context(nc.sbuf_tensor(name, shape, dt))

        def sem(name):
            return ctx.enter_context(nc.semaphore(name))

        h = sb("h", [P, T, D])
        xh = sb("xh", [P, DC, SEQ], F32R)
        xl = sb("xl", [P, DC, SEQ], F32R)
        wh = sb("wh", [P, 2, SLOT], F32R)
        wl = sb("wl", [P, 2, SLOT], F32R)
        Wh = sb("Wh", [P, 2, 2, SEQ], F32R)
        Wl = sb("Wl", [P, 2, 2, SEQ], F32R)
        ring = sb("ring", [P, RING, SLOT])
        arena = sb("arena", [P, ARENA])
        kst = sb("kst", [P, CONST])
        smr = sb("smr", [P, ROWS])
        sm = sb("sm", [P, LAYERS, COLS])
        idx2 = sb("idx2", [P, 2, SEQ, 2], BF16)
        g3 = sb("g3", [P, 3, SEQ, 2], BF16)
        iota = sb("iota", [P, P // 2, 2], BF16)
        posi = sb("posi", [P, T], I32)
        posf = sb("posf", [P, T])
        sin = sb("sin", [P, T, NANG])
        cos = sb("cos", [P, T, NANG])
        lams = sb("lams", [P, LAYERS, 2])
        lame = sb("lame", [P, LAYERS, 2])
        lam = sb("lam", [P, LAYERS])
        ss = sb("ss", [P, T])
        rstd = sb("rstd", [P, 3, T])
        gate = sb("gate", [P, T, 3, NSA_H])

        psum = ctx.enter_context(nc.psum_tensor("psum", [P, 8, 512], F32))

        def ar(off, *dims, parts=P):
            n = int(np.prod(dims))
            v = arena[0:parts, off:off + n]
            if len(dims) == 1:
                return v
            names = "abcd"[:len(dims)]
            return v.rearrange(f"p ({' '.join(names)}) -> p {' '.join(names)}", **dict(zip(names[1:], dims[1:])))

        def bank(b, *dims, parts=P, at=0):
            n = int(np.prod(dims))
            v = psum[0:parts, b, at:at + n]
            if len(dims) == 1:
                return v
            names = "abcd"[:len(dims)]
            return v.rearrange(f"p ({' '.join(names)}) -> p {' '.join(names)}", **dict(zip(names[1:], dims[1:])))

        def last(v, n):
            return v.unsqueeze(len(v.shape)).to_broadcast(list(v.shape) + [n])

        def mid(v, at, n):
            s = list(v.shape)
            return v.unsqueeze(at).to_broadcast(s[:at] + [n] + s[at:])

        ident = kst[:, K_ID:K_ID + P]
        zeros = kst[:, K_MASK:K_MASK + P // 2].bitcast(BF16)
        finite = kst[:, K_ID:K_ID + SEQ].bitcast(BF16)
        ang, angk = ar(A_ANG, T, NANG), ar(A_ANG + T * NANG, T, NANG)
        lamp = ar(A_ANG + 2 * T * NANG, LAYERS, 2, DQK)
        pc, pcT, vcx, kcT = ar(A_PC, T, NSA_H, NCP), ar(A_PCT, T, P), ar(A_VCX, 2 * HD), ar(A_KCT, NCP)
        gss, fl = ar(A_PT, 3, T, NG), ar(A_PT + 3 * T * NG, 6, T, FOX_H)
        nmax, den, rden = (ar(A_SM + k * T * UNITS, UNITS, T) for k in range(3))
        cst, cf = (ar(A_SM + 3 * T * UNITS + k * 3 * T * NSA_H, *d) for k, d in enumerate(((3, T, NSA_H), (T, 3, NSA_H))))
        dst, kst4 = ar(A_SM + 3 * T * (UNITS + 2 * NSA_H), 3, T, DIFF_H), ar(A_SM + 3 * T * (UNITS + 2 * NSA_H + DIFF_H), 4, 2)
        rem = ar(A_X + 512, SEQ)
        proj = ar(A_PROJ, T, PW)
        rope = ar(A_ROPE, T, C_KC - C_NQ)
        fa = ar(A_FA, T, 2, FOX_H, HD + 2)
        fT = ar(A_FT, 2, FOX_H, SEQ)
        qnT = ar(A_QNT, 4, SEQ)
        qrT = ar(A_QRT, 4, SEQ)
        kswT = ar(A_KSW, 2, SEQ)
        kcvT = ar(A_KCV, 2, SEQ)
        dqT = ar(A_DQ, 2, SEQ)
        dkT = ar(A_DK, 2, SEQ)
        X = ar(A_X, 2, CMP_LEN, NCP)
        vbd = ar(A_VBD, NSA_H, HD)
        O = ar(A_O, UNITS, T, HD)
        Oc = ar(A_OC, T, NSA_H, HD)
        mix = ar(A_MIX, T, D)
        Pb = ar(A_P, 4, 384)
        PTb = ar(A_PT, 3, 384)
        xn = ar(A_XN, T, D)
        pqT = ar(A_PQ, HC, SEQ)
        sc = ar(A_SC, T, HC, NKEYS)
        cand = ar(A_CAND, T, PH, TOPK * TOPK)
        Bh = ar(A_B, TB * P).bitcast(BF16).rearrange("p (a b c) -> p a b c", a=2, b=TB)
        Eh = ar(A_E, TB * QI).bitcast(BF16).rearrange("p (a b c) -> p a b c", a=2, b=TB)
        Ah = ar(A_A, 3 * TB * QI).bitcast(BF16).rearrange("p (a k b c) -> p a k b c", a=2, k=3, b=TB)
        GL = ar(A_GL, 2, 512)
        W = ar(A_W, 2, SEQ)
        gres = ar(A_W, SEQ)
        xf = ar(A_XF, DC, SEQ)
        ph, pl = Wh[:, 0], Wl[:, 0]
        v16 = ar(A_RT, T, HC, TOPK)
        i16 = ar(A_RT + 512, T, HC, TOPK).bitcast(U32)
        i16b = ar(A_RT + 1024, T * HC * TOPK // 2).bitcast(BF16)
        c16 = ar(A_RT + 1536, T, PH, TOPK)
        p16 = ar(A_RT + 1792, T, PH, TOPK).bitcast(U32)
        ab16 = ar(A_RT + 2048, 2, T, PH * TOPK).bitcast(U32)
        ranks2 = ar(A_RT + 2560, 2 * T * PH * TOPK).bitcast(BF16).rearrange("p (c n b) -> p c n b", c=2, b=2)
        rout = ar(A_RT + 3072, 3, T, PH * TOPK)
        gden = ar(A_RT + 3840, 2, T, PH)

        ld_x, ld_rows, ld_cols, ld_const, ld_pos = (sem(n) for n in ("ld_x", "ld_rows", "ld_cols", "ld_const", "ld_pos"))
        hi_ok, lo_ok, vlo_ok, vlo2_ok, xf_ok, xh_ok = (sem(n) for n in ("hi_ok", "lo_ok", "vlo_ok", "vlo2_ok", "xf_ok", "xh_ok"))
        w1_ok, w2_ok = sem("w1_ok"), sem("w2_ok")
        slot_ld = [sem(f"slot_ld{i}") for i in range(RING)]
        slot_used = sem("slot_used")
        ang_ok, sin_ok, lam_in, lam_exp = sem("ang_ok"), sem("sin_ok"), sem("lam_in"), sem("lam_exp")
        h_ok = sem("h_ok")
        ss_ok, ms_ok, rt_ok, xn_ok, xt_ps, xt_ok = (sem(n) for n in ("ss_ok", "ms_ok", "rt_ok", "xn_ok", "xt_ps", "xt_ok"))
        pj_dve, pj_act = sem("pj_dve"), sem("pj_act")
        psq_ok, gms_ok, grt_ok, nrm_ok = (sem(n) for n in ("psq_ok", "gms_ok", "grt_ok", "nrm_ok"))
        ff_in, ff_ln, ff_ls, ff_ps = sem("ff_in"), sem("ff_ln"), sem("ff_ls"), sem("ff_ps")
        tok_ok, tb_ps, tb_dve, tb_act = sem("tok_ok"), sem("tb_ps"), sem("tb_dve"), sem("tb_act")
        x_ok, kc_ms, kc_rt, kc_tok, kc_ps, kcT_ok = (sem(n) for n in ("x_ok", "kc_ms", "kc_rt", "kc_tok", "kc_ps", "kcT_ok"))
        cs_ps, cs_ok, ce_ok, pcT_ps, pcT_ok, oc_ps, oc_ok = (sem(n) for n in ("cs_ps", "cs_ok", "ce_ok", "pcT_ps", "pcT_ok", "oc_ps", "oc_ok"))
        s_ps, neg_ok, p_ok, pt_ps, pt_ok, pv_ps, o_ok = (sem(n) for n in ("s_ps", "neg_ok", "p_ok", "pt_ps", "pt_ok", "pv_ps", "o_ok"))
        cf_ok, nsa_step = sem("cf_ok"), sem("nsa_step")
        rem_ok, rem_ps = sem("rem_ok"), sem("rem_ps")
        gate_ok, dms_ok, drt_ok, mix_ok = (sem(n) for n in ("gate_ok", "dms_ok", "drt_ok", "mix_ok"))
        ld_keys = sem("ld_keys")
        q_ok, sc_ps, sc_ok = sem("q_ok"), sem("sc_ps"), sem("sc_ok")
        ge_in, ge_ok, rout_ok, rout_ps, rout_dve = (sem(n) for n in ("ge_in", "ge_ok", "rout_ok", "rout_ps", "rout_dve"))
        b_ok, e_ok, a_ok, a3_ok, g_ps, g_ok = (sem(n) for n in ("b_ok", "e_ok", "a_ok", "a3_ok", "g_ps", "g_ok"))
        gelu_ok, w_ok, acc_ps = sem("gelu_ok"), sem("w_ok"), sem("acc_ps")
        sg_ok, ph_ok, pl_ok = sem("sg_ok"), sem("ph_ok"), sem("pl_ok")
        dve_step, act_step, rot_step = sem("dve_step"), sem("act_step"), sem("rot_step")
        out_st = sem("out_st")

        def split_ready(eng, L, n, i=0):
            m = ORDER[n]
            k = L * SLOTS + n
            eng.wait_ge(slot_ld[k % RING], 16 * (i + k // RING + 1))
            if m >= 2 or L:
                eng.wait_ge(slot_used, (L * SLOTS + SPLIT[m - 2] if m >= 2 else (L - 1) * SLOTS + SPLIT[m - 2]) + 4 * i + 1)

        def buffer_of(L, n):
            return (L * len(SPLIT) + ORDER[n]) % 2

        def half_of(n, j):
            return slice(j * WIDTH[n] // 2, (j + 1) * WIDTH[n] // 2)

        def high(L, n, i=0):
            split_ready(nc.scalar, L, n, i)
            for j in range(2):
                c = half_of(n, j)
                nc.scalar.activation(wh[:, buffer_of(L, n), c], ring[:, (L * SLOTS + n) % RING, c], ACT.Copy).then_inc(hi_ok, 1)

        def low_half(eng, L, n, i, j, done):
            m, b, c = ORDER[n], buffer_of(L, n), half_of(n, j)
            split_ready(eng, L, n, i)
            eng.wait_ge(hi_ok, 2 * (L * len(SPLIT) + m + 4 * i) + j + 1)
            eng.tensor_tensor(wl[:, b, c], ring[:, (L * SLOTS + n) % RING, c], wh[:, b, c].bitcast(F32),
                              ALU.subtract).then_inc(done, 1)

        def used(eng, L, n):
            eng.wait_ge(slot_used, L * SLOTS + n + 1)

        def heads(v):
            return v.rearrange("p t (g d) -> p t g d", d=HD)

        def rotate(eng, t, c0, n, d, f, tmp, step, settle):
            hf = d // 2
            src = proj[:, t, c0:c0 + n * d].rearrange("p (g s d) -> p g s d", s=2, d=hf)
            dst_ = rope[:, t, c0 - C_NQ:c0 - C_NQ + n * d].rearrange("p (g s d) -> p g s d", s=2, d=hf)
            cs, sn = cos[:, t, f:f + hf], sin[:, t, f:f + hf]
            t1, t2 = ar(tmp, n, hf), ar(tmp + n * hf, n, hf)
            settle()
            step(eng.tensor_tensor(dst_, src, mid(mid(cs, 1, 2), 1, n), ALU.mult))
            step(eng.tensor_tensor(t1, src[:, :, 1, :], mid(sn, 1, n), ALU.mult))
            step(eng.tensor_tensor(t2, src[:, :, 0, :], mid(sn, 1, n), ALU.mult))
            settle()
            step(eng.tensor_tensor(dst_[:, :, 0, :], dst_[:, :, 0, :], t1, ALU.subtract))
            step(eng.tensor_tensor(dst_[:, :, 1, :], dst_[:, :, 1, :], t2, ALU.add))

        block = ctx.enter_context(nc.Block())

        @block.sync
        def _(sp):
            sp.dma_start(h[:, :, :], x.rearrange("o (t p) d -> p (o t) d", p=P)).then_inc(ld_x, 16)
            for s in range(RING):
                sp.dma_start(ring[:, s, :], stream[s]).then_inc(slot_ld[s], 16)
                if s == 0:
                    sp.dma_start(kst[:, :], consts).then_inc(ld_const, 16)
                    sp.dma_start(sm[:, :, :], cols.rearrange("l p n -> p l n")).then_inc(ld_cols, 16)
                    sp.dma_start(smr[:, :], rows[0]).then_inc(ld_rows, 16)
                    sp.dma_start(posi[:, :], positions.rearrange("o (t p) -> p (o t)", p=P),
                                 allow_slow_non_contiguous=True).then_inc(ld_pos, 16)
            with sp.Fori(1, LAYERS * SLOTS // RING) as i:
                for s in range(RING):
                    sp.wait_ge(slot_used, RING * i + (s - RING + 1))
                    sp.dma_start(ring[:, s, :], stream[RING * i + s]).then_inc(slot_ld[s], 16)
            for k in range(LAYERS * SLOTS // RING * RING, LAYERS * SLOTS):
                sp.wait_ge(slot_used, k - RING + 1)
                sp.dma_start(ring[:, k % RING, :], stream[k]).then_inc(slot_ld[k % RING], 16)

        @block.tensor
        def _(pe):
            def parts(L, n):
                return wh[:, buffer_of(L, n), :], wl[:, buffer_of(L, n), :]

            def half(L, n, j, i=0):
                if n in V_ALL[0:QP]:
                    pe.wait_ge((vlo_ok, vlo2_ok)[j], L * (2 * PAIRS - QP, QP)[j] + V_ALL.index(n) + 4 * i + 1)
                elif n in V_ALL:
                    pe.wait_ge(vlo_ok, L * (2 * PAIRS - QP) + 2 * (V_ALL.index(n) + V_STEP[n] * i) - QP + j + 1)
                else:
                    pe.wait_ge(lo_ok, 2 * (L * len(REST) + REST.index(n) + U_STEP[n] * i) + j + 1)

            def product(o, a, b, start, stop, **kw):
                pe.matmul(o, a[0], b[0], start=start, stop=False, **kw)
                pe.matmul(o, a[0], b[1], start=False, stop=False, **kw)
                return pe.matmul(o, a[1], b[0], start=False, stop=stop, **kw)

            def slot(L, n):
                n += L * SLOTS
                pe.wait_ge(slot_ld[n % RING], 16 * (n // RING + 1))
                return ring[:, n % RING, :]

            def keep_clock(n, b):
                for _ in range(n):
                    pe.matmul(bank(b, 512), zeros, finite, start=True, stop=True)

            def transposes(L, j):
                n = 3 * L + j
                if j == 1:
                    keep_clock(24, 0)
                elif j == 0 and L:
                    pe.wait_ge(sg_ok, N_PLEG * (L - 1) + 1)
                    keep_clock(24, 0)
                pe.wait_ge(xn_ok, n + 1)
                for b in range(DC // 2):
                    for c in range(2):
                        for t in range(T):
                            k = 2 * b + c
                            ins = pe.transpose(bank(b, P, at=c * SEQ + t * P), xn[:, t, k * P:(k + 1) * P], ident)
                    ins.then_inc(xt_ps, 1)

            def token_major(b, L, s):
                n = CHUNK
                w = parts(L, s)
                wv = [a[:, 0:DC * n].rearrange("p (k n) -> p k n", k=DC) for a in w]
                for t in range(T):
                    for k in range(DC):
                        if t == 0 and k % (DC // 2) == 0:
                            half(L, s, 2 * k // DC)
                        ins = product(bank(b, n, at=t * CHUNK), [a[:, k, t * P:(t + 1) * P] for a in (xh, xl)],
                                      [a[:, k, :] for a in wv], k == 0, k == DC - 1)
                return ins

            def rows_of(u):
                if u < U_SLC:
                    v = C_FV + u * HD
                    return fT[0:HD + 2, 0, u, :], fT[0:HD + 2, 1, u, :], v
                if u < U_DIFF:
                    kind, j = (u - U_SLC) // NSA_H, (u - U_SLC) % NSA_H
                    r = slice(HD * (j % 2), HD * (j % 2) + HD)
                    return qrT[r, j // 2, :], kswT[r, kind, :], (C_VS, C_VW)[kind] + (j % 2) * HD
                c = u - U_DIFF
                r = slice(DQK * (c % 4), DQK * (c % 4) + DQK)
                return dqT[r, c // 4, :], dkT[r, c // 4, :], C_DV + (c // 2) * HD

            pe.wait_ge(ld_const, 16)
            pe.wait_ge(ld_cols, 16)
            for L in range(LAYERS):
                transposes(L, 0)
                keep_clock(12, 4)
                pe.wait_ge(xt_ok, 4 * (4 * L) + 4)
                for i in range(N_IN):
                    if i >= 4:
                        pe.wait_ge((pj_dve, pj_act)[i % 2], L * N_IN // 2 + (i - 4) // 2 + 1)
                    if i < N_IN - 1:
                        ins = token_major(4 + i % 4, L, S_IN + i)
                    else:
                        half(L, S_IN + i, 0)
                        half(L, S_IN + i, 1)
                        w = [a[:, 0:DC * REM].rearrange("p (k n) -> p k n", k=DC) for a in parts(L, S_IN + i)]
                        for k in range(DC):
                            ins = product(bank(7, SEQ, parts=REM), [a[:, k, :] for a in w], [xh[:, k, :], xl[:, k, :]],
                                          k == 0, k == DC - 1)
                    ins.then_inc(slot_used, 1)
                pe.wait_ge(rem_ok, L + 1)
                for t in range(T):
                    ins = pe.transpose(bank(7, REM, at=SEQ + t * REM), rem[0:REM, t * P:(t + 1) * P], ident[0:REM, 0:REM])
                ins.then_inc(rem_ps, 1)
                NQ0 = [C_NQ + i * P for i in range(4)]
                batches = [[proj[:, t, c:c + P] for c in (C_KC, C_VC) for t in range(T)]]
                batches += [[proj[:, t, c:c + P] for c in NQ0] for t in range(T)]
                batches += [[rope[:, t, c - C_NQ:c - C_NQ + P] for c in (C_KS, C_KW) for t in range(T)]]
                batches += [[rope[:, t, c - C_NQ:c - C_NQ + P] for c in NQ0] for t in range(T)]
                batches += [[fa[:, t, s, i, :] for i in range(FOX_H)] for s in range(2) for t in range(T)]
                batches += [[rope[:, t, c - C_NQ + b * P:c - C_NQ + (b + 1) * P] for b in range(2) for t in range(T)]
                            for c in (C_DQ, C_DK)]
                for n, batch in enumerate(batches):
                    if n == 0:
                        pe.wait_ge(pj_act, N_IN // 2 * L + 4)
                    elif n == 1:
                        pe.wait_ge(nrm_ok, L + 1)
                    elif n == 3:
                        pe.wait_ge(ff_ls, L + 1)
                        tri, one = kst[:, K_TRI:K_TRI + P], kst[:, K_ONE:K_ONE + P]
                        pe.matmul(bank(4, FOX_H), tri, fl[:, 5, 0, :], start=True, stop=True)
                        pe.matmul(bank(4, FOX_H, at=FOX_H), one, fl[:, 5, 0, :], start=True, stop=False)
                        pe.matmul(bank(4, FOX_H, at=FOX_H), tri, fl[:, 5, 1, :], start=False, stop=True).then_inc(ff_ps, 1)
                        pe.wait_ge(tok_ok, L + 1)
                    if n >= 4:
                        pe.wait_ge((tb_act, tb_dve)[n % 2], 6 * L + (n - 4) // 2 + 1)
                    if n == 10:
                        pe.wait_ge(rot_step, 5 * T * (L + 1))
                    for i, src in enumerate(batch):
                        rows = src.shape[1]
                        ins = pe.transpose(bank(n % 4, P, parts=rows, at=i * P), src, ident)
                    ins.then_inc(tb_ps, 1)
                pe.wait_ge(x_ok, L + 1)
                for kv in range(2):
                    w = slot(L, S_CMP + kv)
                    for g in range(2):
                        r = slice(HD * g, HD * g + HD)
                        for l in range(CMP_LEN):
                            ins = pe.matmul(bank(4 + g, HD, parts=NCP, at=kv * HD), X[r, kv, l, :],
                                            w[r, l * HD:(l + 1) * HD], start=(l == 0), stop=(l == CMP_LEN - 1))
                    ins.then_inc(slot_used, 1)
                keep_clock(12, 6)
                pe.wait_ge(kc_tok, L + 1)
                pe.transpose(bank(4, NCP, at=256), ar(A_KCX, 2 * HD, parts=NCP), ident[0:NCP, 0:NCP])
                pe.matmul(bank(5, 2 * HD, at=256), kst[0:NCP, K_REP:K_REP + P], vcx[0:NCP, :], start=True, stop=True).then_inc(kc_ps, 1)
                keep_clock(5, 6)
                pe.wait_ge(kcT_ok, L + 1)
                pe.wait_ge(tb_act, 6 * L + 6)
                pe.wait_ge(tb_dve, 6 * L + 6)
                for g in range(2):
                    r = slice(HD * g, HD * g + HD)
                    for t in range(T):
                        for j in range(4):
                            ins = pe.matmul(bank(4 + g, NCP, at=(4 * t + j) * NCP), qnT[r, j, t * P:(t + 1) * P],
                                            kcT[r, :], start=True, stop=True)
                ins.then_inc(cs_ps, 1)
                keep_clock(16, 6)
                for s in range(UNITS + 3):
                    if s < UNITS:
                        q, k, _ = rows_of(s)
                        if s >= 4:
                            pe.wait_ge(neg_ok, UNITS * L + s - 3)
                        pe.matmul(bank(s % 4, P), q[:, 0:P], k[:, 0:P], start=True, stop=True)
                        pe.matmul(bank(s % 4, SEQ, at=P), q[:, P:SEQ], k, start=True, stop=True).then_inc(s_ps, 1)
                    if s == 1:
                        pe.wait_ge(ce_ok, L + 1)
                        for t in range(T):
                            ins = pe.transpose(bank(4, P, at=t * P), pc[:, t, :, :].rearrange("p j n -> p (j n)"), ident)
                        ins.then_inc(pcT_ps, 1)
                        pe.wait_ge(pcT_ok, L + 1)
                        for t in range(T):
                            ins = pe.matmul(bank(6 + t, 512), pcT[:, t, :], vbd.rearrange("p j d -> p (j d)"),
                                            start=True, stop=True)
                        ins.then_inc(oc_ps, 1)
                    u = s - 2
                    if 0 <= u < UNITS:
                        pe.wait_ge(p_ok, UNITS * L + u + 1)
                        if u >= 2:
                            pe.wait_ge(pt_ok, UNITS * L + u - 1)
                        for i in range(3):
                            ins = pe.transpose(bank(4 + u % 2, P, at=i * P), Pb[:, u % 4, i * P:(i + 1) * P], ident)
                        ins.then_inc(pt_ps, 1)
                    u = s - 3
                    if 0 <= u < UNITS:
                        _, _, v = rows_of(u)
                        if u == 0:
                            pe.wait_ge(oc_ok, L + 1)
                        if u % 4 == 0 and u >= 8:
                            pe.wait_ge(o_ok, 7 * L + u // 4 - 1)
                        pe.wait_ge(pt_ok, UNITS * L + u + 1)
                        o = [bank(6 + u // 4 % 2, HD, at=(u % 4) * P + t * HD) for t in range(T)]
                        PT = PTb[:, u % 3, :]
                        pe.matmul(o[0], PT[:, 0:P], proj[:, 0, v:v + HD], start=True, stop=True)
                        pe.matmul(o[1], PT[:, P:2 * P], proj[:, 0, v:v + HD], start=True, stop=False)
                        pe.matmul(o[1], PT[:, 2 * P:3 * P], proj[:, 1, v:v + HD], start=False, stop=True).then_inc(pv_ps, 1)
                keep_clock(24, 0)
                pe.wait_ge(mix_ok, L + 1)
                pe.wait_ge(nsa_step, NSA_STEPS * (L + 1))
                for b in range(4):
                    for c in range(2):
                        for t in range(T):
                            k = 2 * b + c
                            ins = pe.transpose(bank(b, P, at=c * SEQ + t * P), mix[:, t, k * P:(k + 1) * P], ident)
                    ins.then_inc(xt_ps, 1)
                keep_clock(16, 4)
                pe.wait_ge(xt_ok, 4 * (4 * L + 1) + 4)
                for i in range(N_OUT):
                    ins = token_major(4 + i, L, S_OUT + i)
                    ins.then_inc(slot_used, 1)
                transposes(L, 1)
                keep_clock(12, 4)
                pe.wait_ge(xt_ok, 4 * (4 * L + 2) + 4)
                def scores(g):
                    pe.wait_ge(q_ok, N_Q * L + 2 * g + 2)
                    for t in range(T):
                        n = 2 * g + t
                        if n >= 4:
                            pe.wait_ge(sc_ok, 8 * L + n - 3)
                        for j in range(4):
                            m = 4 * g + j
                            ins = pe.matmul(bank(4 + n % 4, P, at=j * P), pqT[:, m, t * P:(t + 1) * P], subkeys[:, m, :],
                                            start=True, stop=True)
                        ins.then_inc(sc_ps, 1)

                subkeys = ar(A_KEYS, HC, NKEYS)
                pe.wait_ge(ld_keys, 16 * (L + 1))
                for i in range(N_Q):
                    w = [a.rearrange("p (k n) -> p k n", k=DC) for a in parts(L, S_Q + i)]
                    if i >= 4:
                        pe.wait_ge(q_ok, N_Q * L + i - 3)
                    for c in range(2):
                        for k in range(DC):
                            if c == 0 and k % (DC // 2) == 0:
                                half(L, S_Q + i, 2 * k // DC)
                            ins = product(bank(i % 4, SEQ, at=c * SEQ), [a[:, k, c * P:(c + 1) * P] for a in w],
                                          [xh[:, k, :], xl[:, k, :]], k == 0, k == DC - 1)
                    ins.then_inc(slot_used, 1)
                    if i >= 2 and i % 2 == 0:
                        scores(i // 2 - 1)
                def spread(n, par, early=None):
                    pe.wait_ge(b_ok, n + 1)
                    pe.wait_ge(a_ok, n + 1)
                    if early is not None:
                        pe.wait_ge(a3_ok, L * NB + early + 1)
                    if early is None or early >= 2:
                        pe.wait_ge(g_ok, n - 1)
                    for i in range(TB):
                        for k in range(3):
                            ins = pe.matmul(bank(6 + par, QI, at=i * QI), Bh[:, par, i, :], Ah[:, par, k, i, :],
                                            start=(k == 0), stop=(k == 2))
                    ins.then_inc(g_ps, 1)

                def hidden(i, p, step=2):
                    w = [a.rearrange("p (e k n) -> p e k n", e=2, k=DC) for a in parts(L, u_slot(p))]
                    if p + L > 1 or not isinstance(i, int):
                        pe.wait_ge(gelu_ok, L * PAIRS + step * i + p - 1)
                    for e in range(2):
                        half(L, u_slot(p), e, i)
                        for k in range(DC):
                            ins = product(bank(4 + p % 2, SEQ, at=e * SEQ), [a[:, e, k, :] for a in w],
                                          [xh[:, k, :], xl[:, k, :]], k == 0, k == DC - 1)
                    ins.then_inc(slot_used, 1)

                def weighted(i, p, step=2):
                    w = [a.rearrange("p (e n) -> p e n", e=2) for a in parts(L, v_slot(p))]
                    pe.wait_ge(w_ok, L * PAIRS + step * i + p + 1)
                    for e in range(2):
                        half(L, v_slot(p), e, i)
                        for t in range(T):
                            for c in range(2):
                                ins = product(bank(2 * t + c, 512), [a[:, e, t * P:(t + 1) * P] for a in (Wh[:, p % 2], Wl[:, p % 2])],
                                              [a[:, e, c * 512:(c + 1) * 512] for a in w], False, False,
                                              skip_group_check=True)
                    ins.then_inc(slot_used, 1)

                q0 = L * NB * QUARTERS
                pe.wait_ge(sc_ok, 8 * L + 6)
                hidden(0, 0, 4)
                scores(3)
                for k in range(1, 4):
                    hidden(0, k, 4)
                with pe.Fori(1, QP // 4 - 1) as i:
                    for k in range(4):
                        hidden(i, k, 4)
                hidden(0, QP - 4)
                for b in range(4):
                    pe.matmul(bank(b, 512), zeros, finite, start=True, stop=False, skip_group_check=True)
                pe.wait_ge(rout_ok, L + 1)
                pe.wait_ge(sc_ok, 8 * L + 8)
                for k in range(3):
                    for t in range(T):
                        ins = pe.transpose(bank(6 + k // 2, P, at=(k % 2) * SEQ + t * P), rout[:, k, t, :], ident)
                ins.then_inc(rout_ps, 1)
                hidden(0, QP - 3)
                pe.wait_ge(rout_dve, L + 1)
                for n in range(NB):
                    spread(q0 + n, n % 2, n)
                    if n in (1, 3, 5):
                        hidden(0, QP - 2 + n // 2)
                with pe.Fori(0, QP // 4) as i:
                    for k in range(4):
                        weighted(i, k, 4)
                        spread(q0 + NB + 4 * i + k, k % 2)
                for quarter in range(1, QUARTERS):
                    with pe.Fori(0, QP // 2 - (quarter == QUARTERS - 1)) as i:
                        for k in range(2):
                            p = quarter * QP + k
                            hidden(i, p + 1)
                            weighted(i, p)
                            if quarter < QUARTERS - 1:
                                spread(q0 + (quarter + 1) * NB + 2 * i + k, k)
                hidden(0, PAIRS - 1)
                weighted(0, PAIRS - 2)
                weighted(0, PAIRS - 1)
                for b in range(4):
                    ins = pe.matmul(bank(b, 512), zeros, finite, start=False, stop=True, skip_group_check=True)
                ins.then_inc(acc_ps, 1)
                w = [a.rearrange("p (c n) -> p c n", c=2) for a in parts(L, S_PLEP)]
                pe.wait_ge(pl_ok, L + 1)
                pe.wait_ge(gelu_ok, PAIRS * (L + 1))
                half(L, S_PLEP, 0)
                half(L, S_PLEP, 1)
                for i in range(N_PLEG):
                    for t in range(T):
                        for c in range(2):
                            ins = product(bank(4 + i, CHUNK, at=t * CHUNK), [a[:, c, t * P:(t + 1) * P] for a in (ph, pl)],
                                          [a[:, c, i * CHUNK:(i + 1) * CHUNK] for a in w], c == 0, c == 1)
                ins.then_inc(slot_used, 1)
                transposes(L, 2)
                pe.wait_ge(xt_ok, 4 * (4 * L + 3) + 4)
                for i in range(N_PLEG):
                    ins = token_major(i, L, S_PLEG + i)
                    ins.then_inc(slot_used, 1)

        @block.scalar
        def _(act):
            def square_rows(L, j):
                n = 3 * L + j
                if n:
                    act.wait_ge(h_ok, n)
                else:
                    act.wait_ge(ld_x, 16)
                for t in range(T):
                    if n or t:
                        act.wait_ge(ss_ok, 2 * n + t)
                    act.activation(ar(A_XSQ, D), h[:, t, :], ACT.Square, accum_out=ss[:, t:t + 1]).then_inc(ss_ok, 1)
                act.wait_ge(ms_ok, n + 1)
                act.activation(rstd[:, 1, :], rstd[:, 0, :], ACT.Sqrt).then_inc(rt_ok, 1)

            act.wait_ge(ang_ok, 1)
            act.activation(sin[:, :, :], ang[:, :, :], ACT.Sin)
            act.activation(cos[:, :, :], ang[:, :, :], ACT.Sin, scale=0.5).then_inc(sin_ok, 1)
            act.wait_ge(lam_in, 1)
            act.activation(lame[:, :, :], lams[:, :, :], ACT.Exp).then_inc(lam_exp, 1)

            def first_parts(n):
                for b in range(4):
                    act.wait_ge(xf_ok, 4 * n + b + 1)
                    src = ar(A_MIXT, DC, SEQ) if n % 4 == 1 else xf
                    act.activation(xh[:, 2 * b:2 * b + 2, :], src[:, 2 * b:2 * b + 2, :], ACT.Copy).then_inc(xh_ok, 1)

            for L in range(LAYERS):
                high(L, S_IN)
                high(L, S_IN + 1)
                square_rows(L, 0)
                first_parts(4 * L)
                high(L, S_IN + 2)
                for i in range(1, N_IN, 2):
                    if i == 7:
                        act.wait_ge(pj_dve, N_IN // 2 * L + 4)
                        act.wait_ge(pj_act, N_IN // 2 * L + 3)
                        for t in range(T):
                            act.activation(ar(A_SQ, T, C_KC)[:, t, :], proj[:, t, 0:C_KC], ACT.Square).then_inc(psq_ok, 1)
                    for n in (i + 2, i + 3):
                        if n < N_IN:
                            high(L, S_IN + n)
                        if n == i + 2:
                            used(act, L, S_IN + i)
                            c = min(CHUNK, PW - i * CHUNK)
                            if i < N_IN - 1:
                                src = bank(4 + i % 4, T, CHUNK)
                            else:
                                act.activation(rem[0:REM, :], bank(7, SEQ, parts=REM), ACT.Copy).then_inc(rem_ok, 1)
                                act.wait_ge(rem_ps, L + 1)
                                src = bank(7, T, REM, at=SEQ)
                            act.activation(proj[:, :, i * CHUNK:i * CHUNK + c], src, ACT.Copy).then_inc(pj_act, 1)
                    if i == 7:
                        act.wait_ge(gms_ok, L + 1)
                        act.activation(gss[:, 1, :, :], gss[:, 0, :, :], ACT.Sqrt).then_inc(grt_ok, 1)
                act.wait_ge(ff_in, L + 1)
                act.activation(fl[:, 3, :, :], fl[:, 2, :, :], ACT.Exp).then_inc(act_step, 1)
                act.wait_ge(act_step, L + 1)
                act.activation(fl[:, 4, :, :], fl[:, 3, :, :], ACT.Ln, bias=1.0).then_inc(ff_ln, 1)
                act.wait_ge(pj_dve, N_IN // 2 * (L + 1))
                act.wait_ge(pj_act, N_IN // 2 * (L + 1))
                act.activation(gate[:, :, :, :].rearrange("p t k j -> p t (k j)"), proj[:, :, C_NG:PW],
                               ACT.Sigmoid).then_inc(gate_ok, 1)
                for n in range(0, 12, 2):
                    act.wait_ge(tb_ps, 12 * L + n + 1)
                    if n == 0:
                        dst_ = kcvT.rearrange("p k t -> p (k t)")
                    elif n in (2, 4):
                        dst_ = (qnT, qrT)[n // 4][:, :, (1 if n == 2 else 0) * P:][:, :, 0:P]
                    elif n in (6, 8):
                        dst_ = fT[0:HD + 2, n // 2 - 3, :, 0:P]
                    else:
                        dst_ = dqT.rearrange("p k t -> p (k t)")
                    height = HD + 2 if n in (6, 8) else P
                    src = bank(n % 4, 4, P, parts=height) if n in (2, 4, 6, 8) else bank(n % 4, 512)
                    act.activation(dst_, src, ACT.Copy).then_inc(tb_act, 1)
                high(L, S_OUT)
                high(L, S_OUT + 1)
                act.wait_ge(kc_ms, L + 1)
                act.activation(kst4[0:NCP, 2, :], kst4[0:NCP, 1, :], ACT.Sqrt).then_inc(kc_rt, 1)
                act.wait_ge(cs_ok, L + 1)
                act.activation(pc[:, :, :, :], pc[:, :, :, :], ACT.Exp, scale=HD ** -0.5).then_inc(ce_ok, 1)
                act.wait_ge(pcT_ps, L + 1)
                act.activation(pcT[:, :, :], bank(4, T, P), ACT.Copy).then_inc(pcT_ok, 1)
                act.wait_ge(oc_ps, L + 1)
                act.activation(Oc.rearrange("p t j d -> p t (j d)"), psum[:, 6:8, :], ACT.Copy).then_inc(oc_ok, 1)
                for u in range(UNITS + 4):
                    if u < UNITS:
                        act.wait_ge(neg_ok, UNITS * L + u + 1)
                        Pu = Pb[:, u % 4, :]
                        act.activation(Pu[:, 0:P], Pu[:, 0:P], ACT.Exp, bias=nmax[:, u, 0:1], scale=-1.0,
                                       accum_out=den[:, u, 0:1])
                        act.activation(Pu[:, P:384], Pu[:, P:384], ACT.Exp, bias=nmax[:, u, 1:2], scale=-1.0,
                                       accum_out=den[:, u, 1:2]).then_inc(p_ok, 1)
                    if u >= 7 and u % 4 == 3:
                        g = (u - 7) // 4
                        act.wait_ge(pv_ps, UNITS * L + 4 * g + 4)
                        act.activation(O[:, 4 * g:4 * g + 4, :, :].rearrange("p u t d -> p (u t d)"),
                                       bank(6 + g % 2, 512), ACT.Copy).then_inc(o_ok, 1)
                act.wait_ge(dms_ok, L + 1)
                act.activation(dst[:, 1, :, :], dst[:, 0, :, :], ACT.Sqrt).then_inc(drt_ok, 1)
                act.wait_ge(mix_ok, L + 1)
                if L < LAYERS - 1:
                    act.dma_start(smr[:, :], rows[L + 1]).then_inc(ld_rows, 16)
                act.dma_start(ar(A_KEYS, SLOT), keys[L]).then_inc(ld_keys, 16)
                first_parts(4 * L + 1)
                high(L, S_OUT + 2)
                high(L, S_OUT + 3)
                high(L, S_Q)
                high(L, S_Q + 1)
                square_rows(L, 1)
                first_parts(4 * L + 2)
                def scores_out(g):
                    for t in range(T):
                        n = 2 * g + t
                        act.wait_ge(sc_ps, 8 * L + n + 1)
                        act.activation(sc[:, t, 4 * g:4 * g + 4, :], bank(4 + n % 4, 4, P), ACT.Copy).then_inc(sc_ok, 1)

                for i in range(N_Q):
                    high(L, S_Q + i + 2 if i + 2 < N_Q else u_slot(i + 2 - N_Q))
                    used(act, L, S_Q + i)
                    act.activation(pqT[:, 2 * i:2 * i + 2, :], bank(i % 4, 2, SEQ), ACT.Copy).then_inc(q_ok, 1)
                    if i >= 2 and i % 2 == 0:
                        scores_out(i // 2 - 1)

                def gelu(i, p, step=2):
                    used(act, L, u_slot(p) + 4 * i)
                    if p < QP:
                        out_ = ar(A_LEAD, QP * 512)[:, bass.ds((step * i + p) * 512, 512)]
                    else:
                        if p > QP:
                            act.wait_ge(w_ok, L * PAIRS + step * i + p - 1)
                        out_ = GL[:, p % 2, :]
                    act.activation(out_, bank(4 + p % 2, 512), ACT.Gelu).then_inc(gelu_ok, 1)

                def gates_out(quarter, i, n, step=2):
                    act.wait_ge(g_ps, (L * QUARTERS + quarter) * NB + step * i + n + 1)
                    buf = ar((quarter % 2) * SEQ * QI, SEQ * QI)
                    act.activation(buf[:, bass.ds((step * i + n) * TB * QI, TB * QI)], bank(6 + n % 2, 512),
                                   ACT.Copy).then_inc(g_ok, 1)

                def lead(i, ks):
                    for k in ks:
                        gelu(i, k, 4)
                        high(L, u_slot(0) + k + 2, i)

                gelu(0, 0)
                high(L, u_slot(2))
                scores_out(3)
                lead(0, range(1, 4))
                with act.Fori(1, QP // 4 - 1) as i:
                    lead(i, range(4))
                act.wait_ge(ge_in, L + 1)
                act.activation(c16, c16, ACT.Exp).then_inc(ge_ok, 1)
                lead(QP // 4 - 1, range(2))
                act.wait_ge(rout_dve, L + 1)
                for n in range(NB):
                    gates_out(0, 0, n)
                    if n in (1, 3):
                        lead(QP // 4 - 1, (2 + n // 2,))
                    elif n == 5:
                        gelu(0, QP)

                def first_quarter(i, ks):
                    for k in ks:
                        high(L, v_slot(k + 1), i)
                        gates_out(1, i, k, 4)

                with act.Fori(0, QP // 4 - 1) as i:
                    first_quarter(i, range(4))
                first_quarter(QP // 4 - 1, range(3))
                high(L, u_slot(QP + 1))
                high(L, v_slot(QP))
                gates_out(1, 0, QP - 1)
                for quarter in range(1, QUARTERS):
                    act.wait_ge(w_ok, L * PAIRS + quarter * QP)
                    with act.Fori(0, QP // 2 - (quarter == QUARTERS - 1)) as i:
                        for k in range(2):
                            p = quarter * QP + k
                            gelu(i, p + 1)
                            high(L, u_slot(p + 2), i)
                            high(L, v_slot(p + 1), i)
                            if quarter < QUARTERS - 1:
                                gates_out(quarter + 1, i, k)
                gelu(0, PAIRS - 1)
                high(L, v_slot(PAIRS - 1))
                high(L, S_PLEP)
                used(act, L, v_slot(PAIRS - 2))
                act.activation(ph, sm[:, L, M_PT:M_PT + 2 * SEQ].rearrange("p (c n) -> p c n", c=2), ACT.Copy).then_inc(ph_ok, 1)
                high(L, S_PLEG)
                square_rows(L, 2)
                first_parts(4 * L + 3)
                for i in range(N_PLEG):
                    if i + 1 < N_PLEG:
                        high(L, S_PLEG + i + 1)
                    used(act, L, S_PLEG + i)
                    act.activation(ar(i * 512, 512), bank(i, 512), ACT.Sigmoid).then_inc(sg_ok, 1)
            act.wait_ge(h_ok, 3 * LAYERS)
            act.dma_start(out.rearrange("o (t p) d -> p (o t) d", p=P), h[:, :, :]).then_inc(out_st, 16)
            act.wait_ge(out_st, 16)

        @block.gpsimd
        def _(pool):
            def low(L, n, i=0):
                for j in range(2):
                    low_half(pool, L, n, i, j, lo_ok)

            steps = [0]

            def step(ins):
                steps[0] += 1
                ins.then_inc(rot_step, 1)

            def settle():
                if steps[0]:
                    pool.wait_ge(rot_step, steps[0])

            for L in range(LAYERS):
                for n in REST:
                    if n < S_CMP:
                        low(L, n)
                pool.wait_ge(nrm_ok, L + 1)
                for t in range(T):
                    rotate(pool, t, C_DQ, ROPE32, DQK, HD // 2, A_ROT + t * (C_KC - C_DQ), step, settle)
                low(L, S_OUT)
                low(L, S_OUT + 1)
                for g in range(5):
                    pool.wait_ge(cf_ok, 5 * L + g + 1)
                    pool.wait_ge(o_ok, 7 * L + g + 1)
                    Og = O[:, 4 * g:4 * g + 4, :, :].rearrange("p u t d -> p t u d")
                    if g == 0:
                        pool.wait_ge(oc_ok, L + 1)
                        rd = rden[:, 0:4, :].rearrange("p u t -> p t u")
                        pool.tensor_tensor(heads(mix[:, :, 0:256]), Og, last(rd, HD), ALU.mult).then_inc(nsa_step, 1)
                        pool.tensor_tensor(heads(mix[:, :, 256:768]), Oc, last(cf[:, :, 0, :], HD), ALU.mult).then_inc(nsa_step, 1)
                    else:
                        k, j = 1 + (g - 1) // 2, 4 * ((g - 1) % 2)
                        tmp = ar(A_COMB + (g % 2) * 512, T, 4, HD)
                        nm = heads(mix[:, :, 256 + j * HD:512 + j * HD])
                        pool.tensor_tensor(tmp, Og, last(cf[:, :, k, j:j + 4], HD), ALU.mult).then_inc(nsa_step, 1)
                        pool.wait_ge(nsa_step, NSA_STEPS * L + 2 * g + 1)
                        pool.tensor_tensor(nm, nm, tmp, ALU.add).then_inc(nsa_step, 1)
                for n in REST:
                    if S_OUT + 1 < n < S_EXP:
                        low(L, n)
                with pool.Fori(0, QP // 4 - 1) as i:
                    for k in range(4):
                        low(L, u_slot(k), i)
                for p in range(QP - 4, QP - 1):
                    low(L, u_slot(p))
                for n in range(NB):
                    pool.wait_ge(e_ok, L * QUARTERS * NB + n + 1)
                    pool.tensor_tensor(Ah[:, n % 2, 2, :, :], Eh[:, n % 2, :, :],
                                       last(g3[:, 2, n * TB:(n + 1) * TB, 0], QI), ALU.mult).then_inc(a3_ok, 1)
                    if n in (1, 3):
                        low(L, u_slot(QP - 1 + n // 2))
                with pool.Fori(0, QP // 4) as i:
                    for k in range(4):
                        low_half(pool, L, v_slot(k), i, 1, vlo2_ok)
                low(L, u_slot(QP + 1))
                with pool.Fori(0, (PAIRS - QP) // 2 - 1) as i:
                    for k in range(2):
                        low(L, u_slot(QP + k + 2), i)
                low(L, S_PLEP)
                pool.wait_ge(ph_ok, L + 1)
                pool.tensor_tensor(pl, sm[:, L, M_PT:M_PT + 2 * SEQ].rearrange("p (c n) -> p c n", c=2), ph.bitcast(F32),
                                   ALU.subtract).then_inc(pl_ok, 1)
                for i in range(N_PLEG):
                    low(L, S_PLEG + i)

        @block.vector
        def _(dve):
            steps = [0]

            def step(ins):
                steps[0] += 1
                ins.then_inc(dve_step, 1)

            def settle():
                dve.wait_ge(dve_step, steps[0])

            def feature_major(n, weight=None):
                dst_ = xf if weight is not None else ar(A_MIXT, DC, SEQ)
                for b in range(5):
                    r = slice(2 * b, 2 * b + 2)
                    if b < 4:
                        dve.wait_ge(xt_ps, 4 * n + b + 1)
                        if weight is not None:
                            dve.tensor_tensor(dst_[:, r, :], bank(b, 2, SEQ), last(weight[:, r], SEQ), ALU.mult).then_inc(xf_ok, 1)
                        else:
                            dve.tensor_copy(dst_[:, r, :], bank(b, 2, SEQ)).then_inc(xf_ok, 1)
                    if b:
                        r = slice(2 * b - 2, 2 * b)
                        dve.wait_ge(xf_ok, 4 * n + b)
                        dve.wait_ge(xh_ok, 4 * n + b)
                        dve.tensor_tensor(xl[:, r, :], dst_[:, r, :], xh[:, r, :].bitcast(F32), ALU.subtract).then_inc(xt_ok, 1)

            def mean_rstd(L, j):
                n = 3 * L + j
                dve.wait_ge(ss_ok, 2 * n + 2)
                dve.tensor_scalar(rstd[:, 0, :], ss[:, :], 1.0 / D, EPS, ALU.mult, ALU.add).then_inc(ms_ok, 1)
                dve.wait_ge(rt_ok, n + 1)
                step(dve.reciprocal(rstd[:, 2, :], rstd[:, 1, :]))
                settle()
                for t in range(T):
                    ins = dve.tensor_scalar(xn[:, t, :], h[:, t, :], rstd[:, 2, t:t + 1], None, ALU.mult)
                ins.then_inc(xn_ok, 1)
                feature_major(4 * L + (0, 2, 3)[j], sm[:, L, M_COL + j * DC:M_COL + (j + 1) * DC])

            dve.wait_ge(ld_pos, 16)
            dve.wait_ge(ld_const, 16)
            step(dve.tensor_copy(iota[:, :, :], kst[:, K_IOTA:K_IOTA + P].rearrange("p (a b) -> p a b", b=2)))
            step(dve.tensor_copy(posf[:, :], posi[:, :]))
            settle()
            for t in range(T):
                step(dve.tensor_scalar(ang[:, t, :], kst[:, K_F64:K_F64 + NANG], posf[:, t:t + 1], None, ALU.mult))
            settle()
            step(dve.tensor_scalar(angk[:, :, :], ang[:, :, :], float(1 / TWO_PI), MAGIC, ALU.mult, ALU.add))
            settle()
            step(dve.tensor_scalar(angk[:, :, :], angk[:, :, :], -MAGIC, None, ALU.add))
            for c in PI_C:
                settle()
                step(dve.scalar_tensor_tensor(out=ang[:, :, :], in0=angk[:, :, :], scalar=-c, in1=ang[:, :, :],
                                              op0=ALU.mult, op1=ALU.add))
            settle()
            dve.tensor_scalar(ang[:, :, :], ang[:, :, :], 3.1415925, -3.1415925, ALU.min, ALU.max).then_inc(ang_ok, 1)
            dve.wait_ge(sin_ok, 1)
            step(dve.tensor_tensor(cos[:, :, :], cos[:, :, :], cos[:, :, :], ALU.mult))
            settle()
            step(dve.tensor_scalar(cos[:, :, :], cos[:, :, :], -2.0, 1.0, ALU.mult, ALU.add))
            dve.wait_ge(ld_cols, 16)
            lv = sm[:, :, M_LAM:M_LAM + 4 * DQK].rearrange("p l (a b c) -> p l a b c", a=2, b=2)
            for L in range(LAYERS):
                step(dve.tensor_tensor(lamp[:, L, :, :], lv[:, L, :, 0, :], lv[:, L, :, 1, :], ALU.mult))
            settle()
            dve.tensor_reduce(lams[:, :, :], lamp[:, :, :, :], AX, ALU.add).then_inc(lam_in, 1)
            dve.wait_ge(lam_exp, 1)
            step(dve.tensor_tensor(lam[:, :], lame[:, :, 1], lame[:, :, 0], ALU.subtract))
            settle()
            step(dve.tensor_tensor(lam[:, :], lam[:, :], kst[:, K_LI:K_LI + LAYERS], ALU.subtract))

            for L in range(LAYERS):
                mean_rstd(L, 0)
                def projected(chunks):
                    for i in chunks:
                        used(dve, L, S_IN + i)
                        n = min(CHUNK, PW - i * CHUNK)
                        dve.tensor_copy(proj[:, :, i * CHUNK:i * CHUNK + n], bank(4 + i % 4, T, CHUNK)[:, :, 0:n]).then_inc(pj_dve, 1)

                projected(range(0, 8, 2))
                dve.wait_ge(psq_ok, T * (L + 1))
                sq = ar(A_SQ, T, C_KC)
                for t in range(T):
                    step(dve.tensor_reduce(gss[:, 0, t, 0:G64], sq[:, t, 0:C_DQ].rearrange("p (g d) -> p g d", d=HD), AX, ALU.add))
                    step(dve.tensor_reduce(gss[:, 0, t, G64:NG], sq[:, t, C_DQ:C_KC].rearrange("p (g d) -> p g d", d=DQK), AX, ALU.add))
                settle()
                dve.tensor_scalar(gss[:, 0, :, 0:G64], gss[:, 0, :, 0:G64], 1.0 / HD, EPS, ALU.mult, ALU.add)
                dve.tensor_scalar(gss[:, 0, :, G64:NG], gss[:, 0, :, G64:NG], 1.0 / DQK, EPS, ALU.mult, ALU.add).then_inc(gms_ok, 1)
                dve.wait_ge(grt_ok, L + 1)
                step(dve.reciprocal(gss[:, 2, :, :], gss[:, 1, :, :]))
                for t in range(T):
                    a = proj[:, t, 0:C_DQ].rearrange("p (g d) -> p g d", d=HD)
                    b = proj[:, t, C_DQ:C_KC].rearrange("p (g d) -> p g d", d=DQK)
                    settle()
                    step(dve.tensor_tensor(a, a, last(gss[:, 2, t, 0:G64], HD), ALU.mult))
                    step(dve.tensor_tensor(b, b, last(gss[:, 2, t, G64:NG], DQK), ALU.mult))
                settle()
                dve.wait_ge(ld_rows, 16 * (L + 1))
                for t in range(T):
                    ins = dve.tensor_tensor(proj[:, t, 0:C_KC], proj[:, t, 0:C_KC], smr[:, 0:C_KC], ALU.mult)
                ins.then_inc(nrm_ok, 1)
                dve.wait_ge(nrm_ok, L + 1)
                rotate(dve, 0, C_NQ, ROPE64, HD, 0, A_TMP, step, settle)
                projected(range(8, N_IN, 2))
                dve.wait_ge(pj_act, N_IN // 2 * (L + 1))
                dve.wait_ge(pj_dve, N_IN // 2 * (L + 1))
                step(dve.tensor_tensor(fl[:, 0, :, :], proj[:, :, C_FF:C_FF + FOX_H], mid(smr[:, M_FB:M_FB + FOX_H], 1, T), ALU.add))
                settle()
                step(dve.tensor_scalar(fl[:, 1, :, :], fl[:, 0, :, :], 0.0, None, ALU.min))
                step(dve.tensor_scalar(fl[:, 2, :, :], fl[:, 0, :, :], -1.0, None, ALU.mult))
                settle()
                dve.tensor_tensor(fl[:, 2, :, :], fl[:, 2, :, :], fl[:, 0, :, :], ALU.min).then_inc(ff_in, 1)
                rotate(dve, 1, C_NQ, ROPE64, HD, 0, A_TMP, step, settle)
                dve.wait_ge(ff_ln, L + 1)
                dve.tensor_tensor(fl[:, 5, :, :], fl[:, 1, :, :], fl[:, 4, :, :], ALU.subtract).then_inc(ff_ls, 1)
                for t in range(T):
                    for s in range(2):
                        dve.tensor_copy(fa[:, t, s, :, 0:HD], proj[:, t, s * 256:(s + 1) * 256].rearrange("p (g d) -> p g d", d=HD))
                        dve.memset(fa[:, t, s, :, HD + 1 - s:HD + 2 - s], 1.0)
                dve.wait_ge(ff_ps, L + 1)
                cps = bank(4, T, FOX_H)
                root = float(HD ** 0.5)
                for t in range(T):
                    dve.tensor_scalar(fa[:, t, 0, :, HD], cps[:, t, :], root, None, ALU.mult)
                    ins = dve.tensor_scalar(fa[:, t, 1, :, HD + 1], cps[:, t, :], -root, None, ALU.mult)
                step(ins)
                settle()
                dve.memset(X[:, :, :, NCMP:NCP], 0.0).then_inc(tok_ok, 1)
                for n in range(1, 12, 2):
                    dve.wait_ge(tb_ps, 12 * L + n + 1)
                    if n == 1:
                        dve.wait_ge(tb_act, 6 * L + 1)
                        pos = sm[:, L, M_POS:M_POS + 2 * CMP_LEN].rearrange("p (k l) -> p k l", k=2)
                        for kv in range(2):
                            for s in range(2):
                                win = kcvT[:, kv, s * 16:s * 16 + NCMP * 16].rearrange("p (n l) -> p l n", l=16)
                                ins = dve.tensor_tensor(X[:, kv, s * 16:s * 16 + 16, 0:NCMP], win,
                                                        last(pos[:, kv, s * 16:s * 16 + 16], NCMP), ALU.add)
                        ins.then_inc(x_ok, 1)
                    if n in (1, 5):
                        dst_ = (qnT, qrT)[n // 4][:, :, (0 if n == 1 else 1) * P:][:, :, 0:P]
                    elif n in (7, 9):
                        dst_ = fT[0:HD + 2, n // 2 - 3, :, P:SEQ]
                    elif n == 3:
                        dst_ = kswT.rearrange("p k t -> p (k t)")
                    else:
                        dst_ = dkT.rearrange("p k t -> p (k t)")
                    height = HD + 2 if n in (7, 9) else P
                    src = bank(n % 4, 4, P, parts=height) if n in (1, 5, 7, 9) else bank(n % 4, 512)
                    dve.tensor_copy(dst_, src).then_inc(tb_dve, 1)
                used(dve, L, S_CMP + 1)
                kcx = ar(A_KCX, 2, HD, parts=NCP)
                kcs = ar(A_KCS, 2, HD, parts=NCP)
                for g in range(2):
                    step(dve.tensor_copy(kcx[:, g, :], bank(4 + g, HD, parts=NCP)))
                    dve.tensor_copy(vcx[0:NCP, g * HD:(g + 1) * HD], bank(4 + g, HD, parts=NCP, at=HD))
                settle()
                step(dve.tensor_tensor(kcs, kcx, kcx, ALU.mult))
                settle()
                step(dve.tensor_reduce(kst4[0:NCP, 0, :], kcs, AX, ALU.add))
                settle()
                dve.tensor_scalar(kst4[0:NCP, 1, :], kst4[0:NCP, 0, :], 1.0 / HD, EPS, ALU.mult, ALU.add).then_inc(kc_ms, 1)
                dve.wait_ge(kc_rt, L + 1)
                step(dve.reciprocal(kst4[0:NCP, 3, :], kst4[0:NCP, 2, :]))
                settle()
                step(dve.tensor_tensor(kcx, kcx, last(kst4[0:NCP, 3, :], HD), ALU.mult))
                settle()
                dve.tensor_tensor(kcx, kcx, smr[0:NCP, M_KN:M_KN + 2 * HD].rearrange("p (g d) -> p g d", g=2), ALU.mult).then_inc(kc_tok, 1)
                dve.wait_ge(kc_ps, L + 1)
                vb = vbd.rearrange("p (j g) d -> p j g d", g=2)
                blk = kst[:, K_BLK:K_BLK + NSA_H].rearrange("p (j g) -> p j g", g=2)
                for g in range(2):
                    dve.tensor_tensor(vb[:, :, g, :], mid(bank(5, HD, at=256 + g * HD), 1, 4), last(blk[:, :, g], HD), ALU.mult)
                dve.tensor_copy(kcT[:, :], bank(4, NCP, at=256)).then_inc(kcT_ok, 1)
                dve.wait_ge(cs_ps, L + 1)
                pv = pc[:, :, :, :].rearrange("p t (j g) n -> p t j g n", g=2)
                for g in range(2):
                    for t in range(T):
                        step(dve.tensor_tensor(pv[:, t, :, g, :], bank(4 + g, 4, NCP, at=t * 4 * NCP),
                                               mid(kst[:, K_CM + t * NCP:K_CM + (t + 1) * NCP], 1, 4), ALU.add))
                settle()
                step(dve.tensor_reduce(cst[:, 0, :, :], pc[:, :, :, :], AX, ALU.max))
                settle()
                dve.tensor_tensor(pc[:, :, :, :], pc[:, :, :, :], last(cst[:, 0, :, :], NCP), ALU.subtract).then_inc(cs_ok, 1)
                def combine(g):
                    dve.wait_ge(p_ok, UNITS * L + 4 * g + 4)
                    us = slice(4 * g, 4 * g + 4)
                    if g < 5:
                        rd = rden[:, us, :].rearrange("p u t -> p t u")
                        step(dve.reciprocal(rden[:, us, :], den[:, us, :]))
                        if g == 0:
                            dve.wait_ge(gate_ok, L + 1)
                            step(dve.reciprocal(cst[:, 2, :, :], cst[:, 1, :, :]))
                            settle()
                            step(dve.tensor_tensor(cst[:, 2, :, :], cst[:, 2, :, :], last(kst[:, K_CV:K_CV + T], NSA_H), ALU.mult))
                            settle()
                            dve.tensor_tensor(cf[:, :, 0, :], gate[:, :, 0, :], cst[:, 2, :, :], ALU.mult).then_inc(cf_ok, 1)
                        else:
                            settle()
                            k, j = 1 + (g - 1) // 2, 4 * ((g - 1) % 2)
                            dve.tensor_tensor(cf[:, :, k, j:j + 4], gate[:, :, k, j:j + 4], rd, ALU.mult).then_inc(cf_ok, 1)
                    else:
                        dve.wait_ge(o_ok, 7 * L + g + 1)
                        step(dve.reciprocal(rden[:, us, :], den[:, us, :]))
                        rr = rden[:, us, :].rearrange("p (h c) t -> p h c t", c=2)
                        settle()
                        step(dve.tensor_scalar(rr[:, :, 1, :], rr[:, :, 1, :], lam[:, L:L + 1], None, ALU.mult))
                        settle()
                        j = 2 * (g - 5)
                        dm = heads(mix[:, :, 768 + j * HD:896 + j * HD])
                        od = O[:, us, :, :].rearrange("p (h c) t d -> p h c t d", c=2)
                        tm = ar(A_TMP, T, 2, HD)
                        for c, o in ((0, dm), (1, tm)):
                            step(dve.tensor_tensor(o, od[:, :, c, :, :].rearrange("p h t d -> p t h d"),
                                                   last(rr[:, :, c, :].rearrange("p h t -> p t h"), HD), ALU.mult))
                        settle()
                        step(dve.tensor_tensor(dm, dm, tm, ALU.add))
                        settle()
                        step(dve.tensor_tensor(tm, dm, dm, ALU.mult))
                        settle()
                        step(dve.tensor_reduce(dst[:, 0, :, j:j + 2], tm, AX, ALU.add))

                for s in range(UNITS + 3):
                    u = s
                    if u < UNITS:
                        dve.wait_ge(s_ps, UNITS * L + u + 1)
                        if u >= 4:
                            dve.wait_ge(pt_ps, UNITS * L + u - 3)
                        scale = (DQK if u >= U_DIFF else HD) ** -0.5
                        mask = kst[:, K_MASK:K_MASK + SEQ]
                        Pu = Pb[:, u % 4, :]
                        dve.tensor_tensor_reduce(Pu[:, 0:P], bank(u % 4, P), mask[:, P:SEQ], -scale, 3e38, ALU.add, ALU.min,
                                                 nmax[:, u, 0:1])
                        dve.tensor_tensor_reduce(Pu[:, P:384], bank(u % 4, SEQ, at=P), mask, -scale, 3e38, ALU.add, ALU.min,
                                                 nmax[:, u, 1:2]).then_inc(neg_ok, 1)
                    if u == 1:
                        dve.wait_ge(ce_ok, L + 1)
                        step(dve.tensor_reduce(cst[:, 1, :, :], pc[:, :, :, :], AX, ALU.add))
                    u = s - 2
                    if 0 <= u < UNITS:
                        dve.wait_ge(pt_ps, UNITS * L + u + 1)
                        if u >= 3:
                            dve.wait_ge(pv_ps, UNITS * L + u - 2)
                        dve.tensor_copy(PTb[:, u % 3, :], bank(4 + u % 2, 384)).then_inc(pt_ok, 1)
                    if s >= 9 and s % 4 == 1:
                        combine((s - 9) // 4)
                combine(UNITS // 4 - 1)
                settle()
                dve.tensor_scalar(dst[:, 0, :, :], dst[:, 0, :, :], 1.0 / HD, EPS, ALU.mult, ALU.add).then_inc(dms_ok, 1)
                dve.wait_ge(drt_ok, L + 1)
                step(dve.reciprocal(dst[:, 2, :, :], dst[:, 1, :, :]))
                settle()
                step(dve.tensor_scalar(dst[:, 2, :, :], dst[:, 2, :, :], kst[:, K_LI + LAYERS + L:K_LI + LAYERS + L + 1], None, ALU.mult))
                settle()
                dm = heads(mix[:, :, 768:D])
                step(dve.tensor_tensor(dm, dm, last(dst[:, 2, :, :], HD), ALU.mult))
                settle()
                for t in range(T):
                    ins = dve.tensor_tensor(mix[:, t, 768:D], mix[:, t, 768:D], smr[:, M_SUB:M_SUB + 256], ALU.mult)
                ins.then_inc(mix_ok, 1)
                feature_major(4 * L + 1)
                for i in range(N_OUT):
                    used(dve, L, S_OUT + i)
                    hc_ = h[:, :, i * CHUNK:(i + 1) * CHUNK]
                    ins = dve.tensor_tensor(hc_, bank(4 + i, T, CHUNK), hc_, ALU.add)
                ins.then_inc(h_ok, 1)

                mean_rstd(L, 1)

                def best16(values, indices, scores):
                    for o in (0, 8):
                        for v, _, s in zip(values, indices, scores):
                            step(dve.max(v[:, o:o + 8], s))
                        settle()
                        for v, i, s in zip(values, indices, scores):
                            step(dve.max_index(i[:, o:o + 8], v[:, o:o + 8], s))
                        settle()
                        if o == 0:
                            for v, s in zip(values, scores):
                                step(dve.match_replace(s, v[:, 0:8], s, -3.0e38))
                            settle()

                for n in range(8):
                    g, t = n // 2, n % 2
                    dve.wait_ge(sc_ok, 8 * L + n + 1)
                    m = range(4 * g, 4 * g + 4)
                    best16([v16[:, t, j, :] for j in m], [i16[:, t, j, :] for j in m], [sc[:, t, j, :] for j in m])
                for t in range(T):
                    c4 = cand[:, t, :, :].rearrange("p h (a b) -> p h a b", a=TOPK)
                    vv = v16[:, t, :, :].rearrange("p (h c) k -> p h c k", c=2)
                    step(dve.tensor_tensor(c4, last(vv[:, :, 0, :], TOPK), mid(vv[:, :, 1, :], 2, TOPK), ALU.add))
                settle()
                for t in range(T):
                    m = range(PH)
                    best16([c16[:, t, j, :] for j in m], [p16[:, t, j, :] for j in m], [cand[:, t, j, :] for j in m])
                step(dve.tensor_copy(gden[:, 0, :, :], c16[:, :, :, 0]))
                step(dve.tensor_scalar(ab16[:, 0, :, :], p16.rearrange("p t h k -> p t (h k)"), 4, None, ALU.logical_shift_right))
                step(dve.tensor_scalar(ab16[:, 1, :, :], p16.rearrange("p t h k -> p t (h k)"), 15, None, ALU.bitwise_and))
                step(dve.tensor_copy(i16b, i16.rearrange("p t m k -> p (t m k)")))
                settle()
                dve.tensor_tensor(c16, c16, last(gden[:, 0, :, :], TOPK), ALU.subtract).then_inc(ge_in, 1)
                step(dve.tensor_copy(ranks2, last(ab16.rearrange("p c t n -> p c (t n)"), 2)))
                settle()
                N16 = T * PH * TOPK
                eq = [ar(A_EQ + c * N16 * 8, N16 * 8).bitcast(BF16) for c in range(2)]
                fold = [ar(A_CAND + c * N16 * 4, N16 * 4).bitcast(BF16).rearrange("p (n r) -> p n r", r=8) for c in range(2)]
                for c in range(2):
                    step(dve.tensor_tensor(eq[c].rearrange("p (n r b) -> p n r b", r=8, b=2), mid(ranks2[:, c], 2, TOPK // 2),
                                           mid(iota[:, 0:TOPK // 2, :], 1, N16), ALU.is_equal))
                settle()
                for c in range(2):
                    e4 = eq[c].rearrange("p (m k r) -> p m k r", k=TOPK, r=TOPK)
                    ii = i16b.rearrange("p (m c r) -> p m c r", c=2, r=TOPK)[:, :, c, :]
                    step(dve.tensor_tensor(e4, e4, mid(ii, 2, TOPK), ALU.mult))
                settle()
                for c in range(2):
                    e3 = eq[c].rearrange("p (n r) -> p n r", r=TOPK)
                    step(dve.tensor_tensor(fold[c], e3[:, :, 0:8], e3[:, :, 8:16], ALU.add))
                settle()
                for c in range(2):
                    step(dve.tensor_reduce(rout[:, c, :, :].rearrange("p t n -> p (t n)"), fold[c], AX, ALU.add))
                dve.wait_ge(ge_ok, L + 1)
                step(dve.tensor_reduce(gden[:, 0, :, :], c16, AX, ALU.add))
                settle()
                step(dve.reciprocal(gden[:, 1, :, :], gden[:, 0, :, :]))
                settle()
                dve.tensor_tensor(rout[:, 2, :, :].rearrange("p t (h k) -> p t h k", k=TOPK), c16,
                                  last(gden[:, 1, :, :], TOPK), ALU.mult).then_inc(rout_ok, 1)
                dve.wait_ge(rout_ps, L + 1)
                step(dve.tensor_copy(idx2[:, :, :, :], last(bank(6, 2, SEQ), 2)))
                step(dve.tensor_copy(gres, bank(7, SEQ)))
                for k in range(3):
                    settle()
                    ins = dve.tensor_copy(g3[:, k, :, :], last(gres, 2))
                    if k < 2:
                        step(ins)
                        settle()
                        step(dve.tensor_tensor(gres, gres, g3[:, k, :, 0], ALU.subtract))
                ins.then_inc(rout_dve, 1)

                def onehots(quarter, i, n, step_=2, first=False):
                    m = (L * QUARTERS + quarter) * NB
                    if not first:
                        dve.wait_ge(g_ps, m + step_ * i + n - 1)
                    at = bass.ds((step_ * i + n) * TB, TB)
                    def pairs(v, n_):
                        return mid(v, len(v.shape) - 1, n_)

                    def cut(v):
                        return v.rearrange("p t (a b) -> p t a b", b=2)

                    E_ = cut(Eh[:, n % 2, :, :])
                    first_ = iota[:, quarter * QI // 2:(quarter + 1) * QI // 2, :]
                    dve.tensor_tensor(E_, pairs(idx2[:, 0, at, :], QI // 2), mid(first_, 1, TB), ALU.is_equal).then_inc(e_ok, 1)
                    dve.tensor_tensor(cut(Bh[:, n % 2, :, :]), pairs(idx2[:, 1, at, :], P // 2), mid(iota[:, :, :], 1, TB),
                                      ALU.is_equal).then_inc(b_ok, 1)
                    dve.wait_ge(e_ok, m + step_ * i + n + 1)
                    for k in range(3 if quarter else 2):
                        ins = dve.tensor_tensor(cut(Ah[:, n % 2, k, :, :]), E_, pairs(g3[:, k, at, :], QI // 2), ALU.mult)
                    ins.then_inc(a_ok, 1)

                def weigh(i, p, step_=2):
                    n = L * PAIRS + step_ * i + p
                    dve.wait_ge(gelu_ok, n + 1)
                    src = ar(A_LEAD, QP * 512)[:, bass.ds((step_ * i + p) * 512, 512)] if p < QP else GL[:, p % 2, :]
                    if L or not isinstance(i, int) or step_ * i + p:
                        dve.wait_ge(w_ok, n)
                    g = ar(p // QP % 2 * SEQ * QI, SEQ, QI)
                    gv = g[:, :, bass.ds(2 * step_ * i + 2 * (p % QP), 2)].rearrange("p t e -> p e t")
                    dve.tensor_tensor(W, src.rearrange("p (e t) -> p e t", e=2), gv, ALU.mult).then_inc(w1_ok, 1)
                    dve.wait_ge(w1_ok, n + 1)
                    if not isinstance(i, int):
                        used(dve, L, v_slot(p) - (2 if p < QP else 3) + 4 * i)
                    elif step_ * i + p >= 2:
                        used(dve, L, v_slot(step_ * i + p - 2))
                    elif L:
                        used(dve, L - 1, S_PLEP)
                    dve.tensor_copy(Wh[:, p % 2], W).then_inc(w2_ok, 1)
                    dve.wait_ge(w2_ok, n + 1)
                    dve.tensor_tensor(Wl[:, p % 2], W, Wh[:, p % 2].bitcast(F32), ALU.subtract).then_inc(w_ok, 1)

                def low(i, p):
                    for j in range(1 if p < QP else 2):
                        low_half(dve, L, v_slot(p), i, j, vlo_ok)

                def ahead(quarter, i, k, step_=2):
                    if not isinstance(i, int) or step_ * i + k < NB - 1:
                        onehots(quarter + 1, i, k + 1, step_)
                    elif quarter < QUARTERS - 2:
                        onehots(quarter + 2, 0, 0)

                for n in range(NB):
                    onehots(0, 0, n, first=(L == 0 and n < 2))
                low(0, 0)
                dve.wait_ge(g_ok, (L * QUARTERS + 1) * NB)

                def first_quarter(i):
                    for k in range(4):
                        weigh(i, k, 4)
                        if isinstance(i, int) and 4 * i + k == 0:
                            onehots(1, 0, 0)
                        ahead(0, i, k, 4)
                        if not isinstance(i, int) or 4 * i + k < QP - 1:
                            low(i, k + 1)

                first_quarter(0)
                with dve.Fori(1, QP // 4 - 1) as i:
                    first_quarter(i)
                first_quarter(QP // 4 - 1)
                for quarter in range(1, QUARTERS):
                    dve.wait_ge(g_ok, (L * QUARTERS + quarter + 1) * NB)

                    def body(i):
                        for k in range(2):
                            weigh(i, quarter * QP + k)
                            low(i, quarter * QP + k)
                            if quarter < QUARTERS - 1:
                                ahead(quarter, i, k)

                    with dve.Fori(0, QP // 2 - 1) as i:
                        body(i)
                    if quarter < QUARTERS - 1:
                        body(QP // 2 - 1)
                for p in (PAIRS - 2, PAIRS - 1):
                    weigh(0, p)
                    low(0, p)
                dve.wait_ge(acc_ps, L + 1)
                for t in range(T):
                    for half in range(2):
                        hh = h[:, t, half * 512:(half + 1) * 512]
                        ins = dve.tensor_tensor(hh, bank(2 * t + half, 512), hh, ALU.add)
                ins.then_inc(h_ok, 1)
                mean_rstd(L, 2)
                used(dve, L, S_PLEP)
                for i in range(N_PLEG):
                    dve.wait_ge(sg_ok, N_PLEG * L + i + 1)
                    g2 = ar(i * 512, 512)
                    step(dve.tensor_tensor(g2, bank(4 + i, 512), g2, ALU.mult))
                settle()
                for i in range(N_PLEG):
                    hc_ = h[:, :, i * CHUNK:(i + 1) * CHUNK]
                    ins = dve.tensor_tensor(hc_, ar(i * 512, T, CHUNK), hc_, ALU.add)
                ins.then_inc(h_ok, 1)


def _columns():
    widths = (256, 256, 256, 4, 512, 128, 128, 128, 128, 128, 128, 24, 256, 256, 256)
    at = np.concatenate([[0], np.cumsum(widths)])
    fq, fk, fv, ff, nq, kc, vc, ks, vs, kw, vw, ng, dq, dk, dv = (np.arange(at[i], at[i + 1]) for i in range(15))
    nq = nq.reshape(NSA_H, HD)[PAIRED].reshape(-1)
    ng = ng.reshape(NSA_H, 3)[PAIRED].T.reshape(-1)
    return np.concatenate([fq, fk, nq, ks, kw, dq, dk, kc, vc, fv, dv, vs, vw, ff, ng])


def _consts():
    c = np.zeros((P, CONST), np.float32)
    r = np.arange(P)
    c[:, K_ID:K_ID + P] = np.eye(P)
    c[:, K_TRI:K_TRI + P] = r[:, None] <= r[None, :]
    c[:, K_ONE:K_ONE + P] = 1.0
    c[:, K_MASK + P:K_MASK + SEQ] = np.where(r[None, :] <= r[:, None], 0.0, -BIG)
    c[:, K_IOTA:K_IOTA + P] = r[None, :]
    c[:, K_BLK:K_BLK + NSA_H] = (r[:, None] // NCP) == np.arange(NSA_H)[None, :]
    c[0:NCP, K_REP:K_REP + P] = np.arange(NCP)[:, None] == (r[None, :] % NCP)
    for t in range(T):
        end = np.arange(NCP) * CMP_STRIDE + CMP_LEN - 1
        ok = (end[None, :] <= (t * P + r)[:, None]) & (np.arange(NCP) < NCMP)[None, :]
        c[:, K_CM + t * NCP:K_CM + (t + 1) * NCP] = np.where(ok, 0.0, -BIG)
        c[:, K_CV + t] = ok.any(1)
    for at, d in ((K_F64, HD), (K_F32, DQK)):
        half = d // 2
        f = np.float32(THETA) ** (-np.arange(half, dtype=np.float32) / np.float32(half))
        c[:, at:at + half] = f.astype(np.float32)
    for i in range(LAYERS):
        init = 0.8 - 0.6 * np.exp(-0.3 * i)
        c[:, K_LI + i] = init
        c[:, K_LI + LAYERS + i] = 1.0 - init
    return c


def _stream(a):
    s = np.zeros((LAYERS, SLOTS, P, SLOT), np.float32)
    cols = _columns()

    def wide(dst, w):
        for i in range(-(-w.shape[1] // CHUNK)):
            part = w[:, i * CHUNK:(i + 1) * CHUNK]
            n = part.shape[1]
            dst[i, :, 0:DC * n] = part.reshape(DC, P, n).transpose(1, 0, 2).reshape(P, DC * n)

    for L in range(LAYERS):
        wide(s[L, S_IN:S_CMP], a["w_in"][L][:, cols])
        for kv in range(2):
            w = a["nsa_cmp_w"][L, kv].reshape(CMP_LEN, HD, HD).transpose(1, 0, 2).reshape(HD, SLOT)
            s[L, S_CMP + kv, 0:HD] = w
            s[L, S_CMP + kv, HD:P] = w
        wo = a["w_out"][L]
        nsa = wo[256:768].reshape(NSA_H, HD, D)[PAIRED].reshape(512, D)
        wide(s[L, S_OUT:S_Q], np.concatenate([wo[0:256], nsa, wo[768:]]))
        wide(s[L, S_Q:S_EXP], a["peer_w_q"][L])
        u = a["peer_u"][L].reshape(PAIRS, 2, P, DC, P).transpose(0, 4, 1, 3, 2).reshape(PAIRS, P, SLOT)
        v = a["peer_v"][L].reshape(PAIRS, 2, P, D).transpose(0, 2, 1, 3).reshape(PAIRS, P, SLOT)
        for i in range(PAIRS):
            s[L, u_slot(i)] = u[i]
            s[L, v_slot(i)] = v[i]
        s[L, S_PLEP] = a["ple_w_proj"][L].reshape(2, P, D).transpose(1, 0, 2).reshape(P, SLOT)
        wide(s[L, S_PLEG:SLOTS], a["ple_w_gate"][L])
    return s.reshape(LAYERS * SLOTS, P, SLOT)


def _keys(a):
    return np.ascontiguousarray(a["peer_sub_keys"].reshape(LAYERS, HC, NKEYS, P).transpose(0, 3, 1, 2).reshape(LAYERS, P, SLOT))


def _rows(a):
    s = np.zeros((LAYERS, P, ROWS), np.float32)
    for L in range(LAYERS):
        rows = [np.tile(a["fox_q_norm_w"][L], FOX_H), np.tile(a["fox_k_norm_w"][L], FOX_H),
                np.tile(a["nsa_q_norm_w"][L], NSA_H), np.tile(a["nsa_k_norm_w"][L], 4),
                np.tile(a["diff_q_norm_w"][L], 2 * DIFF_H), np.tile(a["diff_k_norm_w"][L], 2 * DIFF_H),
                a["fox_f_bias"][L], np.tile(a["nsa_k_norm_w"][L], 2), np.tile(a["diff_subln_w"][L], DIFF_H)]
        s[L] = np.concatenate(rows)[None, :]
    return s


def _cols(a):
    s = np.zeros((LAYERS, P, COLS), np.float32)
    for L in range(LAYERS):
        for j, name in enumerate(("attn_norm_w", "ffn_norm_w", "ple_norm_w")):
            s[L, :, M_COL + j * DC:M_COL + (j + 1) * DC] = a[name][L].reshape(DC, P).T
        pos = a["nsa_cmp_pos"][L].transpose(2, 0, 1).reshape(HD, 2 * CMP_LEN)
        s[L, 0:HD, M_POS:M_PT] = pos
        s[L, HD:P, M_POS:M_PT] = pos
        s[L, :, M_PT:M_LAM] = a["p"][L, 0].T.reshape(2, P, SEQ).transpose(1, 0, 2).reshape(P, 2 * SEQ)
        s[L, :, M_LAM:COLS] = a["diff_lambda"][L].reshape(1, -1)
    return s


def kernel(**inputs):
    import numpy as _np
    import concourse.bacc as _bacc
    from concourse import mybir as _mybir
    from concourse.bass_utils import run_bass_kernel_spmd as _run

    a = {k: _np.asarray(v) for k, v in inputs.items()}
    arrays = {
        "x": _np.ascontiguousarray(a["x"]),
        "positions": _np.ascontiguousarray(a["positions"]),
        "rows": _rows(a),
        "cols": _cols(a),
        "consts": _consts(),
        "keys": _keys(a),
        "stream": _stream(a),
    }
    nc = _bacc.Bacc("TRN2", target_bir_lowering=False, num_devices=1)
    args = [nc.dram_tensor(k, v.shape, _mybir.dt.from_np(v.dtype), kind="ExternalInput").ap() for k, v in arrays.items()]
    out = nc.dram_tensor("out", (1, SEQ, D), _mybir.dt.float32, kind="ExternalOutput").ap()
    trunk(nc, *args, out)
    r = _run(nc, [arrays], core_ids=[0])
    return r.results[0]["out"]
```
